# Optimizing a Trainium2 kernel written in Bass

```python
import math
import jax, jax.numpy as jnp
from jax import lax
import numpy as np

D_MODEL = 1024
BATCH = 1
SEQ = 4096
DEPTH = 1
DEC_BATCH = 8
DEC_SEQ = 4
PAST_LEN = 4096
PAGE_SIZE = 128

D_MIX = D_MODEL
POOL_W = D_MIX // 2
POOL_WINDOWS = (2, 4, 8, 16)
POOL_GROUPS = len(POOL_WINDOWS)
POOL_GC = POOL_W // POOL_GROUPS
POOL_HIST = max(POOL_WINDOWS) - 1
ATTN_W = D_MIX - POOL_W
HEAD_DIM = 64
N_HEADS = ATTN_W // HEAD_DIM
D_IN = 2 * POOL_W + 4 * ATTN_W + N_HEADS
Q_BLOCK = 128
EPS = 1e-6
ATTN_SCALE = 1.0 / math.sqrt(HEAD_DIM)

kernel_name = "hymba_pool_fox_decode_step"

def rmsnorm(x, w):
    xf = x.astype(jnp.float32)
    r = lax.rsqrt(jnp.mean(xf * xf, axis=-1, keepdims=True) + EPS)
    return (xf * r * w.astype(jnp.float32)).astype(x.dtype)

def project(h, w_in_l, b_f_l):
    b, t, _ = h.shape
    z = jnp.einsum('btd,de->bte', h, w_in_l)
    o = 0
    u_pool = z[..., o:o + POOL_W]; o += POOL_W
    g_pool = z[..., o:o + POOL_W]; o += POOL_W
    q = z[..., o:o + ATTN_W].reshape(b, t, N_HEADS, HEAD_DIM); o += ATTN_W
    k = z[..., o:o + ATTN_W].reshape(b, t, N_HEADS, HEAD_DIM); o += ATTN_W
    v = z[..., o:o + ATTN_W].reshape(b, t, N_HEADS, HEAD_DIM); o += ATTN_W
    g_attn = z[..., o:o + ATTN_W]; o += ATTN_W
    f_logit = z[..., o:o + N_HEADS]
    logf = jax.nn.log_sigmoid(f_logit.astype(jnp.float32) + b_f_l.astype(jnp.float32))
    return u_pool, g_pool, q, k, v, g_attn, logf

def pool_mix(u_hist, u_new, start_pos, pool_w_l, pool_scale_l):
    b, t, _ = u_new.shape
    ext = jnp.concatenate([u_hist.astype(u_new.dtype), u_new], axis=1)
    extf = ext.astype(jnp.float32)
    cs = jnp.concatenate([jnp.zeros((b, 1, POOL_W), jnp.float32), jnp.cumsum(extf, axis=1)], axis=1)
    end = cs[:, POOL_HIST + 1:POOL_HIST + 1 + t]
    pos = start_pos + jnp.arange(t, dtype=jnp.int32)
    uf = u_new.astype(jnp.float32)
    outs = []
    for g, w in enumerate(POOL_WINDOWS):
        sl = slice(g * POOL_GC, (g + 1) * POOL_GC)
        start = cs[:, POOL_HIST + 1 - w:POOL_HIST + 1 - w + t, sl]
        cnt = jnp.minimum(w, pos + 1).astype(jnp.float32)[None, :, None]
        outs.append((end[..., sl] - start) / cnt - uf[..., sl])
    pooled = jnp.stack(outs, axis=2)
    mixed = jnp.einsum('btgc,gcd->btgd', pooled, pool_w_l.astype(jnp.float32)).reshape(b, t, POOL_W)
    mixed = (mixed * pool_scale_l.astype(jnp.float32)).astype(u_new.dtype)
    return mixed, ext[:, -POOL_HIST:]

def fox_block(q, k, v, fq, fk, q_pos, k_pos):
    s = jnp.einsum('bqhd,bkhd->bhqk', q, k, preferred_element_type=jnp.float32) * ATTN_SCALE
    s = s + (jnp.transpose(fq, (0, 2, 1))[..., :, None] - jnp.transpose(fk, (0, 2, 1))[..., None, :])
    mask = k_pos[None, :] <= q_pos[:, None]
    s = jnp.where(mask[None, None], s, -jnp.inf)
    p = jax.nn.softmax(s, axis=-1)
    return jnp.einsum('bhqk,bkhd->bqhd', p.astype(v.dtype), v)

def merge(x, pool_out, g_pool, attn_out, g_attn, w_out_l):
    b, t, _ = x.shape
    mix = jnp.concatenate([pool_out * jax.nn.silu(g_pool),
                           attn_out.reshape(b, t, ATTN_W) * jax.nn.silu(g_attn)], axis=-1)
    return x + jnp.einsum('bte,ed->btd', mix, w_out_l)

def setup_inputs(seed: int = 0) -> dict:
    key = jax.random.key(seed)
    ks = jax.random.split(key, 16)
    n_pages = PAST_LEN // PAGE_SIZE
    n_used = DEC_BATCH * n_pages
    n_phys = (5 * n_used) // 4
    x_prompt = jax.random.normal(ks[0], (BATCH, SEQ, D_MODEL), jnp.float32)
    x_sample = jax.random.normal(ks[1], (DEC_BATCH, DEC_SEQ, D_MODEL), jnp.float32)
    cache_k = jax.random.normal(ks[2], (DEPTH, n_phys, PAGE_SIZE, N_HEADS, HEAD_DIM), jnp.float32)
    cache_v = jax.random.normal(ks[3], (DEPTH, n_phys, PAGE_SIZE, N_HEADS, HEAD_DIM), jnp.float32)
    cache_logf = jax.nn.log_sigmoid(1.0 + jax.random.normal(ks[4], (DEPTH, n_phys, PAGE_SIZE, N_HEADS), jnp.float32))
    state_pool = jax.random.normal(ks[5], (DEPTH, DEC_BATCH, POOL_HIST, POOL_W), jnp.float32)
    page_table = jax.random.permutation(ks[6], n_phys)[:n_used].reshape(DEC_BATCH, n_pages).astype(jnp.int32)
    norm_w = 1.0 + 0.05 * jax.random.normal(ks[7], (DEPTH, D_MODEL), jnp.float32)
    w_in = jax.random.normal(ks[8], (DEPTH, D_MODEL, D_IN), jnp.float32) * D_MODEL ** -0.5
    b_forget = 1.0 + 0.5 * jax.random.normal(ks[9], (DEPTH, N_HEADS), jnp.float32)
    pool_w = jax.random.normal(ks[10], (DEPTH, POOL_GROUPS, POOL_GC, POOL_GC), jnp.float32) * POOL_GC ** -0.5
    pool_scale = 1.0 + 0.1 * jax.random.normal(ks[11], (DEPTH, POOL_W), jnp.float32)
    w_out = jax.random.normal(ks[12], (DEPTH, D_MIX, D_MODEL), jnp.float32) * D_MIX ** -0.5
    norm_f = 1.0 + 0.05 * jax.random.normal(ks[13], (D_MODEL,), jnp.float32)
    return {"x_prompt": x_prompt, "x_sample": x_sample, "cache_k": cache_k, "cache_v": cache_v,
            "cache_logf": cache_logf, "state_pool": state_pool, "page_table": page_table,
            "norm_w": norm_w, "w_in": w_in, "b_forget": b_forget, "pool_w": pool_w,
            "pool_scale": pool_scale, "w_out": w_out, "norm_f": norm_f}

def reference(x_prompt, x_sample, cache_k, cache_v, cache_logf, state_pool, page_table,
              norm_w, w_in, b_forget, pool_w, pool_scale, w_out, norm_f):
    b_p, seq, _ = x_prompt.shape
    b_s, t_s, _ = x_sample.shape
    n_pages = page_table.shape[1]
    past = n_pages * cache_k.shape[2]
    n_blocks = seq // Q_BLOCK

    xp, xs = x_prompt, x_sample
    kp_l, vp_l, fp_l, pp_l = [], [], [], []
    ks_l, vs_l, fs_l, ps_l = [], [], [], []
    for l in range(DEPTH):
        h = rmsnorm(xp, norm_w[l])
        u, gp, q, k, v, ga, logf = project(h, w_in[l], b_forget[l])
        hist0 = jnp.zeros((b_p, POOL_HIST, POOL_W), u.dtype)
        pool_out, pool_new = pool_mix(hist0, u, 0, pool_w[l], pool_scale[l])
        F = jnp.cumsum(logf, axis=1)
        k_pos = jnp.arange(seq, dtype=jnp.int32)
        q_blk = jnp.moveaxis(q.reshape(b_p, n_blocks, Q_BLOCK, N_HEADS, HEAD_DIM), 1, 0)
        f_blk = jnp.moveaxis(F.reshape(b_p, n_blocks, Q_BLOCK, N_HEADS), 1, 0)
        pos_blk = k_pos.reshape(n_blocks, Q_BLOCK)
        o_blk = lax.map(lambda a: fox_block(a[0], k, v, a[1], F, a[2], k_pos), (q_blk, f_blk, pos_blk))
        attn = jnp.moveaxis(o_blk, 0, 1).reshape(b_p, seq, N_HEADS, HEAD_DIM)
        xp = merge(xp, pool_out, gp, attn, ga, w_out[l])
        kp_l.append(k); vp_l.append(v); fp_l.append(logf.astype(cache_logf.dtype)); pp_l.append(pool_new)

        h = rmsnorm(xs, norm_w[l])
        u, gp, q, k, v, ga, logf = project(h, w_in[l], b_forget[l])
        pool_out, pool_new = pool_mix(state_pool[l], u, past, pool_w[l], pool_scale[l])
        k_past = cache_k[l][page_table].reshape(b_s, past, N_HEADS, HEAD_DIM)
        v_past = cache_v[l][page_table].reshape(b_s, past, N_HEADS, HEAD_DIM)
        f_past = cache_logf[l][page_table].reshape(b_s, past, N_HEADS)
        k_all = jnp.concatenate([k_past.astype(k.dtype), k], axis=1)
        v_all = jnp.concatenate([v_past.astype(v.dtype), v], axis=1)
        F = jnp.cumsum(jnp.concatenate([f_past.astype(jnp.float32), logf], axis=1), axis=1)
        kpos = jnp.arange(past + t_s, dtype=jnp.int32)
        attn = fox_block(q, k_all, v_all, F[:, past:], F, kpos[past:], kpos)
        xs = merge(xs, pool_out, gp, attn, ga, w_out[l])
        ks_l.append(k); vs_l.append(v); fs_l.append(logf.astype(cache_logf.dtype)); ps_l.append(pool_new)

    y_prompt = rmsnorm(xp, norm_f)
    y_sample = rmsnorm(xs, norm_f)
    k_prompt = jnp.stack(kp_l, axis=0)
    v_prompt = jnp.stack(vp_l, axis=0)
    logf_prompt = jnp.stack(fp_l, axis=0)
    pool_prompt = jnp.stack(pp_l, axis=0)
    k_sample = jnp.stack(ks_l, axis=0)
    v_sample = jnp.stack(vs_l, axis=0)
    logf_sample = jnp.stack(fs_l, axis=0)
    pool_sample = jnp.stack(ps_l, axis=0)
    return (y_prompt, y_sample, k_prompt, v_prompt, logf_prompt, pool_prompt,
            k_sample, v_sample, logf_sample, pool_sample)


_drawn_inputs = setup_inputs


def setup_inputs(seed=0):
    import zlib

    import numpy as np

    out = dict(_drawn_inputs(seed))
    spreads = {}
    factors = {}
    for name, (base, spread) in spreads.items():
        noise = np.random.default_rng([zlib.crc32(name.encode()), seed]).standard_normal(out[name].shape)
        drawn = base * np.exp(spread * noise) if base else spread * noise
        out[name] = __import__('jax').numpy.asarray(drawn.astype(out[name].dtype))
    for name, factor in factors.items():
        out[name] = (out[name] * factor).astype(out[name].dtype)
    return out
```

```python
from contextlib import ExitStack

import concourse.bass as bass
from concourse import mybir

F32 = mybir.dt.float32
F32R = mybir.dt.float32r
BF16 = mybir.dt.bfloat16
I32 = mybir.dt.int32
U32 = mybir.dt.uint32
ALU = mybir.AluOpType
ACT = mybir.ActivationFunctionType
AX_X = mybir.AxisListType.X

P = 128
D = 1024
KC = D // P
W = 512
CH = W // P
H = 8
HD = 64
SEQ = 4096
TILE = 512
NT = SEQ // TILE
TT = TILE // P
NBLK = SEQ // P
DB, DS = 8, 4
NS = DB * DS
NPAGE = 32
PAGE = 128
HIST = 15
WINDOWS = (2, 4, 8, 16)
EPS = 1e-6
ROOT_D = D ** 0.5
QSCALE = HD ** -0.5
BIG = 1e30

U0, GP0, Q0, K0, V0, GA0, FL0 = 0, W, 2 * W, 3 * W, 4 * W, 5 * W, 6 * W


class Alloc:

    def __init__(self, nc, ctx, prefix):
        self.nc, self.ctx, self.prefix, self.sems = nc, ctx, prefix, []
        ctx.callback(self.clear)

    def clear(self):
        if self.sems:
            self.nc.clear_and_free_semaphores(self.sems)
            self.nc.all_engine_barrier()

    def sb(self, name, shape, dt=F32):
        return self.ctx.enter_context(self.nc.sbuf_tensor(f"{self.prefix}_{name}", list(shape), dt))

    def ps(self, name, shape, dt=F32):
        return self.ctx.enter_context(self.nc.psum_tensor(f"{self.prefix}_{name}", list(shape), dt))

    def sem(self, name):
        self.sems.append(self.nc.alloc_semaphore(f"{self.prefix}_{name}"))
        return self.sems[-1]


class Chain:

    def __init__(self, eng, sem, base=0):
        self.eng, self.sem, self.base, self.n = eng, sem, base, 0

    def link(self, ins):
        self.n += 1
        ins.then_inc(self.sem, 1)
        self.eng.wait_ge(self.sem, self.base + self.n)


def split(nc, high, low, x):
    return (lambda: nc.vector.tensor_copy(high, x),
            lambda: nc.vector.tensor_tensor(low, x, high.bitcast(F32), ALU.subtract))


def three_pass(nc, out, lhs_high, lhs_low, rhs_high, rhs_low, first, last):
    nc.tensor.matmul(out, lhs_high, rhs_high, start=first, stop=False)
    nc.tensor.matmul(out, lhs_high, rhs_low, start=False, stop=False)
    return nc.tensor.matmul(out, lhs_low, rhs_high, start=False, stop=last)


def phase_project(nc, io, keep):
    NQ = 3 * W + H
    FB = 3 * W
    with ExitStack() as ctx:
        m = Alloc(nc, ctx, "pj")
        w_high = m.sb("w_high", [P, KC, NQ], F32R)
        w_low = m.sb("w_low", [P, KC, NQ], F32R)
        norm_col = m.sb("norm_col", [P, KC])
        x = m.sb("x", [P, 2, D])
        xs = m.sb("xs", [NS, D])
        h_t = m.sb("h_t", [P, KC, TILE])
        h_high = m.sb("h_high", [P, KC, TILE], F32R)
        h_low = m.sb("h_low", [P, KC, TILE], F32R)
        stage = m.sb("stage", [P, 2, CH, TILE])
        q_stage, k_stage = stage[:, 0], stage[:, 1]
        w_raw = stage[:].rearrange("p a c t -> p (a c t)")
        k_rows = m.sb("k_rows", [P, 2, W])
        v_rows = m.sb("v_rows", [P, 2, W])
        junk = m.sb("junk", [P, D], BF16)
        squares = m.sb("squares", [P, TT + 1])
        rms = m.sb("rms", [P, TT + 1])
        minus_half = m.sb("minus_half", [P, 1])
        eps_sum = m.sb("eps_sum", [P, 1])
        b_col = m.sb("b_col", [H, 1])
        b_row = m.sb("b_row", [NS, H])
        f_z = m.sb("f_z", [H, TILE])
        f_e = m.sb("f_e", [H, TILE])
        f_log = m.sb("f_log", [H, TILE])
        f_sum = m.sb("f_sum", [H, TILE])
        f_neg = m.sb("f_neg", [H, TILE])
        f_base = m.sb("f_base", [H, 1])
        f_ones = m.sb("f_ones", [H, TILE])
        lf_cols = m.sb("lf_cols", [P, NBLK, H])
        fs = m.sb("fs", [NS, 4, H])
        s_rows = m.sb("s_rows", [NS, 3, W])

        acc = m.ps("acc", [P, 3, TILE])
        tp = m.ps("tp", [P, KC, P])
        f_ps = m.ps("f_ps", [P, TILE])
        kt_ps = m.ps("kt_ps", [P, W])
        ft_ps = m.ps("ft_ps", [P, 2, TT, H])

        const_loaded = m.sem("const_loaded")
        xs_loaded = m.sem("xs_loaded")
        x_loaded = [m.sem(f"x_loaded{i}") for i in range(2)]
        w_loaded = [m.sem(f"w_loaded{i}") for i in range(2)]
        pool_const = m.sem("pool_const")
        pool_chain = m.sem("pool_chain")
        squares_ready = m.sem("squares_ready")
        rms_ready = m.sem("rms_ready")
        h_ready = m.sem("h_ready")
        turned = m.sem("turned")
        h_t_ready = m.sem("h_t_ready")
        h_t_stored = m.sem("h_t_stored")
        h_split = m.sem("h_split")
        w_high_ready = m.sem("w_high_ready")
        w_low_dve = m.sem("w_low_dve")
        w_low_pool = m.sem("w_low_pool")
        acc_done = m.sem("acc_done")
        qk_evac = m.sem("qk_evac")
        v_evac = m.sem("v_evac")
        q_stored = m.sem("q_stored")
        k_stored = m.sem("k_stored")
        f_done = m.sem("f_done")
        f_evac = m.sem("f_evac")
        f_abs = m.sem("f_abs")
        f_soft = m.sem("f_soft")
        f_rows_ready = m.sem("f_rows_ready")
        f_neg_stored = m.sem("f_neg_stored")
        f_turned = m.sem("f_turned")
        f_turned_evac = m.sem("f_turned_evac")
        k_turned = m.sem("k_turned")
        k_rows_evac = m.sem("k_rows_evac")
        k_rows_stored = [m.sem(f"k_rows_stored{i}") for i in range(2)]
        v_rows_stored = [m.sem(f"v_rows_stored{i}") for i in range(2)]
        dve_chain = m.sem("dve_chain")
        act_chain = m.sem("act_chain")
        s_turned = m.sem("s_turned")
        s_split = m.sem("s_split")
        s_done = m.sem("s_done")
        s_evac = m.sem("s_evac")
        s_f = m.sem("s_f")
        s_out = m.sem("s_out")
        ends_stored = m.sem("ends_stored")

        x_rows = io["x_prompt"][0].rearrange("(g p) d -> g p d", p=P)
        w_in = io["w_in"][0]
        k_out = io["k_prompt"].rearrange("l b t h d -> (l b t) (h d)")
        v_out = io["v_prompt"].rearrange("l b t h d -> (l b t) (h d)")
        DVE_PER_TILE = 3

        block = ctx.enter_context(nc.Block())

        @block.sync
        def _(sp):
            sp.dma_start(xs[:], io["x_sample"].rearrange("b t d -> (b t) d")).then_inc(xs_loaded, 16)
            for t in range(2):
                sp.dma_start(x[:, t], x_rows[t]).then_inc(x_loaded[t], 16)
            sp.dma_start(norm_col[:], io["norm_w"].rearrange("l (c p) -> p (l c)", p=P), allow_slow_non_contiguous=True).then_inc(const_loaded, 16)
            sp.dma_start(b_col[:], io["b_forget"].rearrange("l h -> h l"), allow_slow_non_contiguous=True).then_inc(const_loaded, 16)
            sp.dma_start(b_row[:], io["b_forget"].to_broadcast([NS, H])).then_inc(const_loaded, 16)
            for c in range(KC):
                if c >= 2:
                    sp.wait_ge(w_low_dve, c - 1)
                    sp.wait_ge(w_low_pool, c - 1)
                rows = w_in[c * P:(c + 1) * P]
                slot = w_raw[:, (c % 2) * NQ:(c % 2 + 1) * NQ]
                sp.dma_start(slot[:, 0:FB], rows[:, Q0:Q0 + FB]).then_inc(w_loaded[c % 2], 16)
                sp.dma_start(slot[:, FB:NQ], rows[:, FL0:FL0 + H]).then_inc(w_loaded[c % 2], 16)
                if c in (0, 1):
                    sp.wait_ge(turned, c + 1)
                    sp.dma_start(x[:, c], x_rows[2 + c]).then_inc(x_loaded[c], 16)
            sp.wait_ge(s_evac, 3)
            sp.dma_start(io["q_s"], s_rows[:, 0]).then_inc(s_out, 16)
            sp.dma_start(io["k_sample"].rearrange("l b t h d -> (l b t) (h d)"), s_rows[:, 1]).then_inc(s_out, 16)
            sp.dma_start(io["v_sample"].rearrange("l b t h d -> (l b t) (h d)"), s_rows[:, 2]).then_inc(s_out, 16)
            sp.wait_ge(s_f, 4)
            sp.dma_start(io["logf_sample"].rearrange("l b t h -> (l b t) h"), fs[:, 3]).then_inc(s_out, 16)

            def super_tile(s, more):
                if more:
                    for t in range(2):
                        sp.wait_ge(turned, s * TT + (TT + t - 1))
                        sp.dma_start(x[:, t], x_rows[bass.ds(s * TT + (TT + t), 1)].rearrange("a p d -> p (a d)")).then_inc(x_loaded[t], 16)
                sp.wait_ge(h_t_ready, s * TT + TT)
                sp.dma_start(io["h_t"][bass.ds(s, 1)].rearrange("a p k t -> p (a k) t"), h_t[:]).then_inc(h_t_stored, 16)
                if more:
                    for t in range(2, 4):
                        sp.wait_ge(turned, s * TT + (TT + t - 1))
                        sp.dma_start(x[:, t % 2], x_rows[bass.ds(s * TT + (TT + t), 1)].rearrange("a p d -> p (a d)")).then_inc(x_loaded[t % 2], 16)
                sp.wait_ge(qk_evac, s * 2 * CH + CH)
                sp.dma_start(io["q_t"].rearrange("c p t -> p c t")[:, :, bass.ds(s * TILE, TILE)], q_stage).then_inc(q_stored, 16)
                sp.wait_ge(qk_evac, s * 2 * CH + 2 * CH)
                sp.dma_start(io["k_t"].rearrange("c p t -> p c t")[:, :, bass.ds(s * TILE, TILE)], k_stage).then_inc(k_stored, 16)
                for t in range(TT):
                    sp.wait_ge(k_rows_evac, s * TT + (t + 2))
                    sp.dma_start(k_out[bass.ds(s * TILE + t * P, P)], k_rows[:, t % 2]).then_inc(k_rows_stored[t % 2], 16)
                sp.wait_ge(f_rows_ready, s + 1)
                sp.dma_start(io["f_neg"][:, bass.ds(s * TILE, TILE)], f_neg[:]).then_inc(f_neg_stored, 16)
                for t in range(TT):
                    sp.wait_ge(v_evac, s * TT + (TT + t + 1))
                    sp.dma_start(v_out[bass.ds(s * TILE + t * P, P)], v_rows[:, t % 2]).then_inc(v_rows_stored[t % 2], 16)

            with sp.Fori(0, NT - 1) as s:
                super_tile(s, True)
            super_tile(NT - 1, False)
            sp.wait_ge(f_turned_evac, NT + 1)
            sp.dma_start(io["logf_prompt"].rearrange("l b (g p) h -> p (l b g) h", p=P), lf_cols[:]).then_inc(ends_stored, 16)
            sp.wait_ge(ends_stored, 16)
            sp.wait_ge(s_out, 64)
            sp.wait_ge(h_t_stored, 16 * NT)
            sp.wait_ge(q_stored, 16 * (NT + 1))
            sp.wait_ge(k_stored, 16 * (NT + 1))
            sp.wait_ge(f_neg_stored, 16 * (NT + 1))
            for i in range(2):
                sp.wait_ge(k_rows_stored[i], 16 * (2 * NT + 1))
                sp.wait_ge(v_rows_stored[i], 16 * (2 * NT + 1))

        @block.gpsimd
        def _(pool):
            pool.sem_inc(q_stored, 16)
            pool.sem_inc(k_stored, 16)
            pool.sem_inc(f_neg_stored, 16)
            pool.sem_inc(k_turned, TT)
            pool.sem_inc(k_rows_evac, 1)
            pool.sem_inc(f_evac, 1)
            pool.sem_inc(f_turned_evac, 1)
            pool.sem_inc(f_turned, 1)
            pool.sem_inc(v_evac, TT)
            for i in range(2):
                pool.sem_inc(k_rows_stored[i], 16)
                pool.sem_inc(v_rows_stored[i], 16)
            chain = Chain(pool, pool_chain)
            chain.link(nc.gpsimd.memset(keep["ident"][:], 0.0))
            chain.link(nc.gpsimd.memset(minus_half[:], -0.5))
            chain.link(nc.gpsimd.memset(eps_sum[:], D * EPS))
            chain.link(nc.gpsimd.memset(keep["ones"][:], 1.0))
            nc.gpsimd.affine_select(out=keep["ident"][:], in_=keep["ident"][:], compare_op=ALU.not_equal,
                                    fill=1.0, base=0, pattern=[[-1, P]], channel_multiplier=1).then_inc(pool_const, 1)

            def rms_of(n, count, chain):
                pool.wait_ge(squares_ready, count)
                rows = NS if n == TT else P
                out = rms[0:rows, n:n + 1]
                chain.link(nc.gpsimd.tensor_tensor(out, squares[0:rows, n:n + 1], eps_sum[0:rows], ALU.add))
                nc.gpsimd.tensor_tensor(out, out, minus_half[0:rows], ALU.pow).then_inc(rms_ready, 1)

            for n in range(TT + 1):
                rms_of((n + TT) % (TT + 1), n + 1, chain)
                if n == 2:
                    before = chain.n
            for c in range(KC):
                pool.wait_ge(w_high_ready, c + 1)
                raw = w_raw[:, (c % 2) * NQ:(c % 2) * NQ + 640]
                nc.gpsimd.tensor_tensor(w_low[:, c, 0:640], raw, w_high[:, c, 0:640].bitcast(F32), ALU.subtract).then_inc(w_low_pool, 1)
            first = chain.n
            with pool.Fori(0, NT - 1) as s:
                chain = Chain(pool, pool_chain, s * TT + first)
                for t in range(TT):
                    rms_of(t, s * TT + (TT + t + 2), chain)

        @block.scalar
        def _(act):
            def square(t, slot, count, before):
                act.wait_ge(squares_ready, before)
                act.wait_ge(x_loaded[slot], count)
                nc.scalar.activation(junk[:], x[:, slot], ACT.Square, accum_out=squares[:, t:t + 1]).then_inc(squares_ready, 1)

            def copy_turned(g, t):
                act.wait_ge(turned, g + 1)
                nc.scalar.activation(h_t[:, :, t * P:(t + 1) * P], tp[:], ACT.Copy).then_inc(h_t_ready, 1)

            act.wait_ge(xs_loaded, 16)
            nc.scalar.activation(junk[0:NS], xs[:], ACT.Square, accum_out=squares[0:NS, TT:TT + 1]).then_inc(squares_ready, 1)
            square(0, 0, 16, 1)
            square(1, 1, 16, 2)
            copy_turned(0, 0)
            square(2, 0, 32, 3)
            copy_turned(1, 1)
            square(3, 1, 32, 4)
            copy_turned(2, 2)
            copy_turned(3, 3)
            act.wait_ge(s_done, 1)
            nc.scalar.activation(s_rows[:, 0], acc[0:NS, 0], ACT.Copy, scale=QSCALE).then_inc(s_evac, 1)
            act.wait_ge(s_done, 2)
            nc.scalar.activation(s_rows[:, 1], acc[0:NS, 1], ACT.Copy).then_inc(s_evac, 1)
            act.wait_ge(s_f, 2)
            nc.scalar.activation(fs[:, 1], fs[:, 1], ACT.Exp, scale=-1.0).then_inc(act_chain, 1)
            act.wait_ge(act_chain, 1)
            nc.scalar.activation(fs[:, 2], fs[:, 1], ACT.Ln, bias=1.0).then_inc(s_f, 1)
            act.wait_ge(const_loaded, 48)

            def evac(s, u, dst, scale):
                act.wait_ge(acc_done, s * 12 + (u + 1))
                nc.scalar.activation(dst, acc[:, u % 3], ACT.Copy, scale=scale).then_inc(qk_evac, 1)

            def super_tile(s, more):
                for c in range(CH):
                    if more and c == 0:
                        for t in range(2):
                            square(t, t, s * 32 + 48, s * TT + (TT + 1 + t))
                    if c == 0:
                        act.wait_ge(q_stored, s * 16 + 16)
                    evac(s, c, q_stage[:, c], QSCALE)
                    if more and c >= 1:
                        if c == 1:
                            act.wait_ge(h_t_stored, s * 16 + 16)
                            act.wait_ge(h_split, s * TT + TT)
                        copy_turned(s * TT + (TT + c - 1), c - 1)
                        if c < 3:
                            square(c + 1, (c + 1) % 2, s * 32 + 64, s * TT + (TT + 2 + c))
                for c in range(CH):
                    if c == 0:
                        act.wait_ge(k_stored, s * 16 + 16)
                        act.wait_ge(k_turned, s * TT + TT)
                    evac(s, CH + c, k_stage[:, c], 1.0)
                    if more and c == 0:
                        copy_turned(s * TT + (TT + 3), 3)
                act.wait_ge(f_done, s + 1)
                nc.scalar.activation(f_z[:], f_ps[0:H], ACT.Identity, bias=b_col[:]).then_inc(f_evac, 1)
                act.wait_ge(f_abs, s + 1)
                nc.scalar.activation(f_e[:], f_e[:], ACT.Exp, scale=-1.0).then_inc(act_chain, 1)
                act.wait_ge(act_chain, s + 2)
                nc.scalar.activation(f_e[:], f_e[:], ACT.Ln, bias=1.0).then_inc(f_soft, 1)

            with act.Fori(0, NT - 1) as s:
                super_tile(s, True)
            super_tile(NT - 1, False)

        @block.vector
        def _(dve):
            chain = Chain(dve, dve_chain)
            nc.vector.memset(f_ones[:], 1.0)
            nc.vector.memset(keep["f_tot"][:], 0.0)
            chain.link(nc.vector.memset(f_base[:], 0.0))

            def scale_x(slot, t, count):
                dve.wait_ge(rms_ready, count)
                nc.vector.tensor_scalar(x[:, slot], x[:, slot], rms[:, t:t + 1], ROOT_D, ALU.mult, ALU.mult).then_inc(h_ready, 1)

            dve.wait_ge(rms_ready, 1)
            nc.vector.tensor_scalar(xs[:], xs[:], rms[0:NS, TT:TT + 1], ROOT_D, ALU.mult, ALU.mult).then_inc(h_ready, 1)
            scale_x(0, 0, 2)
            scale_x(1, 1, 3)
            dve.wait_ge(const_loaded, 48)

            def prepare_weights(c):
                dve.wait_ge(w_loaded[c % 2], 32 * (c // 2 + 1))
                raw = w_raw[:, (c % 2) * NQ:(c % 2 + 1) * NQ]
                chain.link(nc.vector.tensor_scalar(raw, raw, norm_col[:, c:c + 1], None, ALU.mult))
                chain.link(nc.vector.tensor_copy(w_high[:, c], raw))
                nc.vector.nop().then_inc(w_high_ready, 1)
                nc.vector.tensor_tensor(w_low[:, c, 640:NQ], raw[:, 640:NQ], w_high[:, c, 640:NQ].bitcast(F32), ALU.subtract).then_inc(w_low_dve, 1)

            dve.wait_ge(s_turned, 1)
            hs = tp[:, :, 0:NS]
            chain.link(nc.vector.tensor_copy(keep["hs_high"][:], hs))
            nc.vector.tensor_tensor(keep["hs_low"][:], hs, keep["hs_high"][:].bitcast(F32), ALU.subtract).then_inc(s_split, 1)
            prepare_weights(0)
            scale_x(0, 2, 4)
            prepare_weights(1)
            scale_x(1, 3, 5)
            for c in range(2, KC):
                prepare_weights(c)

            def split_h(s, t, chain):
                cols = slice(t * P, (t + 1) * P)
                dve.wait_ge(h_t_ready, s * TT + (t + 1))
                chain.link(nc.vector.tensor_copy(h_high[:, :, cols], h_t[:, :, cols]))
                nc.vector.tensor_tensor(h_low[:, :, cols], h_t[:, :, cols], h_high[:, :, cols].bitcast(F32), ALU.subtract).then_inc(h_split, 1)

            for t in range(TT):
                split_h(0, t, chain)
            dve.wait_ge(s_done, 3)
            nc.vector.tensor_copy(s_rows[:, 2], acc[0:NS, 2]).then_inc(s_evac, 1)
            dve.wait_ge(s_done, 4)
            chain.link(nc.vector.tensor_tensor(fs[:, 0], f_ps[0:NS, 0:H], b_row[:], ALU.add))
            nc.vector.nop().then_inc(s_f, 1)
            nc.vector.scalar_tensor_tensor(out=fs[:, 1], in0=fs[:, 0], scalar=-1.0, in1=fs[:, 0], op0=ALU.mult, op1=ALU.max).then_inc(s_f, 1)
            dve.wait_ge(s_f, 3)
            nc.vector.scalar_tensor_tensor(out=fs[:, 3], in0=fs[:, 0], scalar=0.0, in1=fs[:, 2], op0=ALU.min, op1=ALU.subtract).then_inc(s_f, 1)
            first = chain.n
            PER = 3 + TT

            def super_tile(s, more):
                chain = Chain(dve, dve_chain, s * PER + first)
                if more:
                    for t in range(TT):
                        dve.wait_ge(turned, s * TT + (TT + t - 1)) if t >= 2 else None
                        scale_x(t % 2, t, s * TT + (TT + t + 2))
                for t in range(TT):
                    dve.wait_ge(k_turned, s * TT + (TT + t + 1))
                    dve.wait_ge(k_rows_stored[t % 2], s * 32 + (16 * (t // 2) + 16))
                    nc.vector.tensor_copy(k_rows[:, t % 2], kt_ps[:]).then_inc(k_rows_evac, 1)
                dve.wait_ge(f_evac, s + 2)
                nc.vector.scalar_tensor_tensor(out=f_e[:], in0=f_z[:], scalar=-1.0, in1=f_z[:], op0=ALU.mult, op1=ALU.max).then_inc(f_abs, 1)
                dve.wait_ge(f_soft, s + 1)
                dve.wait_ge(f_turned, s + 1)
                dve.wait_ge(f_neg_stored, s * 16 + 16)
                chain.link(nc.vector.scalar_tensor_tensor(out=f_log[:], in0=f_z[:], scalar=0.0, in1=f_e[:], op0=ALU.min, op1=ALU.subtract))
                chain.link(nc.vector.tensor_tensor_scan(f_sum[:], f_ones[:], f_log[:], 0.0, ALU.mult, ALU.add))
                nc.vector.tensor_copy(keep["f_tot"][:, bass.ds(s, 1)], f_sum[:, TILE - 1:TILE])
                chain.link(nc.vector.tensor_scalar(f_neg[:], f_sum[:], -1.0, f_base[:], ALU.mult, ALU.add))
                nc.vector.tensor_copy(f_base[:], f_neg[:, TILE - 1:TILE]).then_inc(f_rows_ready, 1)
                for t in range(TT):
                    if more:
                        dve.wait_ge(acc_done, s * 12 + (8 + t + 1))
                        split_h(s + 1, t, chain)
                    else:
                        chain.n += 1
                    dve.wait_ge(acc_done, s * 12 + (8 + t + 1))
                    dve.wait_ge(v_rows_stored[t % 2], s * 32 + (16 * (t // 2) + 16))
                    nc.vector.tensor_copy(v_rows[:, t % 2], acc[:, (8 + t) % 3]).then_inc(v_evac, 1)
                    if t == 1:
                        dve.wait_ge(f_turned, s + 2)
                        nc.vector.tensor_copy(lf_cols[:, bass.ds(s * TT, TT)], ft_ps[:, 0])
                        nc.vector.tensor_copy(keep["f_cols"][:, bass.ds(s * TT, TT)], ft_ps[:, 1]).then_inc(f_turned_evac, 1)
                assert chain.n == PER

            with dve.Fori(0, NT - 1) as s:
                super_tile(s, True)
            super_tile(NT - 1, False)

        @block.tensor
        def _(pe):
            def turn(src, count, g, done):
                rows = src.shape[0]
                pe.wait_ge(h_ready, count)
                if g is not None:
                    pe.wait_ge(h_t_ready, g)
                for c in range(KC):
                    last = nc.tensor.transpose(tp[:, c, 0:rows], src[:, c * P:(c + 1) * P], keep["ident"][0:rows, 0:rows])
                last.then_inc(done, 1)

            pe.wait_ge(pool_const, 1)
            turn(xs[:], 1, None, s_turned)
            pe.wait_ge(s_split, 1)
            turn(x[:, 0], 2, None, turned)
            turn(x[:, 1], 3, 1, turned)
            turn(x[:, 0], 4, 2, turned)
            turn(x[:, 1], 5, 3, turned)
            pe.wait_ge(w_low_dve, KC)
            pe.wait_ge(w_low_pool, KC)
            for n in range(3):
                for c in range(KC):
                    cols = slice(n * W, (n + 1) * W)
                    last = three_pass(nc, acc[0:NS, n], keep["hs_high"][:, c], keep["hs_low"][:, c],
                                      w_high[:, c, cols], w_low[:, c, cols], c == 0, c == KC - 1)
                last.then_inc(s_done, 1)
            for c in range(KC):
                last = three_pass(nc, f_ps[0:NS, 0:H], keep["hs_high"][:, c], keep["hs_low"][:, c],
                                  w_high[:, c, FB:NQ], w_low[:, c, FB:NQ], c == 0, c == KC - 1)
            last.then_inc(s_done, 1)
            pe.wait_ge(s_evac, 3)
            pe.wait_ge(s_f, 1)

            def super_tile(s, more):
                pe.wait_ge(h_split, s * TT + TT)
                for u in range(2 * CH):
                    if u < 3:
                        pe.wait_ge(v_evac, s * TT + (u + 2))
                    else:
                        pe.wait_ge(qk_evac, s * 2 * CH + (u - 2))
                    cols = slice(u * P, (u + 1) * P)
                    for c in range(KC):
                        last = three_pass(nc, acc[:, u % 3], w_high[:, c, cols], w_low[:, c, cols],
                                          h_high[:, c], h_low[:, c], c == 0, c == KC - 1)
                    last.then_inc(acc_done, 1)
                    if more and 1 <= u <= 4:
                        t = u - 1
                        turn(x[:, t % 2], s * TT + (TT + t + 2), s * TT + (TT + t), turned)
                pe.wait_ge(f_evac, s + 1)
                for c in range(KC):
                    last = three_pass(nc, f_ps[0:H], w_high[:, c, FB:NQ], w_low[:, c, FB:NQ],
                                      h_high[:, c], h_low[:, c], c == 0, c == KC - 1)
                last.then_inc(f_done, 1)
                pe.wait_ge(qk_evac, s * 2 * CH + 2 * CH)
                for t in range(TT):
                    u = 2 * CH + t
                    if t == 3:
                        pe.wait_ge(v_evac, s * TT + (TT + 1))
                    for c in range(KC):
                        last = three_pass(nc, acc[:, u % 3], h_high[:, c, t * P:(t + 1) * P], h_low[:, c, t * P:(t + 1) * P],
                                          w_high[:, c, 2 * W:3 * W], w_low[:, c, 2 * W:3 * W], c == 0, c == KC - 1)
                    last.then_inc(acc_done, 1)
                    if t == 0:
                        for tk in range(TT):
                            pe.wait_ge(k_rows_evac, s * TT + (tk + 1))
                            for c in range(CH):
                                last = nc.tensor.transpose(kt_ps[:, c * P:(c + 1) * P], k_stage[:, c, tk * P:(tk + 1) * P], keep["ident"][:])
                            last.then_inc(k_turned, 1)
                    if t == 1:
                        pe.wait_ge(pool_const, 1)
                        pe.wait_ge(f_rows_ready, s + 1)
                        pe.wait_ge(f_turned_evac, s + 1)
                        for j, rows in enumerate((f_log, f_sum)):
                            for tk in range(TT):
                                last = nc.tensor.transpose(ft_ps[:, j, tk], rows[:, tk * P:(tk + 1) * P], keep["ident"][0:H, 0:H])
                        last.then_inc(f_turned, 1)

            with pe.Fori(0, NT - 1) as s:
                super_tile(s, True)
            super_tile(NT - 1, False)


class Count:

    def __init__(self, sem, per, credit=0):
        self.sem, self.per, self.credit = sem, per, credit

    def at(self, i, k):
        assert k + self.credit >= 1, (k, self.credit)
        return i * self.per + (k + self.credit)


def wait_apart(eng, sem, value, ticks):
    eng.wait_ge(sem, value)
    eng.sem_inc(ticks, 1)


def attend_steps():
    return [(hp, j, e) for hp in range(2) for j in range(NT) for e in range(2 * (j + 1))]


def phase_attend(nc, io, keep):
    STEPS = attend_steps()
    NSTEP = len(STEPS)
    NBLOCK = 2 * NT
    NUNIT = sum(TT * (j + 1) for _ in range(2) for j in range(NT))
    KCHUNK = 1024
    NKC = SEQ // KCHUNK
    RING = 4
    step_of = {key: n for n, key in enumerate(STEPS)}
    last_step = [step_of[(b // NT, b % NT, 2 * (b % NT) + 1)] for b in range(NBLOCK)]
    unit_base = [sum(TT * (c % NT + 1) for c in range(b)) for b in range(NBLOCK + 1)]

    def on_pool(n):
        _, j, e = STEPS[n]
        return e < 2 * j and e % 3 == 1

    pool_adds = [0]
    for n in range(NSTEP):
        pool_adds.append(pool_adds[-1] + on_pool(n))
    dve_adds = [n - pool_adds[n] for n in range(NSTEP + 1)]

    def lo(n, half):
        _, j, e = STEPS[n]
        own = 2 * e + half - TT * j
        return max(own, 0) * P

    def diagonal(n):
        _, j, e = STEPS[n]
        return e >= 2 * j

    masks = [0]
    for n in range(NSTEP):
        masks.append(masks[-1] + diagonal(n))

    def units_in(n):
        hp, j, e = STEPS[n]
        b = hp * NT + j + 1
        if b == NBLOCK or e == 2 * j + 1:
            return []
        total, slots = TT * (b % NT + 1), 2 * j + 1
        return [(b, u) for u in range(total * e // slots, total * (e + 1) // slots)]

    with ExitStack() as ctx:
        m = Alloc(nc, ctx, "at")
        k_raw = m.sb("k_raw", [P, 2, KCHUNK])
        k_all = [m.sb(f"k_all{i}", [P, SEQ], F32R) for i in range(2)]
        k_one = [m.sb(f"k_one{i}", [P, SEQ], F32R) for i in range(2)]
        v = m.sb("v", [P, 2, NBLK, HD])
        f_neg = m.sb("f_neg", [P, 2, SEQ])
        f_diag = m.sb("f_diag", [P, 2, TT, P])
        tri = m.sb("tri", [P, P])
        tri_t = m.sb("tri_t", [P, P])
        q_raw = m.sb("q_raw", [P, 2, TILE])
        q_all = m.sb("q_all", [P, 2, TILE], F32R)
        q_one = m.sb("q_one", [P, 2, TILE], F32R)
        max_parts = m.sb("max_parts", [P, TT, NT + 1])
        max_all = m.sb("max_all", [P, TT])
        zero = m.sb("zero", [P, 1])
        shift = m.sb("shift", [P, TT, P], F32R)
        ones_r = m.sb("ones_r", [P, P], F32R)
        probs = m.sb("probs", [P, RING, 2, TILE])
        den_dve = m.sb("den_dve", [P, 2, 2, TILE])
        den_pool = m.sb("den_pool", [P, 2, 2, TILE])
        den_sb = m.sb("den_sb", [P, TILE])
        den_inv = m.sb("den_inv", [P, TILE])
        o_sb = m.sb("o_sb", [P, TILE])
        o_out = m.sb("o_out", [P, 2, TILE])
        base = m.sb("base", [P, H, NT])
        bias = m.sb("bias", [P, H, NT, NBLK])
        gap = m.sb("gap", [P, H, NT, NT])
        f_pre = m.sb("f_pre", [H, NT])
        f_spread = m.sb("f_spread", [H, H, NT])
        f_one = m.sb("f_one", [H, NT])
        bias_h = m.sb("bias_h", [P, 2, NT, NBLK])
        base_h = m.sb("base_h", [P, 2, NT])

        st = m.ps("st", [P, 2, 2, TILE])
        o_ps = m.ps("o_ps", [P, TILE])
        mx = m.ps("mx", [P, 2, TILE])
        misc = m.ps("misc", [P, TILE])

        setup = m.sem("setup")
        ticks = m.sem("ticks")
        setup_pe = m.sem("setup_pe")
        tri_ready = m.sem("tri_ready")
        k_loaded = [m.sem(f"k_loaded{i}") for i in range(2)]
        v_loaded = [m.sem(f"v_loaded{i}") for i in range(2)]
        f_loaded = [m.sem(f"f_loaded{i}") for i in range(2)]
        q_loaded = [m.sem(f"q_loaded{i}") for i in range(2)]
        k_high = Count(m.sem("k_high"), 2 * NKC)
        k_low = Count(m.sem("k_low"), 2 * NKC, 2)
        q_high = Count(m.sem("q_high"), NBLOCK)
        q_low = Count(m.sem("q_low"), NBLOCK, 2)
        q_shift = Count(m.sem("q_shift"), NBLOCK)
        shift_ready = Count(m.sem("shift_ready"), NBLOCK)
        shift_turned = Count(m.sem("shift_turned"), NBLOCK, 1)
        st_ready = Count(m.sem("st_ready"), NSTEP)
        exp_done = Count(m.sem("exp_done"), NSTEP, 2)
        masked = Count(m.sem("masked"), masks[-1])
        pv_done = Count(m.sem("pv_done"), NSTEP, RING)
        added_dve = Count(m.sem("added_dve"), dve_adds[-1], RING)
        added_pool = Count(m.sem("added_pool"), pool_adds[-1], RING)
        mx_ready = Count(m.sem("mx_ready"), NUNIT)
        mx_done = Count(m.sem("mx_done"), NUNIT, 2)
        f_diag_ready = Count(m.sem("f_diag_ready"), NBLOCK)
        head_ready = Count(m.sem("head_ready"), 2)
        max_chain = Count(m.sem("max_chain"), 2 * NBLOCK)
        den_pool_sum = Count(m.sem("den_pool_sum"), NBLOCK - 2)
        den_sum = Count(m.sem("den_sum"), 2 * NBLOCK)
        den_ready = Count(m.sem("den_ready"), NBLOCK)
        den_logged = Count(m.sem("den_logged"), 2 * NBLOCK, 2)
        den_out = Count(m.sem("den_out"), NBLOCK)
        o_copied = Count(m.sem("o_copied"), NBLOCK, 1)
        o_scaled = Count(m.sem("o_scaled"), 2 * NBLOCK)
        o_done = Count(m.sem("o_done"), NBLOCK, 1)
        o_stored = [m.sem(f"o_stored{i}") for i in range(2)]

        v_rows = io["v_prompt"].rearrange("l b (g p) h d -> p (l b g) h d", p=P)

        def tile_and_chunk(b, u):
            j = b % NT
            return u // (j + 1), u % (j + 1)

        block = ctx.enter_context(nc.Block())

        @block.sync
        def _(sp):
            def load_k(i, n):
                hp, c = divmod(n, NKC)
                sp.wait_ge(k_low.sem, k_low.at(i, n - 1))
                src = io["k_t"][bass.ds(i, 1), hp * HD:(hp + 1) * HD, c * KCHUNK:(c + 1) * KCHUNK].rearrange("a p t -> (a p) t")
                for half in range(2):
                    sp.dma_start(k_raw[half * HD:(half + 1) * HD, n % 2], src).then_inc(k_loaded[n % 2], 16)

            def load_q(i, b):
                hp, j = divmod(b, NT)
                sp.wait_ge(q_low.sem, q_low.at(i, b - 1))
                src = io["q_t"][bass.ds(i, 1), hp * HD:(hp + 1) * HD, j * TILE:(j + 1) * TILE].rearrange("a p t -> (a p) t")
                for half in range(2):
                    sp.dma_start(q_raw[half * HD:(half + 1) * HD, b % 2], src).then_inc(q_loaded[b % 2], 16)

            def load_head(i, hp):
                rows = io["f_neg"][bass.ds(i * 2 + hp, 1)]
                sp.dma_start(f_neg[:, hp], rows.to_broadcast([P, SEQ])).then_inc(f_loaded[hp], 16)
                sp.dma_start(v[:, hp], v_rows[:, :, bass.ds(i * 2 + hp, 1)].rearrange("p g a d -> p g (a d)")).then_inc(v_loaded[hp], 16)

            def store_o(i, b):
                hp, j = divmod(b, NT)
                sp.wait_ge(o_done.sem, o_done.at(i, b + 1))
                for half in range(2):
                    dst = io["attn_t"][half, bass.ds(i, 1), hp * HD:(hp + 1) * HD, j * TILE:(j + 1) * TILE].rearrange("a p t -> (a p) t")
                    sp.dma_start(dst, o_out[half * HD:(half + 1) * HD, b % 2]).then_inc(o_stored[b % 2], 16)

            with sp.Fori(0, CH) as i:
                load_k(i, 0)
                load_q(i, 0)
                load_head(i, 0)
                load_k(i, 1)
                for b in range(NBLOCK):
                    if b + 1 < NBLOCK:
                        load_q(i, b + 1)
                    if b % 2 and b // 2 + 2 < 2 * NKC:
                        load_k(i, b // 2 + 2)
                    if b == NT // 2:
                        load_head(i, 1)
                    if b >= 1:
                        store_o(i, b - 1)
                wait_apart(sp, pv_done.sem, pv_done.at(i, NSTEP), ticks)
                store_o(i, NBLOCK - 1)
            for half in range(2):
                sp.wait_ge(o_stored[half], CH * NBLOCK // 2 * 32 + 32)

        @block.gpsimd
        def _(pool):
            for c in (k_low, q_low, shift_turned, exp_done, pv_done, added_dve, added_pool, mx_done,
                      den_logged, o_copied, o_done):
                pool.sem_inc(c.sem, c.credit)
            for c in o_stored:
                pool.sem_inc(c, 32)
            nc.gpsimd.memset(zero[:], 0.0).then_inc(tri_ready, 1)
            nc.gpsimd.memset(tri[:], 0.0).then_inc(tri_ready, 1)
            pool.wait_ge(tri_ready, 2)
            nc.gpsimd.memset(tri_t[:], 0.0).then_inc(tri_ready, 1)
            pool.wait_ge(tri_ready, 3)
            nc.gpsimd.affine_select(out=tri_t[:], in_=tri_t[:], compare_op=ALU.is_ge, fill=-BIG, base=0,
                                    pattern=[[1, P]], channel_multiplier=-1).then_inc(tri_ready, 1)
            nc.gpsimd.affine_select(out=tri[:], in_=tri[:], compare_op=ALU.is_ge, fill=-BIG, base=0,
                                    pattern=[[-1, P]], channel_multiplier=1).then_inc(tri_ready, 1)
            pool.wait_ge(tri_ready, 5)

            def diagonal_f(i, b):
                hp, j = divmod(b, NT)
                pool.wait_ge(f_loaded[hp], i * 16 + 16)
                if b >= 2:
                    pool.wait_ge(mx_done.sem, mx_done.at(i, unit_base[b - 1]))
                row = f_neg[:, hp, j * TILE:(j + 1) * TILE].rearrange("p (t k) -> p t k", t=TT)
                nc.gpsimd.tensor_tensor(f_diag[:, b % 2], row, tri[:].unsqueeze(1).to_broadcast([P, TT, P]), ALU.add).then_inc(f_diag_ready.sem, 1)

            def add(i, n):
                hp, j, e = STEPS[n]
                b = hp * NT + j
                pool.wait_ge(exp_done.sem, exp_done.at(i, n + 1))
                dst, src = den_pool[:, b % 2], probs[:, n % RING]
                if e == 1:
                    nc.gpsimd.tensor_tensor(dst, src, zero[:].unsqueeze(2).to_broadcast([P, 2, TILE]), ALU.add).then_inc(added_pool.sem, 1)
                else:
                    pool.wait_ge(added_pool.sem, added_pool.at(i, pool_adds[n]))
                    nc.gpsimd.tensor_tensor(dst, dst, src, ALU.add).then_inc(added_pool.sem, 1)

            def finish_den(i, b):
                if b % NT == 0:
                    return
                pool.wait_ge(added_pool.sem, added_pool.at(i, pool_adds[last_step[b] + 1]))
                nc.gpsimd.tensor_tensor(den_pool[:, b % 2, 0], den_pool[:, b % 2, 0], den_pool[:, b % 2, 1], ALU.add).then_inc(den_pool_sum.sem, 1)

            def scale_o(i, b):
                pool.wait_ge(den_out.sem, den_out.at(i, b + 1))
                pool.wait_ge(o_copied.sem, o_copied.at(i, b + 1))
                nc.gpsimd.tensor_tensor(o_sb[:], o_sb[:], den_inv[:], ALU.mult).then_inc(o_scaled.sem, 1)
                nc.gpsimd.tensor_tensor(den_sb[:], den_sb[:], den_inv[:], ALU.mult).then_inc(o_scaled.sem, 1)

            with pool.Fori(0, CH) as i:
                diagonal_f(i, 0)
                diagonal_f(i, 1)
                for n in range(NSTEP):
                    hp, j, e = STEPS[n]
                    b = hp * NT + j
                    if e == 0:
                        if b + 2 < NBLOCK:
                            diagonal_f(i, b + 2)
                    if on_pool(n):
                        add(i, n)
                    if e == 2 * j:
                        finish_den(i, b)
                    if b >= 1 and e == (2 if j else 1):
                        scale_o(i, b - 1)
                scale_o(i, NBLOCK - 1)

        @block.scalar
        def _(act):
            def round_k(i, n):
                hp, c = divmod(n, NKC)
                act.wait_ge(k_loaded[n % 2], i * (NKC * 32) + (n // 2 + 1) * 32)
                cols = slice(c * KCHUNK, (c + 1) * KCHUNK)
                nc.scalar.activation(k_all[hp][:, cols], k_raw[:, n % 2], ACT.Copy)
                nc.scalar.activation(k_one[hp][0:HD, cols], k_raw[0:HD, n % 2], ACT.Copy).then_inc(k_high.sem, 1)

            def round_q(i, b):
                act.wait_ge(q_loaded[b % 2], i * (NBLOCK // 2 * 32) + (b // 2 + 1) * 32)
                nc.scalar.activation(q_all[:, b % 2], q_raw[:, b % 2], ACT.Copy).then_inc(q_high.sem, 1)

            def shift_rows(i, b):
                act.wait_ge(shift_turned.sem, shift_turned.at(i, b + 1))
                nc.scalar.activation(q_one[HD:P, b % 2], misc[HD:P], ACT.Copy).then_inc(q_shift.sem, 1)

            def copy_o(i, b):
                act.wait_ge(pv_done.sem, pv_done.at(i, last_step[b] + 1))
                act.wait_ge(o_done.sem, o_done.at(i, b))
                nc.scalar.activation(o_sb[:], o_ps[:], ACT.Copy).then_inc(o_copied.sem, 1)

            def invert_den(i, b):
                act.wait_ge(den_ready.sem, den_ready.at(i, b + 1))
                nc.scalar.activation(den_inv[:], misc[:], ACT.Ln).then_inc(den_logged.sem, 1)
                nc.scalar.activation(den_sb[:], misc[:], ACT.Copy).then_inc(den_logged.sem, 1)
                act.wait_ge(den_logged.sem, den_logged.at(i, 2 * b + 2))
                nc.scalar.activation(den_inv[:], den_inv[:], ACT.Exp, scale=-1.0).then_inc(den_out.sem, 1)

            def exps(i, n):
                hp, j, e = STEPS[n]
                if diagonal(n):
                    act.wait_ge(masked.sem, masked.at(i, masks[n + 1]))
                else:
                    act.wait_ge(st_ready.sem, st_ready.at(i, n + 1))
                act.wait_ge(pv_done.sem, pv_done.at(i, n - RING + 1))
                k = n - RING
                if on_pool(k % NSTEP):
                    act.wait_ge(added_pool.sem, added_pool.at(i, pool_adds[k + 1] if k >= 0 else pool_adds[k + 1 + NSTEP] - pool_adds[-1]))
                else:
                    act.wait_ge(added_dve.sem, added_dve.at(i, dve_adds[k + 1] if k >= 0 else dve_adds[k + 1 + NSTEP] - dve_adds[-1]))
                for half in range(2):
                    blk = 2 * e + half
                    first = lo(n, half)
                    last = nc.scalar.activation(probs[:, n % RING, half, first:TILE], st[:, n % 2, half, first:TILE],
                                                ACT.Exp, bias=bias_h[:, hp, j, blk:blk + 1])
                last.then_inc(exp_done.sem, 1)

            with act.Fori(0, CH) as i:
                round_k(i, 0)
                round_q(i, 0)
                shift_rows(i, 0)
                for n in range(NSTEP):
                    hp, j, e = STEPS[n]
                    b = hp * NT + j
                    if e == 0:
                        if b + 1 < NBLOCK:
                            round_q(i, b + 1)
                        if b % 2 == 0 and b // 2 + 1 < 2 * NKC:
                            round_k(i, b // 2 + 1)
                        if j == 0:
                            act.wait_ge(head_ready.sem, head_ready.at(i, hp + 1))
                    if e == 2 * j + 1 and b + 1 < NBLOCK:
                        shift_rows(i, b + 1)
                    exps(i, n)
                    if e == 0 and b >= 1:
                        copy_o(i, b - 1)
                    if e == 1 and b >= 1:
                        invert_den(i, b - 1)
                copy_o(i, NBLOCK - 1)
                invert_den(i, NBLOCK - 1)

        @block.vector
        def _(dve):
            n_setup = [0]

            def link(ins):
                n_setup[0] += 1
                ins.then_inc(setup, 1)
                dve.wait_ge(setup, n_setup[0])

            for t in k_one:
                link(nc.vector.memset(t[HD:P].bitcast(F32), 0.0))
                link(nc.vector.memset(t[HD:HD + 1].bitcast(F32), 1.0))
            link(nc.vector.memset(ones_r[:].bitcast(F32), 1.0))
            link(nc.vector.memset(max_parts[:], -BIG))
            link(nc.vector.memset(f_one[:], 1.0))
            link(nc.vector.tensor_tensor_scan(f_pre[:], f_one[:], keep["f_tot"][:], 0.0, ALU.mult, ALU.add))
            link(nc.vector.tensor_tensor(f_pre[:], f_pre[:], keep["f_tot"][:], ALU.subtract))
            link(nc.vector.tensor_tensor(f_spread[:], f_pre[:].unsqueeze(1).to_broadcast([H, H, NT]),
                                         keep["ident"][0:H, 0:H].unsqueeze(2).to_broadcast([H, H, NT]), ALU.mult))
            dve.wait_ge(setup_pe, 1)
            link(nc.vector.tensor_copy(base[:], misc[:, 0:H * NT].rearrange("p (h s) -> p h s", h=H)))
            link(nc.vector.tensor_tensor(gap[:], base[:].unsqueeze(3).to_broadcast([P, H, NT, NT]),
                                         base[:].unsqueeze(2).to_broadcast([P, H, NT, NT]), ALU.subtract))
            for h in range(H):
                local = keep["f_cols"][:, :, h].rearrange("p (s t) -> p s t", t=TT)
                last = nc.vector.tensor_tensor(bias[:, h].rearrange("p j (s t) -> p j s t", t=TT),
                                               gap[:, h].unsqueeze(3).to_broadcast([P, NT, NT, TT]),
                                               local.unsqueeze(1).to_broadcast([P, NT, NT, TT]), ALU.subtract)
            link(last)

            def start_head(i, hp):
                h = i * 2 + hp
                nc.vector.tensor_copy(bias_h[:, hp], bias[:, bass.ds(h, 1)].rearrange("p a j g -> p (a j) g"))
                nc.vector.tensor_copy(base_h[:, hp], base[:, bass.ds(h, 1)].rearrange("p a j -> p (a j)")).then_inc(head_ready.sem, 1)

            def low_k(i, n):
                hp, c = divmod(n, NKC)
                dve.wait_ge(k_high.sem, k_high.at(i, n + 1))
                cols = slice(c * KCHUNK, (c + 1) * KCHUNK)
                low = k_all[hp][HD:P, cols]
                nc.vector.tensor_tensor(low, k_raw[HD:P, n % 2], low.bitcast(F32), ALU.subtract).then_inc(k_low.sem, 1)

            def low_q(i, b):
                dve.wait_ge(q_high.sem, q_high.at(i, b + 1))
                nc.vector.tensor_tensor(q_one[0:HD, b % 2], q_raw[0:HD, b % 2], q_all[0:HD, b % 2].bitcast(F32), ALU.subtract).then_inc(q_low.sem, 1)

            def unit(i, b, u):
                hp, j = divmod(b, NT)
                t, c = tile_and_chunk(b, u)
                k = unit_base[b] + u
                if u == 0:
                    if j == 0:
                        dve.wait_ge(f_loaded[hp], i * 16 + 16)
                    dve.wait_ge(f_diag_ready.sem, f_diag_ready.at(i, b + 1))
                wait_apart(dve, mx_ready.sem, mx_ready.at(i, k + 1), ticks)
                bank = mx[:, k % 2]
                if c < j:
                    nc.vector.tensor_tensor_reduce(out=bank, in0=bank, in1=f_neg[:, hp, c * TILE:(c + 1) * TILE], scale=1.0,
                                                   scalar=-BIG, op0=ALU.add, op1=ALU.max,
                                                   accum_out=max_parts[:, t, c + 1:c + 2]).then_inc(mx_done.sem, 1)
                    return
                tile = bank[:, t * P:(t + 1) * P]
                ins = nc.vector.tensor_tensor_reduce(out=tile, in0=tile, in1=f_diag[:, b % 2, t], scale=1.0,
                                                     scalar=-BIG, op0=ALU.add, op1=ALU.max, accum_out=max_parts[:, t, c + 1:c + 2])
                if t > 0:
                    rest = bank[:, 0:t * P]
                    ins = nc.vector.tensor_tensor_reduce(out=rest, in0=rest, in1=f_neg[:, hp, c * TILE:c * TILE + t * P], scale=1.0,
                                                         scalar=-BIG, op0=ALU.add, op1=ALU.max, accum_out=max_parts[:, t, 0:1])
                ins.then_inc(mx_done.sem, 1)

            def shift_of(i, b):
                hp, j = divmod(b, NT)
                dve.wait_ge(mx_done.sem, mx_done.at(i, unit_base[b + 1]))
                dve.wait_ge(head_ready.sem, head_ready.at(i, hp + 1))
                nc.vector.tensor_reduce(max_all[:], max_parts[:, :, 0:j + 2], AX_X, ALU.max).then_inc(max_chain.sem, 1)
                dve.wait_ge(max_chain.sem, max_chain.at(i, 2 * b + 1))
                nc.vector.tensor_scalar(max_all[:], max_all[:], -1.0, base_h[:, hp, j:j + 1], ALU.mult, ALU.subtract).then_inc(max_chain.sem, 1)
                dve.wait_ge(max_chain.sem, max_chain.at(i, 2 * b + 2))
                dve.wait_ge(shift_turned.sem, shift_turned.at(i, b))
                nc.vector.tensor_tensor(shift[:], keep["ident"][:].unsqueeze(1).to_broadcast([P, TT, P]),
                                        max_all[:].unsqueeze(2).to_broadcast([P, TT, P]), ALU.mult).then_inc(shift_ready.sem, 1)

            def mask(i, n):
                hp, j, e = STEPS[n]
                dve.wait_ge(st_ready.sem, st_ready.at(i, n + 1))
                for half in range(2):
                    tile = st[:, n % 2, half, lo(n, half):lo(n, half) + P]
                    last = nc.vector.tensor_tensor(tile, tile, tri_t[:], ALU.add)
                if j == 0 and e == 0:
                    dve.wait_ge(pv_done.sem, pv_done.at(i, n - RING + 1))
                    last = nc.vector.memset(probs[:, n % RING, 1, 0:P], 0.0)
                last.then_inc(masked.sem, 1)

            def add(i, n):
                hp, j, e = STEPS[n]
                b = hp * NT + j
                dve.wait_ge(exp_done.sem, exp_done.at(i, n + 1))
                dst, src = den_dve[:, b % 2], probs[:, n % RING]
                if e == 0:
                    nc.vector.tensor_copy(dst, src).then_inc(added_dve.sem, 1)
                    return
                dve.wait_ge(added_dve.sem, added_dve.at(i, dve_adds[n]))
                if not diagonal(n):
                    nc.vector.tensor_tensor(dst, dst, src, ALU.add).then_inc(added_dve.sem, 1)
                    return
                for half in range(2):
                    cols = slice(lo(n, half), TILE)
                    last = nc.vector.tensor_tensor(dst[:, half, cols], dst[:, half, cols], src[:, half, cols], ALU.add)
                last.then_inc(added_dve.sem, 1)

            def sum_den(i, b):
                d = den_dve[:, b % 2]
                dve.wait_ge(added_dve.sem, added_dve.at(i, dve_adds[last_step[b] + 1]))
                nc.vector.tensor_tensor(d[:, 0], d[:, 0], d[:, 1], ALU.add).then_inc(den_sum.sem, 1)
                dve.wait_ge(den_sum.sem, den_sum.at(i, 2 * b + 1))
                if b % NT:
                    dve.wait_ge(den_pool_sum.sem, i * (NBLOCK - 2) + (b - b // NT))
                    nc.vector.tensor_tensor(d[:, 0], d[:, 0], den_pool[:, b % 2, 0], ALU.add).then_inc(den_sum.sem, 1)
                else:
                    nc.vector.nop().then_inc(den_sum.sem, 1)

            def finish_o(i, b):
                dve.wait_ge(o_scaled.sem, o_scaled.at(i, 2 * b + 2))
                dve.wait_ge(o_stored[b % 2], i * (NBLOCK // 2 * 32) + (b // 2 + 1) * 32)
                nc.vector.scalar_tensor_tensor(out=o_out[:, b % 2], in0=den_sb[:], scalar=2.0, in1=o_sb[:],
                                               op0=ALU.subtract, op1=ALU.mult, reverse0=True).then_inc(o_done.sem, 1)

            dve.wait_ge(tri_ready, 5)

            with dve.Fori(0, CH) as i:
                start_head(i, 0)
                low_k(i, 0)
                low_q(i, 0)
                for u in range(TT):
                    unit(i, 0, u)
                shift_of(i, 0)
                for n in range(NSTEP):
                    hp, j, e = STEPS[n]
                    b = hp * NT + j
                    if e == 0 and b + 1 < NBLOCK:
                        low_q(i, b + 1)
                    if e == 0 and b % 2 == 0 and b // 2 + 1 < 2 * NKC:
                        low_k(i, b // 2 + 1)
                    if b == NT - 1 and e == 0:
                        start_head(i, 1)
                    if diagonal(n):
                        mask(i, n)
                    for bb, u in units_in(n):
                        unit(i, bb, u)
                    if e == 2 * j and b + 1 < NBLOCK:
                        shift_of(i, b + 1)
                    if n >= 1 and not on_pool(n - 1):
                        add(i, n - 1)
                    if e == 0 and b >= 1:
                        sum_den(i, b - 1)
                    if b >= 1 and e == (3 if j else 1):
                        finish_o(i, b - 1)
                add(i, NSTEP - 1)
                sum_den(i, NBLOCK - 1)
                finish_o(i, NBLOCK - 1)

        @block.tensor
        def _(pe):
            pe.wait_ge(setup, 10)
            nc.tensor.matmul(misc[:, 0:H * NT], keep["ones"][0:H], f_spread[:].rearrange("a h s -> a (h s)"), start=True, stop=True).then_inc(setup_pe, 1)
            pe.wait_ge(setup, 11)
            emitted = {}

            def unit(i, b, u):
                hp, j = divmod(b, NT)
                t, c = tile_and_chunk(b, u)
                k = unit_base[b] + u
                if u == 0:
                    pe.wait_ge(q_high.sem, q_high.at(i, b + 1))
                    if b % 2 == 0:
                        pe.wait_ge(k_low.sem, k_low.at(i, b // 2 + 1))
                pe.wait_ge(mx_done.sem, mx_done.at(i, k - 1))
                width = TILE if c < j else (t + 1) * P
                nc.tensor.matmul(mx[:, k % 2, 0:width], q_all[:, b % 2, t * P:(t + 1) * P],
                                 k_all[hp][:, c * TILE:c * TILE + width], start=True, stop=True).then_inc(mx_ready.sem, 1)

            def spread_shift(i, b):
                pe.wait_ge(shift_ready.sem, shift_ready.at(i, b + 1))
                pe.wait_ge(den_logged.sem, den_logged.at(i, 2 * emitted["dens"]))
                if b >= 1:
                    pe.wait_ge(q_shift.sem, q_shift.at(i, b))
                nc.tensor.matmul(misc[:], ones_r[:], shift[:].rearrange("p t q -> p (t q)"), start=True, stop=True).then_inc(shift_turned.sem, 1)
                emitted["shifts"] = b + 1

            def scores(i, n):
                hp, j, e = STEPS[n]
                b = hp * NT + j
                if e == 0:
                    pe.wait_ge(q_shift.sem, q_shift.at(i, b + 1))
                    pe.wait_ge(q_low.sem, q_low.at(i, b + 1))
                pe.wait_ge(exp_done.sem, exp_done.at(i, n - 1))
                for half in range(2):
                    blk = 2 * e + half
                    first = lo(n, half)
                    keys = slice(blk * P, (blk + 1) * P)
                    nc.tensor.matmul(st[:, n % 2, half, first:TILE], k_all[hp][:, keys], q_all[:, b % 2, first:TILE], start=True, stop=False)
                    last = nc.tensor.matmul(st[:, n % 2, half, first:TILE], k_one[hp][:, keys], q_one[:, b % 2, first:TILE], start=False, stop=True)
                last.then_inc(st_ready.sem, 1)

            def weigh(i, n):
                hp, j, e = STEPS[n]
                b = hp * NT + j
                pe.wait_ge(exp_done.sem, exp_done.at(i, n + 1))
                if e == 0:
                    pe.wait_ge(o_copied.sem, o_copied.at(i, b))
                    if j == 0:
                        pe.wait_ge(v_loaded[hp], i * 16 + 16)
                for half in range(2):
                    first = lo(n, half) if b % NT or e else 0
                    last = nc.tensor.matmul(o_ps[half * HD:(half + 1) * HD, first:TILE], v[:, hp, 2 * e + half],
                                            probs[:, n % RING, half, first:TILE], start=(e == 0), stop=(e == 2 * j + 1))
                last.then_inc(pv_done.sem, 1)

            def denominators(i, b):
                pe.wait_ge(den_sum.sem, den_sum.at(i, 2 * b + 2))
                pe.wait_ge(q_shift.sem, q_shift.at(i, emitted["shifts"]))
                pe.wait_ge(den_logged.sem, den_logged.at(i, 2 * b))
                emitted["dens"] = b + 1
                nc.tensor.matmul(misc[:], keep["ones"][:], den_dve[:, b % 2, 0], start=True, stop=True).then_inc(den_ready.sem, 1)

            with pe.Fori(0, CH) as i:
                emitted["dens"] = 0
                for u in range(TT):
                    unit(i, 0, u)
                spread_shift(i, 0)
                for n in range(NSTEP):
                    hp, j, e = STEPS[n]
                    b = hp * NT + j
                    scores(i, n)
                    for bb, u in units_in(n):
                        unit(i, bb, u)
                    if e == 2 * j + 1 and b + 1 < NBLOCK:
                        spread_shift(i, b + 1)
                    if n >= 1:
                        weigh(i, n - 1)
                    if e == 1 and b >= 1:
                        denominators(i, b - 1)
                weigh(i, NSTEP - 1)
                denominators(i, NBLOCK - 1)


BANDS_READY = 25
LAST_COPY = 30


def phase_gates(nc, io, keep):
    NW = 3 * W
    HALO = 16
    with ExitStack() as ctx:
        m = Alloc(nc, ctx, "ga")
        w_high = m.sb("w_high", [P, KC, NW], F32R)
        w_low = m.sb("w_low", [P, KC, NW], F32R)
        norm_col = m.sb("norm_col", [P, KC])
        h_t = m.sb("h_t", [P, KC, TILE])
        h_high = m.sb("h_high", [P, KC, TILE], F32R)
        h_low = m.sb("h_low", [P, KC, TILE], F32R)
        stage = m.sb("stage", [P, 2, CH, TILE])
        pool_stage, gate_stage = stage[:, 0], stage[:, 1]
        w_raw = stage[:].rearrange("p a c t -> p (a c t)")
        u_t = m.sb("u_t", [P, CH, HALO + TILE])
        sums = m.sb("sums", [P, 2, HALO + TILE])
        early = m.sb("early", [P, CH, HALO])
        pooled_high = m.sb("pooled_high", [P, TILE], F32R)
        pooled_low = m.sb("pooled_low", [P, TILE], F32R)
        sig = m.sb("sig", [P, 2, TILE])
        pw_raw = m.sb("pw_raw", [P, CH, P])
        pw_high = m.sb("pw_high", [P, CH, P], F32R)
        pw_low = m.sb("pw_low", [P, CH, P], F32R)
        scale_col = m.sb("scale_col", [P, CH])
        hist = m.sb("hist", [DB * HIST, W])
        us_rows = m.sb("us_rows", [NS, W])
        sig_s = m.sb("sig_s", [NS, 2, W])
        scale_row = m.sb("scale_row", [NS, W])
        band_hist = m.sb("band_hist", [DB * HIST, CH, NS])
        band_new = m.sb("band_new", [NS, CH, NS])
        pooled_s = m.sb("pooled_s", [P, CH, NS])
        u_last = scale_row[0:HIST]

        acc = m.ps("acc", [P, 3, TILE])
        mixed = m.ps("mixed", [P, 2, TILE])
        s_ps = m.ps("s_ps", [P, CH, NS])
        last_ps = m.ps("last_ps", [HIST, W])

        const_loaded = m.sem("const_loaded")
        w_loaded = [m.sem(f"w_loaded{i}") for i in range(2)]
        w_high_ready = m.sem("w_high_ready")
        w_low_dve = m.sem("w_low_dve")
        w_low_pool = m.sem("w_low_pool")
        h_loaded = m.sem("h_loaded")
        h_split = Count(m.sem("h_split"), KC)
        bands = m.sem("bands")
        setup = m.sem("setup")
        s_done = m.sem("s_done")
        s_sig = m.sem("s_sig")
        s_pooled = m.sem("s_pooled")
        s_stored = m.sem("s_stored")
        acc_done = Count(m.sem("acc_done"), 12)
        u_evac = Count(m.sem("u_evac"), CH)
        sig_ready = Count(m.sem("sig_ready"), 2 * CH)
        gate_done = Count(m.sem("gate_done"), 2 * CH, 3)
        halo_free = Count(m.sem("halo_free"), CH, CH)
        pooled_ready = Count(m.sem("pooled_ready"), CH)
        mixed_done = Count(m.sem("mixed_done"), CH)
        pool_out = Count(m.sem("pool_out"), CH, 2)
        PER = 4 * CH + sum(g + 1 for g in range(CH))
        dve_chain = m.sem("dve_chain")
        pool_stored = m.sem("pool_stored")
        gate_stored = m.sem("gate_stored")
        last_turned = m.sem("last_turned")

        w_in = io["w_in"][0]
        SPLIT = 640

        block = ctx.enter_context(nc.Block())

        @block.sync
        def _(sp):
            sp.dma_start(norm_col[:], io["norm_w"].rearrange("l (c p) -> p (l c)", p=P), allow_slow_non_contiguous=True).then_inc(const_loaded, 16)
            sp.dma_start(scale_col[:], io["pool_scale"].rearrange("l (c p) -> p (l c)", p=P), allow_slow_non_contiguous=True).then_inc(const_loaded, 16)
            sp.dma_start(scale_row[:], io["pool_scale"].to_broadcast([NS, W])).then_inc(const_loaded, 16)
            for c in range(KC):
                if c >= 2:
                    sp.wait_ge(w_low_dve, c - 1)
                    sp.wait_ge(w_low_pool, c - 1)
                rows = w_in[c * P:(c + 1) * P]
                slot = w_raw[:, (c % 2) * NW:(c % 2 + 1) * NW]
                sp.dma_start(slot[:, 0:2 * W], rows[:, U0:U0 + 2 * W]).then_inc(w_loaded[c % 2], 16)
                sp.dma_start(slot[:, 2 * W:NW], rows[:, GA0:GA0 + W]).then_inc(w_loaded[c % 2], 16)
                if c == 1:
                    sp.dma_start(h_t[:], io["h_t"][0]).then_inc(h_loaded, 16)
                    sp.dma_start(pw_raw[:], io["pool_w"].rearrange("l g c d -> c (l g) d")).then_inc(const_loaded, 16)
                    sp.dma_start(hist[:], io["state_pool"].rearrange("l b i c -> (l b i) c")).then_inc(const_loaded, 16)
            sp.dma_start(io["pool_sample"][0, :, 0:HIST - DS], io["state_pool"][0, :, DS:HIST]).then_inc(s_stored, 16)
            sp.wait_ge(s_sig, 1)
            for b in range(DB):
                sp.dma_start(io["pool_sample"][0, b, HIST - DS:HIST], us_rows[b * DS:(b + 1) * DS]).then_inc(s_stored, 16)

            def super_tile(s, more):
                if more:
                    sp.wait_ge(h_split.sem, h_split.at(s, KC))
                    sp.dma_start(h_t[:], io["h_t"][bass.ds(s + 1, 1)].rearrange("a p k t -> p (a k) t")).then_inc(h_loaded, 16)
                sp.wait_ge(pool_out.sem, pool_out.at(s, CH))
                sp.dma_start(io["pool_t"].rearrange("c p t -> p c t")[:, :, bass.ds(s * TILE, TILE)], pool_stage).then_inc(pool_stored, 16)
                sp.wait_ge(gate_done.sem, gate_done.at(s, 2 * CH))
                sp.dma_start(io["gate_t"].rearrange("c p t -> p c t")[:, :, bass.ds(s * TILE, TILE)], gate_stage).then_inc(gate_stored, 16)

            with sp.Fori(0, NT - 1) as s:
                super_tile(s, True)
            super_tile(NT - 1, False)
            sp.wait_ge(setup, LAST_COPY)
            sp.dma_start(io["pool_prompt"].rearrange("l b i c -> (l b i) c"), u_last).then_inc(s_stored, 16)
            sp.wait_ge(s_stored, 16 * (DB + 2))
            sp.wait_ge(pool_stored, 16 * (NT + 1))
            sp.wait_ge(gate_stored, 16 * (NT + 1))

        @block.gpsimd
        def _(pool):
            for c in (gate_done, halo_free, pool_out):
                pool.sem_inc(c.sem, c.credit)
            pool.sem_inc(pool_stored, 16)
            pool.sem_inc(gate_stored, 16)
            for c in range(KC):
                pool.wait_ge(w_high_ready, c + 1)
                raw = w_raw[:, (c % 2) * NW:(c % 2) * NW + SPLIT]
                nc.gpsimd.tensor_tensor(w_low[:, c, 0:SPLIT], raw, w_high[:, c, 0:SPLIT].bitcast(F32), ALU.subtract).then_inc(w_low_pool, 1)
            n = 0
            for g, w in enumerate(WINDOWS):
                old, new = band_hist[:, g].rearrange("p (b t) -> p b t", b=DB), band_new[:, g].rearrange("p (b t) -> p b t", b=DB)
                steps = [lambda: nc.gpsimd.memset(old, 1.0 / w), lambda: nc.gpsimd.memset(new, 1.0 / w)]
                steps += [lambda o=o, a=a, p=p, k=k: nc.gpsimd.affine_select(out=o, in_=o, compare_op=ALU.is_ge, fill=0.0,
                                                                           base=a, pattern=p, channel_multiplier=k)
                          for o, a, p, k in ((old, w - HIST - 1, [[-HIST, DB], [-1, DS]], 1), (old, HIST - 1, [[HIST, DB], [0, DS]], -1),
                                             (new, 0, [[-DS, DB], [0, DS]], 1), (new, 0, [[DS, DB], [1, DS]], -1),
                                             (new, w - 1, [[-DS, DB], [-1, DS]], 1))]
                for step in steps:
                    n += 1
                    step().then_inc(bands, 1)
                    pool.wait_ge(bands, n)

        @block.scalar
        def _(act):
            for n in range(3):
                act.wait_ge(s_done, n + 1)
                if n == 0:
                    nc.scalar.activation(us_rows[:], acc[0:NS, 0], ACT.Copy).then_inc(s_sig, 1)
                else:
                    nc.scalar.activation(sig_s[:, n - 1], acc[0:NS, n], ACT.Sigmoid).then_inc(s_sig, 1)

            def super_tile(s):
                for u in range(3 * CH):
                    act.wait_ge(acc_done.sem, acc_done.at(s, u + 1))
                    if u < CH:
                        act.wait_ge(halo_free.sem, halo_free.at(s, u + 1 - CH))
                        nc.scalar.activation(u_t[:, u, HALO:], acc[:, u % 3], ACT.Copy).then_inc(u_evac.sem, 1)
                    else:
                        k = u - CH
                        act.wait_ge(gate_done.sem, gate_done.at(s, k - 1))
                        nc.scalar.activation(sig[:, k % 2], acc[:, u % 3], ACT.Sigmoid).then_inc(sig_ready.sem, 1)

            with act.Fori(0, NT) as s:
                super_tile(s)

        @block.vector
        def _(dve):
            n_setup = [0]

            def link(ins):
                n_setup[0] += 1
                ins.then_inc(setup, 1)
                dve.wait_ge(setup, n_setup[0])

            for g in range(CH):
                link(nc.vector.memset(u_t[:, g, 0:HALO], 0.0))
            link(nc.vector.memset(early[:], 1.0))
            for g, w in enumerate(WINDOWS):
                for t in range(w - 1):
                    last = nc.vector.memset(early[:, g, t:t + 1], w / (t + 1))
            link(last)
            dve.wait_ge(const_loaded, 48)

            for c in range(KC):
                dve.wait_ge(w_loaded[c % 2], 32 * (c // 2 + 1))
                raw = w_raw[:, (c % 2) * NW:(c % 2 + 1) * NW]
                link(nc.vector.tensor_scalar(raw, raw, norm_col[:, c:c + 1], None, ALU.mult))
                link(nc.vector.tensor_copy(w_high[:, c], raw))
                nc.vector.nop().then_inc(w_high_ready, 1)
                nc.vector.tensor_tensor(w_low[:, c, SPLIT:], raw[:, SPLIT:], w_high[:, c, SPLIT:].bitcast(F32), ALU.subtract).then_inc(w_low_dve, 1)
            dve.wait_ge(const_loaded, 80)
            link(nc.vector.tensor_copy(pw_high[:], pw_raw[:]))
            link(nc.vector.tensor_tensor(pw_low[:], pw_raw[:], pw_high[:].bitcast(F32), ALU.subtract))

            def split_h(s, chain):
                dve.wait_ge(h_loaded, s * 16 + 16)
                for c in range(KC):
                    chain.link(nc.vector.tensor_copy(h_high[:, c], h_t[:, c]))
                    nc.vector.tensor_tensor(h_low[:, c], h_t[:, c], h_high[:, c].bitcast(F32), ALU.subtract).then_inc(h_split.sem, 1)

            dve.wait_ge(bands, 7 * CH)
            for g in range(CH):
                last = nc.vector.tensor_tensor(band_new[:, g], band_new[:, g], keep["ident"][0:NS, 0:NS], ALU.subtract)
            link(last)
            ready = n_setup[0]
            dve.wait_ge(s_pooled, 1)
            link(nc.vector.tensor_copy(pooled_s[:], s_ps[:]))
            dve.wait_ge(s_sig, 3)
            link(nc.vector.tensor_tensor(sig_s[:, 0], acc[0:NS, 1], sig_s[:, 0], ALU.mult))
            link(nc.vector.tensor_tensor(sig_s[:, 0], sig_s[:, 0], scale_row[:], ALU.mult))
            nc.vector.tensor_tensor(keep["mix_s"][:, W:D], acc[0:NS, 2], sig_s[:, 1], ALU.mult).then_inc(s_pooled, 1)
            dve.wait_ge(s_pooled, 3)
            link(nc.vector.tensor_tensor(keep["mix_s"][:, 0:W], mixed[0:NS, 0], sig_s[:, 0], ALU.mult))
            nc.vector.nop().then_inc(s_pooled, 1)

            first = Chain(dve, dve_chain)
            split_h(0, first)
            base = first.n

            def super_tile(s, more):
                chain = Chain(dve, dve_chain, s * (PER + KC) + base)
                for g, w in enumerate(WINDOWS):
                    dve.wait_ge(u_evac.sem, u_evac.at(s, g + 1))
                    src, step = u_t[:, g], 1
                    for r in range(g + 1):
                        dst = sums[:, r % 2]
                        chain.link(nc.vector.tensor_tensor(dst[:, 2 * step - 1 if r < g else HALO:], src[:, 2 * step - 1 if r < g else HALO:],
                                                           src[:, (2 * step - 1 if r < g else HALO) - step:HALO + TILE - step], ALU.add))
                        src, step = dst, step * 2
                    chain.link(nc.vector.tensor_tensor(src[:, HALO:2 * HALO], src[:, HALO:2 * HALO], early[:, g], ALU.mult))
                    chain.link(nc.vector.scalar_tensor_tensor(out=src[:, HALO:], in0=src[:, HALO:], scalar=1.0 / w, in1=u_t[:, g, HALO:],
                                                              op0=ALU.mult, op1=ALU.subtract))
                    pooled = src[:, HALO:]
                    nc.vector.tensor_copy(u_t[:, g, 0:HALO], u_t[:, g, TILE:]).then_inc(halo_free.sem, 1)
                    dve.wait_ge(mixed_done.sem, mixed_done.at(s, g)) if g else None
                    if g == 0:
                        dve.wait_ge(pool_out.sem, pool_out.at(s, 0))
                    chain.link(nc.vector.tensor_copy(pooled_high[:], pooled))
                    chain.link(nc.vector.tensor_tensor(pooled_low[:], pooled, pooled_high[:].bitcast(F32), ALU.subtract))
                    nc.vector.nop().then_inc(pooled_ready.sem, 1)
                    if g == 0:
                        dve.wait_ge(pool_stored, s * 16 + 16)
                    dve.wait_ge(sig_ready.sem, sig_ready.at(s, g + 1))
                    gate = pool_stage[:, g]
                    nc.vector.tensor_tensor(gate, acc[:, (CH + g) % 3], sig[:, g % 2], ALU.mult).then_inc(gate_done.sem, 1)
                    dve.wait_ge(gate_done.sem, gate_done.at(s, g + 1))
                    dve.wait_ge(mixed_done.sem, mixed_done.at(s, g + 1))
                    nc.vector.scalar_tensor_tensor(out=gate, in0=mixed[:, g % 2], scalar=scale_col[:, g:g + 1], in1=gate,
                                                   op0=ALU.mult, op1=ALU.mult).then_inc(pool_out.sem, 1)
                for c in range(CH):
                    k = CH + c
                    if c == 0:
                        dve.wait_ge(gate_stored, s * 16 + 16)
                    dve.wait_ge(sig_ready.sem, sig_ready.at(s, k + 1))
                    nc.vector.tensor_tensor(gate_stage[:, c], acc[:, (CH + k) % 3], sig[:, k % 2], ALU.mult).then_inc(gate_done.sem, 1)
                    if c == CH - 1:
                        nc.vector.memset(early[:], 1.0)
                        if more:
                            split_h(s + 1, chain)
                assert chain.n == PER + (KC if more else 0), (chain.n, PER)

            with dve.Fori(0, NT - 1) as s:
                super_tile(s, True)
            super_tile(NT - 1, False)
            dve.wait_ge(last_turned, 1)
            link(nc.vector.tensor_copy(u_last, last_ps[:]))
            assert n_setup[0] == LAST_COPY, n_setup

        @block.tensor
        def _(pe):
            pe.wait_ge(w_low_dve, KC)
            pe.wait_ge(w_low_pool, KC)
            for n in range(3):
                cols = slice(n * W, (n + 1) * W)
                for c in range(KC):
                    last = three_pass(nc, acc[0:NS, n], keep["hs_high"][:, c], keep["hs_low"][:, c],
                                      w_high[:, c, cols], w_low[:, c, cols], c == 0, c == KC - 1)
                last.then_inc(s_done, 1)
            pe.wait_ge(setup, BANDS_READY)
            pe.wait_ge(s_sig, 1)
            for g in range(CH):
                cols = slice(g * P, (g + 1) * P)
                nc.tensor.matmul(s_ps[:, g], hist[:, cols], band_hist[:, g], start=True, stop=False)
                last = nc.tensor.matmul(s_ps[:, g], us_rows[:, cols], band_new[:, g], start=False, stop=True)
            last.then_inc(s_pooled, 1)
            pe.wait_ge(setup, BANDS_READY + 1)
            for g in range(CH):
                last = nc.tensor.matmul(mixed[0:NS, 0, g * P:(g + 1) * P], pooled_s[:, g], pw_raw[:, g], start=True, stop=True)
            last.then_inc(s_pooled, 1)
            pe.wait_ge(s_pooled, 4)

            def super_tile(s):
                for u in range(3 * CH):
                    if u < 3:
                        pe.wait_ge(gate_done.sem, gate_done.at(s, u - 2))
                    elif u < CH + 3:
                        pe.wait_ge(u_evac.sem, u_evac.at(s, u - 2))
                    else:
                        pe.wait_ge(gate_done.sem, gate_done.at(s, u - CH - 2))
                    cols = slice(u * P, (u + 1) * P)
                    for c in range(KC):
                        if u == 0:
                            pe.wait_ge(h_split.sem, h_split.at(s, c + 1))
                        last = three_pass(nc, acc[:, u % 3], w_high[:, c, cols], w_low[:, c, cols],
                                          h_high[:, c], h_low[:, c], c == 0, c == KC - 1)
                    last.then_inc(acc_done.sem, 1)
                    if CH <= u < 2 * CH:
                        g = u - CH
                        pe.wait_ge(pooled_ready.sem, pooled_ready.at(s, g + 1))
                        pe.wait_ge(pool_out.sem, pool_out.at(s, g - 1))
                        three_pass(nc, mixed[:, g % 2], pw_high[:, g], pw_low[:, g], pooled_high[:], pooled_low[:],
                                   True, True).then_inc(mixed_done.sem, 1)

            with pe.Fori(0, NT) as s:
                super_tile(s)
            for g in range(CH):
                last = nc.tensor.transpose(last_ps[:, g * P:(g + 1) * P], u_t[:, g, HALO + TILE - HIST:], keep["ident"][:])
            last.then_inc(last_turned, 1)


def phase_merge(nc, io, keep):
    UNIT = 2 * P
    A0, A1, GATE, POOL = range(4)
    with ExitStack() as ctx:
        m = Alloc(nc, ctx, "mg")
        w_high = m.sb("w_high", [P, KC, D], F32R)
        w_low = m.sb("w_low", [P, KC, D], F32R)
        w_raw = m.sb("w_raw", [P, 2, D])
        raw = m.sb("raw", [P, 2, 4, CH, UNIT])
        mix_high = m.sb("mix_high", [P, 2, KC, UNIT], F32R)
        mix_low = m.sb("mix_low", [P, 2, KC, UNIT], F32R)
        x = m.sb("x", [P, TT, D])
        norm_row = m.sb("norm_row", [P, D])
        junk = m.sb("junk", [P, D], BF16)
        squares = m.sb("squares", [P, TT])
        rms = m.sb("rms", [P, TT])
        minus_half = m.sb("minus_half", [P, 1])
        eps_sum = m.sb("eps_sum", [P, 1])
        xs = m.sb("xs", [NS, D])
        attn_s = m.sb("attn_s", [NS, W])
        ms_high = m.sb("ms_high", [P, KC, NS], F32R)
        ms_low = m.sb("ms_low", [P, KC, NS], F32R)

        acc = m.ps("acc", [P, 2, D])
        s_ps = m.ps("s_ps", [P, KC, NS])

        const_loaded = m.sem("const_loaded")
        w_loaded = [m.sem(f"w_loaded{i}") for i in range(2)]
        w_split = m.sem("w_split")
        setup = m.sem("setup")
        s_turned = m.sem("s_turned")
        s_split = m.sem("s_split")
        s_done = m.sem("s_done")
        s_squares = m.sem("s_squares")
        s_rms = m.sem("s_rms")
        s_ready = m.sem("s_ready")
        s_stored = m.sem("s_stored")
        raw_loaded = [m.sem(f"raw_loaded{i}") for i in range(2)]
        raw_free = [m.sem(f"raw_free{i}") for i in range(2)]
        x_loaded = [m.sem(f"x_loaded{i}") for i in range(2)]
        y_stored = [m.sem(f"y_stored{i}") for i in range(2)]
        mix_ready = Count(m.sem("mix_ready"), 2)
        acc_done = Count(m.sem("acc_done"), TT, TT)
        added = Count(m.sem("added"), TT, 2)
        squares_ready = Count(m.sem("squares_ready"), TT)
        rms_ready = Count(m.sem("rms_ready"), TT)
        y_ready = Count(m.sem("y_ready"), TT)
        dve_chain = m.sem("dve_chain")
        pool_chain = m.sem("pool_chain")

        x_in = io["x_prompt"][0].rearrange("(u k p) d -> p u k d", p=P, k=2)
        y_out = io["y_prompt"][0].rearrange("(u k p) d -> p u k d", p=P, k=2)

        block = ctx.enter_context(nc.Block())

        @block.sync
        def _(sp):
            def load_mix(g, b):
                at = bass.ds(g * TILE + b * UNIT, UNIT)
                for kind, src in ((POOL, io["pool_t"]), (A0, io["attn_t"][0]), (A1, io["attn_t"][1]), (GATE, io["gate_t"])):
                    sp.dma_start(raw[:, b, kind], src.rearrange("c p t -> p c t")[:, :, at]).then_inc(raw_loaded[b], 16)

            def load_x(g, b):
                sp.dma_start(x[:, 2 * b:2 * b + 2], x_in[:, bass.ds(g * 2 + b, 1)].rearrange("p a k d -> p (a k) d")).then_inc(x_loaded[b], 16)

            def store_y(g, b):
                sp.wait_ge(y_ready.sem, y_ready.at(g, 2 * b + 2))
                sp.dma_start(y_out[:, bass.ds(g * 2 + b, 1)].rearrange("p a k d -> p (a k) d"), x[:, 2 * b:2 * b + 2]).then_inc(y_stored[b], 16)

            for c in range(KC):
                if c >= 2:
                    sp.wait_ge(w_split, c - 1)
                sp.dma_start(w_raw[:, c % 2], io["w_out"][0, c * P:(c + 1) * P]).then_inc(w_loaded[c % 2], 16)
                if c == 1:
                    sp.dma_start(attn_s[:], io["attn_s"]).then_inc(const_loaded, 16)
                    sp.dma_start(xs[:], io["x_sample"].rearrange("b t d -> (b t) d")).then_inc(const_loaded, 16)
                    sp.dma_start(norm_row[:], io["norm_f"].rearrange("(a d) -> a d", a=1).to_broadcast([P, D])).then_inc(const_loaded, 16)
            for b in range(2):
                load_mix(0, b)
                load_x(0, b)
            sp.wait_ge(s_ready, 1)
            sp.dma_start(io["y_sample"].rearrange("b t d -> (b t) d"), xs[:]).then_inc(s_stored, 16)

            with sp.Fori(0, NT - 1) as g:
                for b in range(2):
                    sp.wait_ge(raw_free[b], g + 1)
                    load_mix(g + 1, b)
                    store_y(g, b)
                    sp.wait_ge(y_stored[b], g * 16 + 16)
                    load_x(g + 1, b)
            for b in range(2):
                store_y(NT - 1, b)
            sp.wait_ge(s_stored, 16)
            for b in range(2):
                sp.wait_ge(y_stored[b], NT * 16)

        @block.gpsimd
        def _(pool):
            pool.sem_inc(acc_done.sem, acc_done.credit)
            pool.sem_inc(added.sem, added.credit)
            nc.gpsimd.memset(minus_half[:], -0.5)
            nc.gpsimd.memset(eps_sum[:], D * EPS).then_inc(pool_chain, 1)
            pool.wait_ge(pool_chain, 1)

            def rms_of(rows, n, done, chain):
                out = rms[0:rows, n:n + 1]
                chain.link(nc.gpsimd.tensor_tensor(out, squares[0:rows, n:n + 1], eps_sum[0:rows], ALU.add))
                nc.gpsimd.tensor_tensor(out, out, minus_half[0:rows], ALU.pow).then_inc(done, 1)

            pool.wait_ge(s_squares, 1)
            rms_of(NS, 0, s_rms, Chain(pool, pool_chain, 1))
            with pool.Fori(0, NT) as g:
                chain = Chain(pool, pool_chain, g * TT + 2)
                for t in range(TT):
                    pool.wait_ge(squares_ready.sem, squares_ready.at(g, t + 1))
                    rms_of(P, t, rms_ready.sem, chain)

        @block.scalar
        def _(act):
            act.wait_ge(s_done, 2)
            nc.scalar.activation(junk[0:NS], xs[:], ACT.Square, accum_out=squares[0:NS, 0:1]).then_inc(s_squares, 1)
            act.wait_ge(s_ready, 1)
            with act.Fori(0, NT) as g:
                for t in range(TT):
                    act.wait_ge(added.sem, added.at(g, t + 1))
                    if t:
                        act.wait_ge(squares_ready.sem, squares_ready.at(g, t))
                    nc.scalar.activation(junk[:], x[:, t], ACT.Square, accum_out=squares[:, t:t + 1]).then_inc(squares_ready.sem, 1)
                act.wait_ge(squares_ready.sem, squares_ready.at(g, TT))

        @block.vector
        def _(dve):
            start = Chain(dve, setup)
            for c in range(KC):
                dve.wait_ge(w_loaded[c % 2], 16 * (c // 2 + 1))
                start.link(nc.vector.tensor_copy(w_high[:, c], w_raw[:, c % 2]))
                nc.vector.tensor_tensor(w_low[:, c], w_raw[:, c % 2], w_high[:, c].bitcast(F32), ALU.subtract).then_inc(w_split, 1)
                if c == 1:
                    dve.wait_ge(const_loaded, 48)
                    start.link(nc.vector.tensor_tensor(keep["mix_s"][:, W:D], keep["mix_s"][:, W:D], attn_s[:], ALU.mult))
                    nc.vector.nop().then_inc(s_split, 1)
                    start.link(nc.vector.tensor_scalar(norm_row[:], norm_row[:], ROOT_D, None, ALU.mult))
                if c == 2:
                    dve.wait_ge(s_turned, 1)
                    start.link(nc.vector.tensor_copy(ms_high[:], s_ps[:]))
                    nc.vector.tensor_tensor(ms_low[:], s_ps[:], ms_high[:].bitcast(F32), ALU.subtract).then_inc(s_split, 1)

            def split_mix(g, b, chain):
                dve.wait_ge(raw_loaded[b], g * 64 + 64)
                dve.wait_ge(acc_done.sem, acc_done.at(g, 2 * b + 2 - TT))
                r, high, low = raw[:, b], mix_high[:, b], mix_low[:, b]
                nc.vector.tensor_tensor(r[:, A0], r[:, A0], r[:, A1], ALU.add)
                chain.link(nc.vector.tensor_copy(high[:, 0:CH], r[:, POOL]))
                nc.vector.tensor_tensor(low[:, 0:CH], r[:, POOL], high[:, 0:CH].bitcast(F32), ALU.subtract)
                chain.link(nc.vector.tensor_tensor(r[:, A0], r[:, A0], r[:, GATE], ALU.mult))
                chain.link(nc.vector.tensor_copy(high[:, CH:KC], r[:, A0]))
                nc.vector.tensor_tensor(low[:, CH:KC], r[:, A0], high[:, CH:KC].bitcast(F32), ALU.subtract).then_inc(mix_ready.sem, 1)
                nc.vector.nop().then_inc(raw_free[b], 1)

            def add_x(g, t):
                if t % 2 == 0:
                    dve.wait_ge(x_loaded[t // 2], g * 16 + 16)
                dve.wait_ge(acc_done.sem, acc_done.at(g, t + 1))
                nc.vector.tensor_tensor(x[:, t], acc[:, t % 2], x[:, t], ALU.add).then_inc(added.sem, 1)

            def scale(g, t):
                dve.wait_ge(rms_ready.sem, rms_ready.at(g, t + 1))
                nc.vector.scalar_tensor_tensor(out=x[:, t], in0=x[:, t], scalar=rms[:, t:t + 1], in1=norm_row[:],
                                               op0=ALU.mult, op1=ALU.mult).then_inc(y_ready.sem, 1)

            split_mix(0, 0, Chain(dve, dve_chain))
            dve.wait_ge(s_done, 1)
            nc.vector.tensor_tensor(xs[:], acc[0:NS, 0], xs[:], ALU.add).then_inc(s_done, 1)
            dve.wait_ge(s_rms, 1)
            nc.vector.scalar_tensor_tensor(out=xs[:], in0=xs[:], scalar=rms[0:NS, 0:1], in1=norm_row[0:NS],
                                           op0=ALU.mult, op1=ALU.mult).then_inc(s_ready, 1)

            def finish(g, b):
                add_x(g, 2 * b)
                scale(g, 2 * b)
                add_x(g, 2 * b + 1)

            def step(g, last):
                split_mix(g, 1, Chain(dve, dve_chain, g * 6 + 3))
                finish(g, 0)
                if not last:
                    split_mix(g + 1, 0, Chain(dve, dve_chain, g * 6 + 6))
                scale(g, 1)
                finish(g, 1)
                scale(g, 3)

            with dve.Fori(0, NT - 1) as g:
                step(g, False)
            step(NT - 1, True)

        @block.tensor
        def _(pe):
            pe.wait_ge(s_split, 1)
            for c in range(KC):
                last = nc.tensor.transpose(s_ps[:, c], keep["mix_s"][:, c * P:(c + 1) * P], keep["ident"][0:NS, 0:NS])
            last.then_inc(s_turned, 1)
            pe.wait_ge(s_split, 2)
            for c in range(KC):
                pe.wait_ge(w_split, c + 1)
                for half in range(2):
                    cols = slice(half * W, (half + 1) * W)
                    last = three_pass(nc, acc[0:NS, 0, cols], ms_high[:, c], ms_low[:, c], w_high[:, c, cols], w_low[:, c, cols],
                                      c == 0, c == KC - 1)
            last.then_inc(s_done, 1)
            pe.wait_ge(s_done, 2)

            with pe.Fori(0, NT) as g:
                for t in range(TT):
                    b, tile = t // 2, slice(t % 2 * P, (t % 2 + 1) * P)
                    if t % 2 == 0:
                        pe.wait_ge(mix_ready.sem, mix_ready.at(g, b + 1))
                    pe.wait_ge(added.sem, added.at(g, t - 1))
                    for half in range(2):
                        cols = slice(half * W, (half + 1) * W)
                        for c in range(KC):
                            last = three_pass(nc, acc[:, t % 2, cols], mix_high[:, b, c, tile], mix_low[:, b, c, tile],
                                              w_high[:, c, cols], w_low[:, c, cols], c == 0, c == KC - 1)
                    last.then_inc(acc_done.sem, 1)


def phase_decode(nc, io, keep):
    HB = DB // 2
    PG = 2
    STEP = PG * PAGE
    RING = 4
    STEPS = NPAGE // PG
    ITERS = STEPS // RING
    PAST = NPAGE * PAGE
    R = HB * H * DS
    with ExitStack() as ctx:
        m = Alloc(nc, ctx, "dc")
        table = m.sb("table", [1, DB * NPAGE], I32)
        page_of = m.sb("page_of", [P, 2], I32)
        lf_pages = m.sb("lf_pages", [P, 2, PAGE * H])
        lf_rows = m.sb("lf_rows", [P, NPAGE, R])
        after = m.sb("after", [P, NPAGE])
        pages = m.sb("pages", [P, RING, HB, PG, W])
        k_t = m.sb("k_t", [P, 2, HB, CH, STEP])
        s = m.sb("s", [P, PAST + NS])
        probs = m.sb("probs", [P, RING, STEP])
        probs_new = m.sb("probs_new", [P, NS])
        probs_t = m.sb("probs_t", [P, 2, PG, R])
        new_t = m.sb("new_t", [NS, R])
        shift = m.sb("shift", [P, 1])
        sums = m.sb("sums", [P, STEPS + 1])
        inv = m.sb("inv", [P, 1])
        picked = m.sb("picked", [P, 2, W])
        out_s = m.sb("out_s", [NS, W])
        qs = m.sb("qs", [NS, W])
        ks = m.sb("ks", [NS, W])
        vs = m.sb("vs", [NS, W])
        lfs = m.sb("lfs", [NS, H])
        q_blocks = m.sb("q_blocks", [P, DB, CH, H * DS])
        ks_t = m.sb("ks_t", [P, CH, NS])
        later = m.sb("later", [P, PAGE])
        mask_s = m.sb("mask_s", [NS, NS])
        upto_s = m.sb("upto_s", [NS, NS])
        sel = m.sb("sel", [NS, 2, R])
        sel_t = m.sb("sel_t", [P, 2, NS])
        head_sel = m.sb("head_sel", [H, R])
        head_mask = m.sb("head_mask", [P, H])
        lfs_rows = m.sb("lfs_rows", [NS, R])

        kt = m.ps("kt", [P, 4, 512])
        sc = m.ps("sc", [P, 2, 512])
        o = m.ps("o", [P, W])
        misc = m.ps("misc", [P, 512])
        tot_ps, new_ps, pn_ps = misc[:, 0:NPAGE], misc[:, 32:64], misc[0:NS, 64:192]
        hm_ps, sel_ps = misc[:, 192:200], misc[:, 200:264]
        qk_ps = sc[:, 0, 0:2 * CH * NS]

        const_loaded = m.sem("const_loaded")
        table_loaded = m.sem("table_loaded")
        page_loaded = [m.sem(f"page_loaded{k}") for k in range(RING)]
        page_free = [m.sem(f"page_free{k}") for k in range(RING)]
        lf_gathered = m.sem("lf_gathered")
        masks = m.sem("masks")
        consts = m.sem("consts")
        setup = m.sem("setup")
        turned = m.sem("turned")
        lf_turned = m.sem("lf_turned")
        lf_ready = m.sem("lf_ready")
        tot_done = m.sem("tot_done")
        after_ready = m.sem("after_ready")
        bias_done = m.sem("bias_done")
        bias_evac = m.sem("bias_evac")
        new_done = m.sem("new_done")
        kt_done = m.sem("kt_done")
        kt_evac_act = m.sem("kt_evac_act")
        kt_evac_dve = m.sem("kt_evac_dve")
        sc_done = m.sem("sc_done")
        sc_evac = m.sem("sc_evac")
        shift_ready = m.sem("shift_ready")
        exp_done = m.sem("exp_done")
        exp_new = m.sem("exp_new")
        new_turned = m.sem("new_turned")
        new_copied = m.sem("new_copied")
        pt_done = m.sem("pt_done")
        pt_copied = m.sem("pt_copied")
        o_picked = m.sem("o_picked")
        dve_chain = m.sem("dve_chain")
        out_done = m.sem("out_done")
        out_copied = m.sem("out_copied")
        out_stored = m.sem("out_stored")

        block = ctx.enter_context(nc.Block())

        @block.sync
        def _(sp):
            sp.dma_start(table[:], io["page_table"].rearrange("(a b) p -> a (b p)", a=1)).then_inc(table_loaded, 16)
            sp.dma_start(page_of[:], io["page_table"].rearrange("(f b) p -> (b p) f", f=2), allow_slow_non_contiguous=True).then_inc(table_loaded, 16)
            sp.dma_start(qs[:], io["q_s"]).then_inc(const_loaded, 16)
            sp.dma_start(ks[:], io["k_sample"].rearrange("l b t h d -> (l b t) (h d)")).then_inc(const_loaded, 16)
            sp.dma_start(vs[:], io["v_sample"].rearrange("l b t h d -> (l b t) (h d)")).then_inc(const_loaded, 16)
            sp.dma_start(lfs[:], io["logf_sample"].rearrange("l b t h -> (l b t) h")).then_inc(const_loaded, 16)
            sp.wait_ge(table_loaded, 32)
            for half in range(2):
                for kind, cache in enumerate((io["cache_k"], io["cache_v"])):
                    rows = cache[0].rearrange("n t h d -> t n (h d)")
                    with sp.Fori(0, ITERS) as j:
                        for k in range(RING):
                            sp.wait_ge(page_free[k], j + ((half * 2 + kind) * ITERS + 1))
                            for b in range(HB):
                                for g in range(PG):
                                    at = j * (RING * PG) + ((half * HB + b) * NPAGE + k * PG + g)
                                    page = sp.value_load(table[0:1, bass.ds(at, 1)], min_val=0, max_val=cache.shape[1] - 1)
                                    sp.dma_start(pages[:, k, b, g], rows[:, bass.ds(page, 1)].rearrange("t n c -> t (n c)")).then_inc(page_loaded[k], 16)
            sp.wait_ge(out_copied, 1)
            sp.dma_start(io["attn_s"], out_s[:]).then_inc(out_stored, 16)
            sp.wait_ge(out_stored, 16)

        @block.gpsimd
        def _(pool):
            for k in range(RING):
                pool.sem_inc(page_free[k], 1)
            for sem in (kt_evac_act, kt_evac_dve, sc_evac, pt_copied):
                pool.sem_inc(sem, 2)
            pool.sem_inc(sc_done, 2)
            pool.sem_inc(pt_done, RING)
            pool.wait_ge(table_loaded, 32)
            for half in range(2):
                nc.gpsimd.indirect_dma_start(lf_pages[:, half], None, io["cache_logf"][0].rearrange("n t h -> n (t h)"),
                                             bass.IndirectOffsetOnAxis(page_of[:, half:half + 1], 0)).then_inc(lf_gathered, 16)
            chain = Chain(pool, masks)
            chain.link(nc.gpsimd.memset(later[:], 1.0))
            chain.link(nc.gpsimd.affine_select(out=later[:], in_=later[:], compare_op=ALU.is_ge, fill=0.0, base=-1, pattern=[[-1, PAGE]], channel_multiplier=1))
            ms, us = mask_s[:].rearrange("p (b t) -> p b t", b=DB), upto_s[:].rearrange("p (b t) -> p b t", b=DB)
            chain.link(nc.gpsimd.memset(ms, 0.0))
            chain.link(nc.gpsimd.affine_select(out=ms, in_=ms, compare_op=ALU.is_ge, fill=-BIG, base=0, pattern=[[-DS, DB], [-1, DS]], channel_multiplier=1))
            chain.link(nc.gpsimd.affine_select(out=ms, in_=ms, compare_op=ALU.is_ge, fill=-BIG, base=DS - 1, pattern=[[DS, DB], [0, DS]], channel_multiplier=-1))
            chain.link(nc.gpsimd.memset(us, -1.0))
            chain.link(nc.gpsimd.affine_select(out=us, in_=us, compare_op=ALU.is_ge, fill=0.0, base=0, pattern=[[DS, DB], [1, DS]], channel_multiplier=-1))
            nc.gpsimd.affine_select(out=us, in_=us, compare_op=ALU.is_ge, fill=0.0, base=0, pattern=[[-DS, DB], [0, DS]], channel_multiplier=1).then_inc(consts, 1)

        @block.scalar
        def _(act):
            for half in range(2):
                with act.Fori(0, ITERS) as j:
                    for k in range(RING):
                        g = j * RING + (half * STEPS + k)
                        act.wait_ge(sc_done, g + 1)
                        for b in range(HB):
                            act.wait_ge(kt_done, g * 8 + (2 * b + 1))
                            nc.scalar.activation(k_t[:, k % 2, b, 0:2].rearrange("p c t -> p (c t)"), kt[:, 2 * b % 4], ACT.Copy).then_inc(kt_evac_act, 1)
                act.wait_ge(shift_ready, half + 1)
                nc.scalar.activation(probs_new[:], s[:, PAST:], ACT.Exp, bias=shift[:], accum_out=sums[:, STEPS:STEPS + 1]).then_inc(exp_new, 1)
                with act.Fori(0, ITERS) as j:
                    for k in range(RING):
                        act.wait_ge(pt_done, j * RING + (half * STEPS + k + 1))
                        nc.scalar.activation(probs[:, k], s[:, bass.ds(j * (RING * STEP) + k * STEP, STEP)], ACT.Exp, bias=shift[:],
                                             accum_out=sums[:, bass.ds(j * RING + k, 1)]).then_inc(exp_done, 1)

        @block.vector
        def _(dve):
            start = Chain(dve, setup)
            ident = keep["ident"]
            start.link(nc.vector.memset(q_blocks[:], 0.0))
            start.link(nc.vector.memset(after[:, 0:1], 0.0))
            for half in range(2):
                tokens = ident[0:NS, half * HB * DS:(half + 1) * HB * DS].rearrange("p (b q) -> p b q", b=HB)
                nc.vector.tensor_copy(sel[:, half].rearrange("p (b h q) -> p b h q", b=HB, h=H),
                                      tokens.unsqueeze(2).to_broadcast([NS, HB, H, DS]))
            nc.vector.tensor_copy(head_sel[:].rearrange("p (b h q) -> p b h q", b=HB, h=H),
                                  ident[0:H, 0:H].unsqueeze(1).unsqueeze(3).to_broadcast([H, HB, H, DS]))
            dve.wait_ge(const_loaded, 64)
            start.link(nc.vector.tensor_copy(lfs_rows[:].rearrange("p (b h q) -> p b h q", b=HB, h=H),
                                             lfs[:].unsqueeze(1).unsqueeze(3).to_broadcast([NS, HB, H, DS])))
            dve.wait_ge(turned, 1)
            qt = qk_ps[:, 0:CH * NS].rearrange("p (c b q) -> p c b q", c=CH, b=DB)
            for c in range(CH):
                for e in range(2):
                    h = 2 * c + e
                    nc.vector.tensor_copy(q_blocks[e * HD:(e + 1) * HD, :, c, h * DS:(h + 1) * DS], qt[e * HD:(e + 1) * HD, c])
            nc.vector.tensor_copy(ks_t[:], qk_ps[:, CH * NS:].rearrange("p (c t) -> p c t", c=CH))
            nc.vector.tensor_copy(head_mask[:], hm_ps)
            start.link(nc.vector.tensor_copy(sel_t[:], sel_ps.rearrange("p (f t) -> p f t", f=2)))

            n_chain = 0
            for half in range(2):
                dve.wait_ge(lf_turned, half + 1)
                lf = kt[:, 0:2].rearrange("p a (h b g) -> p (a h) b g", h=CH, b=HB)
                for b in range(HB):
                    rows = lf_rows[:].rearrange("p g (b h q) -> p b g h q", b=HB, h=H)[:, b]
                    last = nc.vector.tensor_copy(rows, lf[:, :, b].rearrange("p h g -> p g h").unsqueeze(3).to_broadcast([P, NPAGE, H, DS]))
                last.then_inc(lf_ready, 1)
                dve.wait_ge(tot_done, half + 1)
                nc.vector.tensor_tensor_scan(after[:, 1:NPAGE], keep["ones"][:, 0:NPAGE - 1], tot_ps[:, 0:NPAGE - 1], 0.0, ALU.mult, ALU.add).then_inc(after_ready, 1)
                dve.wait_ge(after_ready, half + 1)
                for n in range(NPAGE // 4):
                    dve.wait_ge(bias_done, half * (NPAGE // 4) + n + 1)
                    for i in range(4):
                        page = 4 * n + i
                        last = nc.vector.tensor_scalar(s[:, page * PAGE:(page + 1) * PAGE], kt[:, n % 4, i * PAGE:(i + 1) * PAGE],
                                                       after[:, NPAGE - 1 - page:NPAGE - page], None, ALU.add)
                    last.then_inc(bias_evac, 1)
                dve.wait_ge(new_done, half + 1)
                nc.vector.tensor_copy(s[:, PAST:], new_ps).then_inc(dve_chain, 1)
                dve.wait_ge(bias_evac, (half + 1) * (NPAGE // 4))
                dve.wait_ge(dve_chain, n_chain + 1)

                with dve.Fori(0, ITERS) as j:
                    def evac_kt(k):
                        g = j * RING + (half * STEPS + k)
                        dve.wait_ge(sc_done, g + 1)
                        for b in range(HB):
                            dve.wait_ge(kt_done, g * 8 + (2 * b + 2))
                            nc.vector.tensor_copy(k_t[:, k % 2, b, 2:4].rearrange("p c t -> p (c t)"), kt[:, (2 * b + 1) % 4]).then_inc(kt_evac_dve, 1)
                        nc.vector.nop().then_inc(page_free[k], 1)

                    def evac_scores(k):
                        g = j * RING + (half * STEPS + k)
                        dve.wait_ge(sc_done, g + 3)
                        cols = s[:, bass.ds(j * (RING * STEP) + k * STEP, STEP)]
                        nc.vector.tensor_tensor(cols, sc[:, k % 2, 0:STEP], cols, ALU.add).then_inc(sc_evac, 1)

                    evac_kt(0)
                    for k in range(1, RING):
                        evac_kt(k)
                        evac_scores(k - 1)
                    evac_scores(RING - 1)

                dve.wait_ge(sc_evac, 2 + (half + 1) * STEPS)
                nc.vector.tensor_reduce(shift[:], s[:], AX_X, ALU.max).then_inc(dve_chain, 1)
                dve.wait_ge(dve_chain, n_chain + 2)
                nc.vector.tensor_scalar(shift[:], shift[:], -1.0, None, ALU.mult).then_inc(shift_ready, 1)
                dve.wait_ge(new_turned, half + 1)
                nc.vector.tensor_copy(new_t[:], pn_ps).then_inc(new_copied, 1)
                with dve.Fori(0, ITERS) as j:
                    for k in range(RING):
                        g = j * RING + (half * STEPS + k)
                        dve.wait_ge(pt_done, g + (RING + 1))
                        dve.wait_ge(page_free[(k + 2) % RING], j + ((half * 2 + 1) * ITERS + (2 if k >= 2 else 1)))
                        nc.vector.tensor_copy(probs_t[:, k % 2].rearrange("p g r -> p (g r)"), kt[:, k % 2, 0:PG * R]).then_inc(pt_copied, 1)
                dve.wait_ge(page_free[RING - 1], (half + 1) * 2 * ITERS + 1)
                nc.vector.tensor_reduce(inv[:], sums[:], AX_X, ALU.add).then_inc(dve_chain, 1)
                dve.wait_ge(dve_chain, n_chain + 3)
                nc.vector.reciprocal(inv[:], inv[:]).then_inc(dve_chain, 1)
                dve.wait_ge(dve_chain, n_chain + 4)
                n_chain += 4
                nc.vector.scalar_tensor_tensor(out=picked[:, half].rearrange("p (h d) -> p h d", h=H), in0=o[:].rearrange("p (h d) -> p h d", h=H),
                                               scalar=inv[:], in1=head_mask[:].unsqueeze(2).to_broadcast([P, H, HD]),
                                               op0=ALU.mult, op1=ALU.mult).then_inc(o_picked, 1)
            dve.wait_ge(out_done, 1)
            nc.vector.tensor_copy(out_s[:], o[0:NS]).then_inc(out_copied, 1)

        @block.tensor
        def _(pe):
            ident = keep["ident"]
            pe.wait_ge(const_loaded, 64)
            pe.wait_ge(setup, 3)
            for n, rows in enumerate((qs, ks)):
                for c in range(CH):
                    nc.tensor.transpose(qk_ps[:, (n * CH + c) * NS:(n * CH + c + 1) * NS], rows[:, c * P:(c + 1) * P], ident[0:NS, 0:NS])
            for half in range(2):
                nc.tensor.transpose(sel_ps[:, half * NS:(half + 1) * NS], sel[:, half], ident[0:NS, 0:NS])
            nc.tensor.matmul(hm_ps, head_sel[:], ident[0:H, 0:H], start=True, stop=True).then_inc(turned, 1)
            pe.wait_ge(setup, 4)
            pe.wait_ge(consts, 1)
            for half in range(2):
                pe.wait_ge(lf_gathered, 32)
                by_head = lf_pages[:, half].rearrange("p (t h) -> p t h", h=H)
                for h in range(H):
                    last = nc.tensor.transpose(kt[:, h // 4, h % 4 * P:(h % 4 + 1) * P], by_head[:, :, h], ident[:])
                last.then_inc(lf_turned, 1)
                pe.wait_ge(lf_ready, half + 1)
                for page in range(NPAGE):
                    last = nc.tensor.matmul(tot_ps[:, NPAGE - 1 - page:NPAGE - page], lf_rows[:, page], keep["ones"][:, 0:1], start=True, stop=True)
                last.then_inc(tot_done, 1)
                for n in range(NPAGE // 4):
                    if n >= 4:
                        pe.wait_ge(bias_evac, half * (NPAGE // 4) + n - 3)
                    for i in range(4):
                        last = nc.tensor.matmul(kt[:, n % 4, i * PAGE:(i + 1) * PAGE], lf_rows[:, 4 * n + i], later[:], start=True, stop=True)
                    last.then_inc(bias_done, 1)
                nc.tensor.matmul(new_ps, sel[:, half], mask_s[:], start=True, stop=False)
                nc.tensor.matmul(new_ps, lfs_rows[:], upto_s[:], start=False, stop=False)
                for c in range(CH):
                    for b in range(HB):
                        last = nc.tensor.matmul(new_ps[b * 32:(b + 1) * 32], q_blocks[:, half * HB + b, c], ks_t[:, c], start=False, stop=(c == CH - 1))
                last.then_inc(new_done, 1)
                pe.wait_ge(bias_evac, (half + 1) * (NPAGE // 4))

                with pe.Fori(0, ITERS) as j:
                    def turn(k):
                        g = j * RING + (half * STEPS + k)
                        pe.wait_ge(page_loaded[k], j * (HB * PG * 16) + (half * 2 * ITERS + 1) * (HB * PG * 16))
                        for b in range(HB):
                            for pair, evac in enumerate((kt_evac_act, kt_evac_dve)):
                                pe.wait_ge(evac, g * HB + (b + 1))
                                bank = kt[:, (2 * b + pair) % 4].rearrange("p (c t) -> p c t", c=2)
                                for c in range(2):
                                    for i in range(PG):
                                        chunk = 2 * pair + c
                                        last = nc.tensor.transpose(bank[:, c, i * PAGE:(i + 1) * PAGE], pages[:, k, b, i, chunk * P:(chunk + 1) * P], ident[:])
                                last.then_inc(kt_done, 1)

                    def score(k):
                        g = j * RING + (half * STEPS + k)
                        pe.wait_ge(kt_evac_act, g * HB + (HB + 2))
                        pe.wait_ge(kt_evac_dve, g * HB + (HB + 2))
                        pe.wait_ge(sc_evac, g + 1)
                        for c in range(CH):
                            for b in range(HB):
                                last = nc.tensor.matmul(sc[b * 32:(b + 1) * 32, k % 2, 0:STEP], q_blocks[:, half * HB + b, c], k_t[:, k % 2, b, c],
                                                        start=(c == 0), stop=(c == CH - 1))
                        last.then_inc(sc_done, 1)

                    turn(0)
                    for k in range(1, RING):
                        turn(k)
                        score(k - 1)
                    score(RING - 1)

                pe.wait_ge(exp_new, half + 1)
                nc.tensor.transpose(pn_ps, probs_new[:], ident[:]).then_inc(new_turned, 1)
                pe.wait_ge(new_copied, half + 1)
                if half:
                    pe.wait_ge(o_picked, half)
                nc.tensor.matmul(o[:], new_t[:], vs[:], start=True, stop=False)

                def turn_probs(j, k):
                    g = j * RING + (half * STEPS + k)
                    pe.wait_ge(exp_done, g + 1)
                    pe.wait_ge(pt_copied, g + 1)
                    for i in range(PG):
                        last = nc.tensor.transpose(kt[:, k % 2, i * R:(i + 1) * R], probs[:, k, i * PAGE:(i + 1) * PAGE], ident[:])
                    last.then_inc(pt_done, 1)

                def weigh(j, k, final):
                    g = j * RING + (half * STEPS + k)
                    pe.wait_ge(pt_copied, g + 3)
                    pe.wait_ge(page_loaded[k], j * (HB * PG * 16) + ((half * 2 + 1) * ITERS + 1) * (HB * PG * 16))
                    for i in range(PG):
                        for b in range(HB):
                            last = nc.tensor.matmul(o[b * 32:(b + 1) * 32], probs_t[:, k % 2, i, b * 32:(b + 1) * 32], pages[:, k, b, i],
                                                    start=False, stop=(final and k == RING - 1 and i == PG - 1))
                    last.then_inc(page_free[k], 1)

                def iteration(j, final):
                    turn_probs(j, 0)
                    for k in range(1, RING):
                        turn_probs(j, k)
                        weigh(j, k - 1, final)
                    weigh(j, RING - 1, final)

                with pe.Fori(0, ITERS - 1) as j:
                    iteration(j, False)
                iteration(ITERS - 1, True)
            pe.wait_ge(o_picked, 2)
            nc.tensor.matmul(o[0:NS], sel_t[:, 0], picked[:, 0], start=True, stop=False)
            nc.tensor.matmul(o[0:NS], sel_t[:, 1], picked[:, 1], start=False, stop=True).then_inc(out_done, 1)


def build(nc, io):
    with ExitStack() as ctx:
        m = Alloc(nc, ctx, "keep")
        keep = {
            "ident": m.sb("ident", [P, P]),
            "ones": m.sb("ones", [P, P]),
            "hs_high": m.sb("hs_high", [P, KC, NS], F32R),
            "hs_low": m.sb("hs_low", [P, KC, NS], F32R),
            "f_cols": m.sb("f_cols", [P, NBLK, H]),
            "f_tot": m.sb("f_tot", [H, NT]),
        }
        phase_project(nc, io, keep)
        phase_decode(nc, io, keep)
        phase_attend(nc, io, keep)
        keep["mix_s"] = m.sb("mix_s", [NS, D])
        phase_gates(nc, io, keep)
        phase_merge(nc, io, keep)


_INS = ["x_prompt", "x_sample", "cache_k", "cache_v", "cache_logf", "state_pool", "page_table",
        "norm_w", "w_in", "b_forget", "pool_w", "pool_scale", "w_out", "norm_f"]
_OUTS = [("y_prompt", (1, SEQ, D)), ("y_sample", (DB, DS, D)),
         ("k_prompt", (1, 1, SEQ, H, HD)), ("v_prompt", (1, 1, SEQ, H, HD)),
         ("logf_prompt", (1, 1, SEQ, H)), ("pool_prompt", (1, 1, HIST, W)),
         ("k_sample", (1, DB, DS, H, HD)), ("v_sample", (1, DB, DS, H, HD)),
         ("logf_sample", (1, DB, DS, H)), ("pool_sample", (1, DB, HIST, W))]
_SCRATCH = [("h_t", (NT, P, KC, TILE)), ("q_t", (CH, P, SEQ)), ("k_t", (CH, P, SEQ)), ("f_neg", (H, SEQ)),
            ("q_s", (NS, W)), ("attn_t", (2, CH, P, SEQ)), ("attn_s", (NS, W)), ("pool_t", (CH, P, SEQ)),
            ("gate_t", (CH, P, SEQ)), ("pool_s", (NS, W)), ("gate_s", (NS, W))]


def kernel(**inputs):
    import numpy as _np
    import concourse.bacc as _bacc
    from concourse import mybir as _mybir
    from concourse.bass_utils import run_bass_kernel_spmd as _run

    nc = _bacc.Bacc("TRN2", target_bir_lowering=False, num_devices=1)
    arrays, io = {}, {}
    for name in _INS:
        a = _np.ascontiguousarray(inputs[name])
        arrays[f"in_{name}_dram"] = a
        io[name] = nc.dram_tensor(f"in_{name}_dram", a.shape, _mybir.dt.from_np(a.dtype), kind="ExternalInput").ap()
    for name, shape in _OUTS:
        io[name] = nc.dram_tensor(f"out_{name}_dram", shape, F32, kind="ExternalOutput").ap()
    for name, shape in _SCRATCH:
        io[name] = nc.dram_tensor(f"scratch_{name}", shape, F32, kind="Internal").ap()
    build(nc, io)
    r = _run(nc, [arrays], core_ids=[0])
    return tuple(r.results[0][f"out_{name}_dram"] for name, _ in _OUTS)
```

```python
from contextlib import ExitStack

import concourse.bass as bass
from concourse import mybir

F32 = mybir.dt.float32
F32R = mybir.dt.float32r
BF16 = mybir.dt.bfloat16
I32 = mybir.dt.int32
U32 = mybir.dt.uint32
ALU = mybir.AluOpType
ACT = mybir.ActivationFunctionType
AX_X = mybir.AxisListType.X

P = 128
D = 1024
KC = D // P
W = 512
CH = W // P
H = 8
HD = 64
SEQ = 4096
TILE = 512
NT = SEQ // TILE
TT = TILE // P
NBLK = SEQ // P
DB, DS = 8, 4
NS = DB * DS
NPAGE = 32
PAGE = 128
HIST = 15
WINDOWS = (2, 4, 8, 16)
EPS = 1e-6
ROOT_D = D ** 0.5
QSCALE = HD ** -0.5
BIG = 1e30

U0, GP0, Q0, K0, V0, GA0, FL0 = 0, W, 2 * W, 3 * W, 4 * W, 5 * W, 6 * W


class Alloc:

    def __init__(self, nc, ctx, prefix):
        self.nc, self.ctx, self.prefix, self.sems = nc, ctx, prefix, []
        ctx.callback(self.clear)

    def clear(self):
        if self.sems:
            self.nc.clear_and_free_semaphores(self.sems)
            self.nc.all_engine_barrier()

    def sb(self, name, shape, dt=F32):
        return self.ctx.enter_context(self.nc.sbuf_tensor(f"{self.prefix}_{name}", list(shape), dt))

    def ps(self, name, shape, dt=F32):
        return self.ctx.enter_context(self.nc.psum_tensor(f"{self.prefix}_{name}", list(shape), dt))

    def sem(self, name):
        self.sems.append(self.nc.alloc_semaphore(f"{self.prefix}_{name}"))
        return self.sems[-1]


class Chain:

    def __init__(self, eng, sem, base=0):
        self.eng, self.sem, self.base, self.n = eng, sem, base, 0

    def link(self, ins):
        self.n += 1
        ins.then_inc(self.sem, 1)
        self.eng.wait_ge(self.sem, self.base + self.n)


def three_pass(nc, out, lhs_high, lhs_low, rhs_high, rhs_low, first, last):
    nc.tensor.matmul(out, lhs_high, rhs_high, start=first, stop=False)
    nc.tensor.matmul(out, lhs_high, rhs_low, start=False, stop=False)
    return nc.tensor.matmul(out, lhs_low, rhs_high, start=False, stop=last)


def phase_project(nc, io, keep):
    NQ = 3 * W + H
    FB = 3 * W
    with ExitStack() as ctx:
        m = Alloc(nc, ctx, "pj")
        w_high = m.sb("w_high", [P, KC, NQ], F32R)
        w_low = m.sb("w_low", [P, KC, NQ], F32R)
        norm_col = m.sb("norm_col", [P, KC])
        x = m.sb("x", [P, 2, D])
        xs = m.sb("xs", [NS, D])
        h_t = m.sb("h_t", [P, KC, TILE])
        h_high = m.sb("h_high", [P, KC, TILE], F32R)
        h_low = m.sb("h_low", [P, KC, TILE], F32R)
        stage = m.sb("stage", [P, 2, CH, TILE])
        q_stage, k_stage = stage[:, 0], stage[:, 1]
        w_raw = stage[:].rearrange("p a c t -> p (a c t)")
        k_rows = m.sb("k_rows", [P, 2, W])
        v_rows = m.sb("v_rows", [P, 2, W])
        junk = m.sb("junk", [P, D], BF16)
        squares = m.sb("squares", [P, TT + 1])
        rms = m.sb("rms", [P, TT + 1])
        minus_half = m.sb("minus_half", [P, 1])
        eps_sum = m.sb("eps_sum", [P, 1])
        b_col = m.sb("b_col", [H, 1])
        b_row = m.sb("b_row", [NS, H])
        f_z = m.sb("f_z", [H, TILE])
        f_e = m.sb("f_e", [H, TILE])
        f_log = m.sb("f_log", [H, TILE])
        f_sum = m.sb("f_sum", [H, TILE])
        f_neg = m.sb("f_neg", [H, TILE])
        f_base = m.sb("f_base", [H, 1])
        f_ones = m.sb("f_ones", [H, TILE])
        lf_cols = m.sb("lf_cols", [P, NBLK, H])
        fs = m.sb("fs", [NS, 4, H])
        s_rows = m.sb("s_rows", [NS, 3, W])

        acc = m.ps("acc", [P, 3, TILE])
        tp = m.ps("tp", [P, KC, P])
        f_ps = m.ps("f_ps", [P, TILE])
        kt_ps = m.ps("kt_ps", [P, W])
        ft_ps = m.ps("ft_ps", [P, 2, TT, H])

        const_loaded = m.sem("const_loaded")
        xs_loaded = m.sem("xs_loaded")
        x_loaded = [m.sem(f"x_loaded{i}") for i in range(2)]
        w_loaded = [m.sem(f"w_loaded{i}") for i in range(2)]
        pool_const = m.sem("pool_const")
        pool_chain = m.sem("pool_chain")
        squares_ready = m.sem("squares_ready")
        rms_ready = m.sem("rms_ready")
        h_ready = m.sem("h_ready")
        turned = m.sem("turned")
        h_t_ready = m.sem("h_t_ready")
        h_t_stored = m.sem("h_t_stored")
        h_split = m.sem("h_split")
        w_high_ready = m.sem("w_high_ready")
        w_low_dve = m.sem("w_low_dve")
        acc_done = m.sem("acc_done")
        qk_evac = m.sem("qk_evac")
        v_evac = m.sem("v_evac")
        q_stored = m.sem("q_stored")
        k_stored = m.sem("k_stored")
        f_done = m.sem("f_done")
        f_evac = m.sem("f_evac")
        f_abs = m.sem("f_abs")
        f_soft = m.sem("f_soft")
        f_rows_ready = m.sem("f_rows_ready")
        f_neg_stored = m.sem("f_neg_stored")
        f_turned = m.sem("f_turned")
        f_turned_evac = m.sem("f_turned_evac")
        k_turned = m.sem("k_turned")
        k_rows_evac = m.sem("k_rows_evac")
        k_rows_stored = [m.sem(f"k_rows_stored{i}") for i in range(2)]
        v_rows_stored = [m.sem(f"v_rows_stored{i}") for i in range(2)]
        dve_chain = m.sem("dve_chain")
        act_chain = m.sem("act_chain")
        s_turned = m.sem("s_turned")
        s_split = m.sem("s_split")
        s_done = m.sem("s_done")
        s_evac = m.sem("s_evac")
        s_f = m.sem("s_f")
        s_out = m.sem("s_out")
        ends_stored = m.sem("ends_stored")

        x_rows = io["x_prompt"][0].rearrange("(g p) d -> g p d", p=P)
        w_in = io["w_in"][0]
        k_out = io["k_prompt"].rearrange("l b t h d -> (l b t) (h d)")
        v_out = io["v_prompt"].rearrange("l b t h d -> (l b t) (h d)")
        K_TILES = ((0,), (1,), (), (2, 3))

        block = ctx.enter_context(nc.Block())

        @block.sync
        def _(sp):
            sp.dma_start(xs[:], io["x_sample"].rearrange("b t d -> (b t) d")).then_inc(xs_loaded, 16)
            for t in range(2):
                sp.dma_start(x[:, t], x_rows[t]).then_inc(x_loaded[t], 16)
            sp.dma_start(norm_col[:], io["norm_w"].rearrange("l (c p) -> p (l c)", p=P), allow_slow_non_contiguous=True).then_inc(const_loaded, 16)
            sp.dma_start(b_col[:], io["b_forget"].rearrange("l h -> h l"), allow_slow_non_contiguous=True).then_inc(const_loaded, 16)
            sp.dma_start(b_row[:], io["b_forget"].to_broadcast([NS, H])).then_inc(const_loaded, 16)
            for c in range(KC):
                if c >= 2:
                    sp.wait_ge(w_low_dve, c - 1)
                rows = w_in[c * P:(c + 1) * P]
                slot = w_raw[:, (c % 2) * NQ:(c % 2 + 1) * NQ]
                sp.dma_start(slot[:, 0:FB], rows[:, Q0:Q0 + FB]).then_inc(w_loaded[c % 2], 16)
                sp.dma_start(slot[:, FB:NQ], rows[:, FL0:FL0 + H]).then_inc(w_loaded[c % 2], 16)
                if c in (0, 1):
                    sp.wait_ge(turned, c + 1)
                    sp.dma_start(x[:, c], x_rows[2 + c]).then_inc(x_loaded[c], 16)
            sp.wait_ge(s_evac, 3)
            sp.dma_start(io["q_s"], s_rows[:, 0]).then_inc(s_out, 16)
            sp.dma_start(io["k_sample"].rearrange("l b t h d -> (l b t) (h d)"), s_rows[:, 1]).then_inc(s_out, 16)
            sp.dma_start(io["v_sample"].rearrange("l b t h d -> (l b t) (h d)"), s_rows[:, 2]).then_inc(s_out, 16)
            sp.wait_ge(s_f, 4)
            sp.dma_start(io["logf_sample"].rearrange("l b t h -> (l b t) h"), fs[:, 3]).then_inc(s_out, 16)

            def super_tile(s, more):
                if more:
                    for t in range(2):
                        sp.wait_ge(turned, s * TT + (TT + t - 1))
                        sp.dma_start(x[:, t], x_rows[bass.ds(s * TT + (TT + t), 1)].rearrange("a p d -> p (a d)")).then_inc(x_loaded[t], 16)
                sp.wait_ge(h_t_ready, s * TT + TT)
                sp.dma_start(io["h_t"][bass.ds(s, 1)].rearrange("a p k t -> p (a k) t"), h_t[:]).then_inc(h_t_stored, 16)
                if more:
                    for t in range(2, 4):
                        sp.wait_ge(turned, s * TT + (TT + t - 1))
                        sp.dma_start(x[:, t % 2], x_rows[bass.ds(s * TT + (TT + t), 1)].rearrange("a p d -> p (a d)")).then_inc(x_loaded[t % 2], 16)
                sp.wait_ge(qk_evac, s * 2 * CH + CH)
                sp.dma_start(io["q_t"].rearrange("c p t -> p c t")[:, :, bass.ds(s * TILE, TILE)], q_stage).then_inc(q_stored, 16)
                sp.wait_ge(qk_evac, s * 2 * CH + 2 * CH)
                sp.dma_start(io["k_t"].rearrange("c p t -> p c t")[:, :, bass.ds(s * TILE, TILE)], k_stage).then_inc(k_stored, 16)
                sp.wait_ge(f_rows_ready, s + 1)
                sp.dma_start(io["f_neg"][:, bass.ds(s * TILE, TILE)], f_neg[:]).then_inc(f_neg_stored, 16)
                for t in range(TT):
                    sp.wait_ge(v_evac, s * TT + (TT + t + 1))
                    sp.dma_start(v_out[bass.ds(s * TILE + t * P, P)], v_rows[:, t % 2]).then_inc(v_rows_stored[t % 2], 16)
                    for tk in K_TILES[t]:
                        sp.wait_ge(k_rows_evac, s * TT + (tk + 2))
                        sp.dma_start(k_out[bass.ds(s * TILE + tk * P, P)], k_rows[:, tk % 2]).then_inc(k_rows_stored[tk % 2], 16)

            with sp.Fori(0, NT - 1) as s:
                super_tile(s, True)
            super_tile(NT - 1, False)
            sp.wait_ge(f_turned_evac, NT + 1)
            sp.dma_start(io["logf_prompt"].rearrange("l b (g p) h -> p (l b g) h", p=P), lf_cols[:]).then_inc(ends_stored, 16)
            sp.wait_ge(ends_stored, 16)
            sp.wait_ge(s_out, 64)
            sp.wait_ge(h_t_stored, 16 * NT)
            sp.wait_ge(q_stored, 16 * (NT + 1))
            sp.wait_ge(k_stored, 16 * (NT + 1))
            sp.wait_ge(f_neg_stored, 16 * (NT + 1))
            for i in range(2):
                sp.wait_ge(k_rows_stored[i], 16 * (2 * NT + 1))
                sp.wait_ge(v_rows_stored[i], 16 * (2 * NT + 1))

        @block.gpsimd
        def _(pool):
            pool.sem_inc(q_stored, 16)
            pool.sem_inc(k_stored, 16)
            pool.sem_inc(f_neg_stored, 16)
            pool.sem_inc(k_turned, TT)
            pool.sem_inc(k_rows_evac, 1)
            pool.sem_inc(f_evac, 1)
            pool.sem_inc(f_turned_evac, 1)
            pool.sem_inc(f_turned, 1)
            pool.sem_inc(v_evac, TT)
            for i in range(2):
                pool.sem_inc(k_rows_stored[i], 16)
                pool.sem_inc(v_rows_stored[i], 16)
            chain = Chain(pool, pool_chain)
            chain.link(nc.gpsimd.memset(keep["ident"][:], 0.0))
            chain.link(nc.gpsimd.memset(minus_half[:], -0.5))
            chain.link(nc.gpsimd.memset(eps_sum[:], D * EPS))
            chain.link(nc.gpsimd.memset(keep["ones"][:], 1.0))
            nc.gpsimd.affine_select(out=keep["ident"][:], in_=keep["ident"][:], compare_op=ALU.not_equal,
                                    fill=1.0, base=0, pattern=[[-1, P]], channel_multiplier=1).then_inc(pool_const, 1)

            def rms_of(n, count, chain):
                pool.wait_ge(squares_ready, count)
                rows = NS if n == TT else P
                out = rms[0:rows, n:n + 1]
                chain.link(nc.gpsimd.tensor_tensor(out, squares[0:rows, n:n + 1], eps_sum[0:rows], ALU.add))
                nc.gpsimd.tensor_tensor(out, out, minus_half[0:rows], ALU.pow).then_inc(rms_ready, 1)

            for n in range(TT + 1):
                rms_of((n + TT) % (TT + 1), n + 1, chain)
                if n == 2:
                    before = chain.n
            first = chain.n
            with pool.Fori(0, NT - 1) as s:
                chain = Chain(pool, pool_chain, s * TT + first)
                for t in range(TT):
                    rms_of(t, s * TT + (TT + t + 2), chain)

        @block.scalar
        def _(act):
            def square(t, slot, count, before):
                act.wait_ge(squares_ready, before)
                act.wait_ge(x_loaded[slot], count)
                nc.scalar.activation(junk[:], x[:, slot], ACT.Square, accum_out=squares[:, t:t + 1]).then_inc(squares_ready, 1)

            def copy_turned(g, t):
                act.wait_ge(turned, g + 1)
                nc.scalar.activation(h_t[:, :, t * P:(t + 1) * P], tp[:], ACT.Copy).then_inc(h_t_ready, 1)

            act.wait_ge(xs_loaded, 16)
            nc.scalar.activation(junk[0:NS], xs[:], ACT.Square, accum_out=squares[0:NS, TT:TT + 1]).then_inc(squares_ready, 1)
            square(0, 0, 16, 1)
            square(1, 1, 16, 2)
            act.wait_ge(const_loaded, 48)

            def round_weights(c):
                act.wait_ge(w_loaded[c % 2], 32 * (c // 2 + 1))
                nc.scalar.activation(w_high[:, c], w_raw[:, (c % 2) * NQ:(c % 2 + 1) * NQ], ACT.Copy, scale=norm_col[:, c:c + 1]).then_inc(w_high_ready, 1)

            round_weights(0)
            copy_turned(0, 0)
            square(2, 0, 32, 3)
            round_weights(1)
            copy_turned(1, 1)
            square(3, 1, 32, 4)
            round_weights(2)
            copy_turned(2, 2)
            round_weights(3)
            copy_turned(3, 3)
            for c in range(4, KC):
                round_weights(c)
            act.wait_ge(s_done, 1)
            nc.scalar.activation(s_rows[:, 0], acc[0:NS, 0], ACT.Copy, scale=QSCALE).then_inc(s_evac, 1)
            act.wait_ge(s_done, 2)
            nc.scalar.activation(s_rows[:, 1], acc[0:NS, 1], ACT.Copy).then_inc(s_evac, 1)
            act.wait_ge(s_f, 2)
            nc.scalar.activation(fs[:, 1], fs[:, 1], ACT.Exp, scale=-1.0).then_inc(act_chain, 1)
            act.wait_ge(act_chain, 1)
            nc.scalar.activation(fs[:, 2], fs[:, 1], ACT.Ln, bias=1.0).then_inc(s_f, 1)
            act.wait_ge(const_loaded, 48)

            def evac(s, u, dst, scale):
                act.wait_ge(acc_done, s * 12 + (u + 1))
                nc.scalar.activation(dst, acc[:, u % 3], ACT.Copy, scale=scale).then_inc(qk_evac, 1)

            def super_tile(s, more):
                for c in range(CH):
                    if more and c == 0:
                        for t in range(2):
                            square(t, t, s * 32 + 48, s * TT + (TT + 1 + t))
                    if c == 0:
                        act.wait_ge(q_stored, s * 16 + 16)
                    evac(s, c, q_stage[:, c], QSCALE)
                    if more and c >= 1:
                        if c == 1:
                            act.wait_ge(h_t_stored, s * 16 + 16)
                            act.wait_ge(h_split, s * TT + TT)
                        copy_turned(s * TT + (TT + c - 1), c - 1)
                        if c < 3:
                            square(c + 1, (c + 1) % 2, s * 32 + 64, s * TT + (TT + 2 + c))
                for c in range(CH):
                    if c == 0:
                        act.wait_ge(k_stored, s * 16 + 16)
                        act.wait_ge(k_turned, s * TT + TT)
                    evac(s, CH + c, k_stage[:, c], 1.0)
                    if more and c == 0:
                        copy_turned(s * TT + (TT + 3), 3)
                act.wait_ge(f_done, s + 1)
                nc.scalar.activation(f_z[:], f_ps[0:H], ACT.Identity, bias=b_col[:]).then_inc(f_evac, 1)
                act.wait_ge(f_abs, s + 1)
                nc.scalar.activation(f_e[:], f_e[:], ACT.Exp, scale=-1.0).then_inc(act_chain, 1)
                act.wait_ge(act_chain, s + 2)
                nc.scalar.activation(f_e[:], f_e[:], ACT.Ln, bias=1.0).then_inc(f_soft, 1)

            with act.Fori(0, NT - 1) as s:
                super_tile(s, True)
            super_tile(NT - 1, False)

        @block.vector
        def _(dve):
            chain = Chain(dve, dve_chain)
            nc.vector.memset(f_ones[:], 1.0)
            nc.vector.memset(keep["f_tot"][:], 0.0)
            chain.link(nc.vector.memset(f_base[:], 0.0))

            def scale_x(slot, t, count):
                dve.wait_ge(rms_ready, count)
                nc.vector.tensor_scalar(x[:, slot], x[:, slot], rms[:, t:t + 1], ROOT_D, ALU.mult, ALU.mult).then_inc(h_ready, 1)

            dve.wait_ge(rms_ready, 1)
            nc.vector.tensor_scalar(xs[:], xs[:], rms[0:NS, TT:TT + 1], ROOT_D, ALU.mult, ALU.mult).then_inc(h_ready, 1)
            scale_x(0, 0, 2)
            scale_x(1, 1, 3)
            dve.wait_ge(const_loaded, 48)

            def prepare_weights(c):
                dve.wait_ge(w_high_ready, c + 1)
                nc.vector.scalar_tensor_tensor(out=w_low[:, c], in0=w_raw[:, (c % 2) * NQ:(c % 2 + 1) * NQ], scalar=norm_col[:, c:c + 1],
                                               in1=w_high[:, c].bitcast(F32), op0=ALU.mult, op1=ALU.subtract).then_inc(w_low_dve, 1)

            dve.wait_ge(s_turned, 1)
            hs = tp[:, :, 0:NS]
            chain.link(nc.vector.tensor_copy(keep["hs_high"][:], hs))
            nc.vector.tensor_tensor(keep["hs_low"][:], hs, keep["hs_high"][:].bitcast(F32), ALU.subtract).then_inc(s_split, 1)
            prepare_weights(0)
            scale_x(0, 2, 4)
            prepare_weights(1)
            scale_x(1, 3, 5)
            for c in range(2, KC):
                prepare_weights(c)

            def split_h(s, t, chain):
                cols = slice(t * P, (t + 1) * P)
                dve.wait_ge(h_t_ready, s * TT + (t + 1))
                chain.link(nc.vector.tensor_copy(h_high[:, :, cols], h_t[:, :, cols]))
                nc.vector.tensor_tensor(h_low[:, :, cols], h_t[:, :, cols], h_high[:, :, cols].bitcast(F32), ALU.subtract).then_inc(h_split, 1)

            for t in range(TT):
                split_h(0, t, chain)
            dve.wait_ge(s_done, 3)
            nc.vector.tensor_copy(s_rows[:, 2], acc[0:NS, 2]).then_inc(s_evac, 1)
            dve.wait_ge(s_done, 4)
            chain.link(nc.vector.tensor_tensor(fs[:, 0], f_ps[0:NS, 0:H], b_row[:], ALU.add))
            nc.vector.nop().then_inc(s_f, 1)
            nc.vector.scalar_tensor_tensor(out=fs[:, 1], in0=fs[:, 0], scalar=-1.0, in1=fs[:, 0], op0=ALU.mult, op1=ALU.max).then_inc(s_f, 1)
            dve.wait_ge(s_f, 3)
            nc.vector.scalar_tensor_tensor(out=fs[:, 3], in0=fs[:, 0], scalar=0.0, in1=fs[:, 2], op0=ALU.min, op1=ALU.subtract).then_inc(s_f, 1)
            first = chain.n
            PER = 3 + TT

            def super_tile(s, more):
                chain = Chain(dve, dve_chain, s * PER + first)
                if more:
                    for t in range(TT):
                        dve.wait_ge(turned, s * TT + (TT + t - 1)) if t >= 2 else None
                        scale_x(t % 2, t, s * TT + (TT + t + 2))
                dve.wait_ge(f_evac, s + 2)
                nc.vector.scalar_tensor_tensor(out=f_e[:], in0=f_z[:], scalar=-1.0, in1=f_z[:], op0=ALU.mult, op1=ALU.max).then_inc(f_abs, 1)
                dve.wait_ge(f_soft, s + 1)
                dve.wait_ge(f_turned, s + 1)
                dve.wait_ge(f_neg_stored, s * 16 + 16)
                chain.link(nc.vector.scalar_tensor_tensor(out=f_log[:], in0=f_z[:], scalar=0.0, in1=f_e[:], op0=ALU.min, op1=ALU.subtract))
                chain.link(nc.vector.tensor_tensor_scan(f_sum[:], f_ones[:], f_log[:], 0.0, ALU.mult, ALU.add))
                nc.vector.tensor_copy(keep["f_tot"][:, bass.ds(s, 1)], f_sum[:, TILE - 1:TILE])
                chain.link(nc.vector.tensor_scalar(f_neg[:], f_sum[:], -1.0, f_base[:], ALU.mult, ALU.add))
                nc.vector.tensor_copy(f_base[:], f_neg[:, TILE - 1:TILE]).then_inc(f_rows_ready, 1)
                for t in range(TT):
                    if more:
                        dve.wait_ge(acc_done, s * 12 + (8 + t + 1))
                        split_h(s + 1, t, chain)
                    else:
                        chain.n += 1
                    dve.wait_ge(acc_done, s * 12 + (8 + t + 1))
                    dve.wait_ge(v_rows_stored[t % 2], s * 32 + (16 * (t // 2) + 16))
                    nc.vector.tensor_copy(v_rows[:, t % 2], acc[:, (8 + t) % 3]).then_inc(v_evac, 1)
                    for tk in K_TILES[t]:
                        if tk == 3:
                            dve.wait_ge(f_turned, s + 2)
                            nc.vector.tensor_copy(lf_cols[:, bass.ds(s * TT, TT)], ft_ps[:, 0])
                            nc.vector.tensor_copy(keep["f_cols"][:, bass.ds(s * TT, TT)], ft_ps[:, 1]).then_inc(f_turned_evac, 1)
                        dve.wait_ge(k_turned, s * TT + (TT + tk + 1))
                        dve.wait_ge(k_rows_stored[tk % 2], s * 32 + (16 * (tk // 2) + 16))
                        nc.vector.tensor_copy(k_rows[:, tk % 2], kt_ps[:]).then_inc(k_rows_evac, 1)
                assert chain.n == PER

            with dve.Fori(0, NT - 1) as s:
                super_tile(s, True)
            super_tile(NT - 1, False)

        @block.tensor
        def _(pe):
            def turn(src, count, g, done):
                rows = src.shape[0]
                pe.wait_ge(h_ready, count)
                if g is not None:
                    pe.wait_ge(h_t_ready, g)
                for c in range(KC):
                    last = nc.tensor.transpose(tp[:, c, 0:rows], src[:, c * P:(c + 1) * P], keep["ident"][0:rows, 0:rows])
                last.then_inc(done, 1)

            pe.wait_ge(pool_const, 1)
            turn(xs[:], 1, None, s_turned)
            pe.wait_ge(s_split, 1)
            turn(x[:, 0], 2, None, turned)
            turn(x[:, 1], 3, 1, turned)
            turn(x[:, 0], 4, 2, turned)
            turn(x[:, 1], 5, 3, turned)
            for c in range(KC):
                pe.wait_ge(w_low_dve, c + 1)
                for n in range(4):
                    cols = slice(n * W, min((n + 1) * W, NQ))
                    out = acc[0:NS, n] if n < 3 else f_ps[0:NS, 0:H]
                    last = three_pass(nc, out, keep["hs_high"][:, c], keep["hs_low"][:, c],
                                      w_high[:, c, cols], w_low[:, c, cols], c == 0, c == KC - 1)
                    if c == KC - 1:
                        last.then_inc(s_done, 1)
            pe.wait_ge(s_evac, 3)
            pe.wait_ge(s_f, 1)

            def super_tile(s, more):
                pe.wait_ge(h_split, s * TT + TT)
                for u in range(2 * CH):
                    if u < 3:
                        pe.wait_ge(v_evac, s * TT + (u + 2))
                    else:
                        pe.wait_ge(qk_evac, s * 2 * CH + (u - 2))
                    cols = slice(u * P, (u + 1) * P)
                    for c in range(KC):
                        last = three_pass(nc, acc[:, u % 3], w_high[:, c, cols], w_low[:, c, cols],
                                          h_high[:, c], h_low[:, c], c == 0, c == KC - 1)
                    last.then_inc(acc_done, 1)
                    if more and 1 <= u <= 4:
                        t = u - 1
                        turn(x[:, t % 2], s * TT + (TT + t + 2), s * TT + (TT + t), turned)
                pe.wait_ge(f_evac, s + 1)
                for c in range(KC):
                    last = three_pass(nc, f_ps[0:H], w_high[:, c, FB:NQ], w_low[:, c, FB:NQ],
                                      h_high[:, c], h_low[:, c], c == 0, c == KC - 1)
                last.then_inc(f_done, 1)
                pe.wait_ge(qk_evac, s * 2 * CH + 2 * CH)
                for t in range(TT):
                    u = 2 * CH + t
                    if t == 3:
                        pe.wait_ge(v_evac, s * TT + (TT + 1))
                    for c in range(KC):
                        last = three_pass(nc, acc[:, u % 3], h_high[:, c, t * P:(t + 1) * P], h_low[:, c, t * P:(t + 1) * P],
                                          w_high[:, c, 2 * W:3 * W], w_low[:, c, 2 * W:3 * W], c == 0, c == KC - 1)
                    last.then_inc(acc_done, 1)
                    for tk in K_TILES[t]:
                        if tk == 3:
                            pe.wait_ge(pool_const, 1)
                            pe.wait_ge(f_rows_ready, s + 1)
                            pe.wait_ge(f_turned_evac, s + 1)
                            for j, rows in enumerate((f_log, f_sum)):
                                for n in range(TT):
                                    last = nc.tensor.transpose(ft_ps[:, j, n], rows[:, n * P:(n + 1) * P], keep["ident"][0:H, 0:H])
                            last.then_inc(f_turned, 1)
                        pe.wait_ge(k_rows_evac, s * TT + (tk + 1))
                        for c in range(CH):
                            last = nc.tensor.transpose(kt_ps[:, c * P:(c + 1) * P], k_stage[:, c, tk * P:(tk + 1) * P], keep["ident"][:])
                        last.then_inc(k_turned, 1)

            with pe.Fori(0, NT - 1) as s:
                super_tile(s, True)
            super_tile(NT - 1, False)


class Count:

    def __init__(self, sem, per, credit=0):
        self.sem, self.per, self.credit = sem, per, credit

    def at(self, i, k):
        assert k + self.credit >= 1, (k, self.credit)
        return i * self.per + (k + self.credit)


def wait_apart(eng, sem, value, ticks):
    eng.wait_ge(sem, value)
    eng.sem_inc(ticks, 1)


def attend_steps():
    return [(hp, j, e) for hp in range(2) for j in range(NT) for e in range(2 * (j + 1))]


def phase_attend(nc, io, keep):
    STEPS = attend_steps()
    NSTEP = len(STEPS)
    NBLOCK = 2 * NT
    NUNIT = sum(TT * (j + 1) for _ in range(2) for j in range(NT))
    KCHUNK = 1024
    NKC = SEQ // KCHUNK
    RING = 4
    AHEAD = 3
    uses = [len(range(k, NBLOCK, AHEAD)) for k in range(AHEAD)]
    step_of = {key: n for n, key in enumerate(STEPS)}
    last_step = [step_of[(b // NT, b % NT, 2 * (b % NT) + 1)] for b in range(NBLOCK)]
    unit_base = [sum(TT * (c % NT + 1) for c in range(b)) for b in range(NBLOCK + 1)]

    def lo(n, half):
        _, j, e = STEPS[n]
        own = 2 * e + half - TT * j
        return max(own, 0) * P

    def diagonal(n):
        _, j, e = STEPS[n]
        return e >= 2 * j

    masks = [0]
    for n in range(NSTEP):
        masks.append(masks[-1] + diagonal(n))

    units_by = [0] * NSTEP
    for n in reversed(range(NSTEP)):
        hp, j, e = STEPS[n]
        b = hp * NT + j
        needed = unit_base[min(b + (2 if e >= 2 * j else 1), NBLOCK)]
        units_by[n] = max(needed, units_by[n + 1] - 3 if n + 1 < NSTEP else 0)
    out = TT
    for n, (hp, j, e) in enumerate(STEPS):
        b = hp * NT + j
        ahead = unit_base[min(b + (3 if e else 2), NBLOCK)]
        out = units_by[n] = min(max(out + 2, units_by[n]), ahead)
    assert all(units_by[last_step[b] - 1] >= unit_base[b + 2] for b in range(NBLOCK - 1))
    block_of = [b for b in range(NBLOCK) for _ in range(unit_base[b + 1] - unit_base[b])]
    spread_at = [TT] + [units_by[last_step[b] - 1] for b in range(NBLOCK - 1)]

    def units_in(n):
        return [(block_of[k], k - unit_base[block_of[k]]) for k in range(units_by[n - 1] if n else TT, units_by[n])]

    with ExitStack() as ctx:
        m = Alloc(nc, ctx, "at")
        k_raw = m.sb("k_raw", [P, 2, KCHUNK])
        k_all = [m.sb(f"k_all{i}", [P, SEQ], F32R) for i in range(2)]
        k_one = [m.sb(f"k_one{i}", [P, SEQ], F32R) for i in range(2)]
        v = m.sb("v", [P, 2, NBLK, HD])
        f_neg = m.sb("f_neg", [P, 2, SEQ])
        f_diag = m.sb("f_diag", [P, AHEAD, TT, P])
        tri = m.sb("tri", [P, P])
        tri_t = m.sb("tri_t", [P, P])
        q_raw = m.sb("q_raw", [P, AHEAD, TILE])
        q_all = m.sb("q_all", [P, AHEAD, TILE], F32R)
        q_one = m.sb("q_one", [P, 2, TILE], F32R)
        max_parts = m.sb("max_parts", [P, 2, TT, NT + 1])
        max_all = m.sb("max_all", [P, TT])
        shift = m.sb("shift", [P, TT, P], F32R)
        ones_r = m.sb("ones_r", [P, P], F32R)
        probs = m.sb("probs", [P, RING, 2, TILE])
        den_out = m.sb("den_out", [P, 2, TILE])
        o_out = m.sb("o_out", [P, 2, TILE])
        base = m.sb("base", [P, H, NT])
        bias = m.sb("bias", [P, H, NT, NBLK])
        gap = m.sb("gap", [P, H, NT, NT])
        f_pre = m.sb("f_pre", [H, NT])
        f_spread = m.sb("f_spread", [H, H, NT])
        f_one = m.sb("f_one", [H, NT])
        bias_h = m.sb("bias_h", [P, 2, NT, NBLK])
        base_h = m.sb("base_h", [P, 2, NT])

        st = m.ps("st", [P, 2, 2, TILE])
        o_ps = m.ps("o_ps", [P, TILE])
        mx = m.ps("mx", [P, 2, TILE])
        den_ps = m.ps("den", [P, TILE])

        setup = m.sem("setup")
        ticks = m.sem("ticks")
        setup_pe = m.sem("setup_pe")
        tri_ready = m.sem("tri_ready")
        k_loaded = [m.sem(f"k_loaded{i}") for i in range(2)]
        v_loaded = [m.sem(f"v_loaded{i}") for i in range(2)]
        f_loaded = [m.sem(f"f_loaded{i}") for i in range(2)]
        q_loaded = [m.sem(f"q_loaded{i}") for i in range(AHEAD)]
        k_high = Count(m.sem("k_high"), 2 * NKC)
        k_low = Count(m.sem("k_low"), 2 * NKC, 2)
        q_high = Count(m.sem("q_high"), NBLOCK)
        q_low = Count(m.sem("q_low"), NBLOCK, 2)
        q_shift = Count(m.sem("q_shift"), NBLOCK)
        shift_ready = Count(m.sem("shift_ready"), NBLOCK)
        shift_turned = Count(m.sem("shift_turned"), NBLOCK, 1)
        st_ready = Count(m.sem("st_ready"), NSTEP)
        exp_done = Count(m.sem("exp_done"), NSTEP, 2)
        masked = Count(m.sem("masked"), masks[-1])
        pv_done = Count(m.sem("pv_done"), NSTEP, RING)
        den_done = Count(m.sem("den_done"), NSTEP // 2, RING // 2)
        den_copied = Count(m.sem("den_copied"), NBLOCK, 1)
        mx_ready = Count(m.sem("mx_ready"), NUNIT)
        mx_done = Count(m.sem("mx_done"), NUNIT, 2)
        f_diag_ready = Count(m.sem("f_diag_ready"), NBLOCK)
        head_ready = Count(m.sem("head_ready"), 2)
        max_chain = Count(m.sem("max_chain"), 2 * NBLOCK)
        o_copied = Count(m.sem("o_copied"), NBLOCK, 1)
        o_stored = [m.sem(f"o_stored{i}") for i in range(2)]
        den_stored = [m.sem(f"den_stored{i}") for i in range(2)]

        v_rows = io["v_prompt"].rearrange("l b (g p) h d -> p (l b g) h d", p=P)

        def tile_and_chunk(b, u):
            j = b % NT
            return u // (j + 1), u % (j + 1)

        block = ctx.enter_context(nc.Block())

        @block.sync
        def _(sp):
            def load_k(i, n):
                hp, c = divmod(n, NKC)
                wait_apart(sp, k_low.sem, k_low.at(i, n - 1), ticks)
                src = io["k_t"][bass.ds(i, 1), hp * HD:(hp + 1) * HD, c * KCHUNK:(c + 1) * KCHUNK].rearrange("a p t -> (a p) t")
                for half in range(2):
                    sp.dma_start(k_raw[half * HD:(half + 1) * HD, n % 2], src).then_inc(k_loaded[n % 2], 16)

            def load_q(i, b):
                hp, j = divmod(b, NT)
                wait_apart(sp, q_low.sem, q_low.at(i, b - AHEAD + 1 if b >= AHEAD else 0), ticks)
                src = io["q_t"][bass.ds(i, 1), hp * HD:(hp + 1) * HD, j * TILE:(j + 1) * TILE].rearrange("a p t -> (a p) t")
                for half in range(2):
                    sp.dma_start(q_raw[half * HD:(half + 1) * HD, b % AHEAD], src).then_inc(q_loaded[b % AHEAD], 16)

            def load_head(i, hp):
                rows = io["f_neg"][bass.ds(i * 2 + hp, 1)]
                sp.dma_start(f_neg[:, hp], rows.to_broadcast([P, SEQ])).then_inc(f_loaded[hp], 16)
                sp.dma_start(v[:, hp], v_rows[:, :, bass.ds(i * 2 + hp, 1)].rearrange("p g a d -> p g (a d)")).then_inc(v_loaded[hp], 16)

            def store_o(i, b):
                hp, j = divmod(b, NT)
                wait_apart(sp, o_copied.sem, o_copied.at(i, b + 1), ticks)
                for half in range(2):
                    dst = io["attn_t"][half, bass.ds(i, 1), hp * HD:(hp + 1) * HD, j * TILE:(j + 1) * TILE].rearrange("a p t -> (a p) t")
                    sp.dma_start(dst, o_out[half * HD:(half + 1) * HD, b % 2]).then_inc(o_stored[b % 2], 16)
                wait_apart(sp, den_copied.sem, den_copied.at(i, b + 1), ticks)
                for part in range(4):
                    sp.dma_start(io["den"][part, bass.ds(i * 2 + hp, 1), j * TILE:(j + 1) * TILE], den_out[part * 32:part * 32 + 1, b % 2]).then_inc(den_stored[b % 2], 16)

            load_k(0, 0)
            load_q(0, 0)
            load_head(0, 0)
            load_q(0, 1)
            load_k(0, 1)
            load_q(0, 2)

            def pair(i, more):
                for b in range(NBLOCK):
                    if b + 3 < NBLOCK:
                        load_q(i, b + 3)
                    if b % 2 == 0 and b // 2 + 2 < 2 * NKC:
                        load_k(i, b // 2 + 2)
                    if b == NT // 2:
                        load_head(i, 1)
                    if more:
                        if b == NT + 2:
                            sp.wait_ge(mx_done.sem, mx_done.at(i, unit_base[NT]))
                            wait_apart(sp, pv_done.sem, pv_done.at(i, last_step[NT - 1] + 1), ticks)
                            load_head(i + 1, 0)
                        if b == NBLOCK - 2:
                            load_k(i + 1, 0)
                            load_k(i + 1, 1)
                        if b == NBLOCK - 1:
                            for n in range(AHEAD):
                                load_q(i + 1, n)
                    if b >= 1:
                        store_o(i, b - 1)
                store_o(i, NBLOCK - 1)

            with sp.Fori(0, CH - 1) as i:
                pair(i, True)
            pair(CH - 1, False)
            for half in range(2):
                sp.wait_ge(o_stored[half], CH * NBLOCK // 2 * 32 + 32)
                sp.wait_ge(den_stored[half], CH * NBLOCK // 2 * 64 + 64)

        @block.gpsimd
        def _(pool):
            for c in (k_low, q_low, shift_turned, exp_done, pv_done, den_done, den_copied, mx_done, o_copied):
                pool.sem_inc(c.sem, c.credit)
            for c in o_stored:
                pool.sem_inc(c, 32)
            for c in den_stored:
                pool.sem_inc(c, 64)
            nc.gpsimd.memset(tri[:], 0.0).then_inc(tri_ready, 1)
            pool.wait_ge(tri_ready, 1)
            nc.gpsimd.memset(tri_t[:], 0.0).then_inc(tri_ready, 1)
            pool.wait_ge(tri_ready, 2)
            nc.gpsimd.affine_select(out=tri_t[:], in_=tri_t[:], compare_op=ALU.is_ge, fill=-BIG, base=0,
                                    pattern=[[1, P]], channel_multiplier=-1).then_inc(tri_ready, 1)
            nc.gpsimd.affine_select(out=tri[:], in_=tri[:], compare_op=ALU.is_ge, fill=-BIG, base=0,
                                    pattern=[[-1, P]], channel_multiplier=1).then_inc(tri_ready, 1)
            pool.wait_ge(tri_ready, 4)

            def diagonal_f(i, b):
                hp, j = divmod(b, NT)
                pool.wait_ge(f_loaded[hp], i * 16 + 16)
                if b == 0:
                    pool.wait_ge(mx_done.sem, mx_done.at(i, 0))
                if b >= AHEAD:
                    pool.wait_ge(mx_done.sem, mx_done.at(i, unit_base[b - AHEAD + 1]))
                row = f_neg[:, hp, j * TILE:(j + 1) * TILE].rearrange("p (t k) -> p t k", t=TT)
                nc.gpsimd.tensor_tensor(f_diag[:, b % AHEAD], row, tri[:].unsqueeze(1).to_broadcast([P, TT, P]), ALU.add).then_inc(f_diag_ready.sem, 1)

            with pool.Fori(0, CH) as i:
                for b in range(NBLOCK):
                    diagonal_f(i, b)

        @block.scalar
        def _(act):
            def round_k(i, n):
                hp, c = divmod(n, NKC)
                act.wait_ge(k_loaded[n % 2], i * (NKC * 32) + (n // 2 + 1) * 32)
                cols = slice(c * KCHUNK, (c + 1) * KCHUNK)
                nc.scalar.activation(k_all[hp][:, cols], k_raw[:, n % 2], ACT.Copy)
                nc.scalar.activation(k_one[hp][0:HD, cols], k_raw[0:HD, n % 2], ACT.Copy).then_inc(k_high.sem, 1)

            def round_q(i, b):
                act.wait_ge(q_loaded[b % AHEAD], i * (uses[b % AHEAD] * 32) + (b // AHEAD + 1) * 32)
                nc.scalar.activation(q_all[:, b % AHEAD], q_raw[:, b % AHEAD], ACT.Copy).then_inc(q_high.sem, 1)

            def shift_rows(i, b):
                act.wait_ge(shift_turned.sem, shift_turned.at(i, b + 1))
                nc.scalar.activation(q_one[HD:P, b % 2], mx[HD:P, spread_at[b] % 2], ACT.Copy).then_inc(q_shift.sem, 1)

            def copy_o(i, b):
                act.wait_ge(pv_done.sem, pv_done.at(i, last_step[b] + 1))
                act.wait_ge(o_stored[b % 2], i * (NBLOCK // 2 * 32) + (b // 2 + 1) * 32)
                nc.scalar.activation(o_out[:, b % 2], o_ps[:], ACT.Copy).then_inc(o_copied.sem, 1)

            def exps(i, n):
                hp, j, e = STEPS[n]
                if diagonal(n):
                    act.wait_ge(masked.sem, masked.at(i, masks[n + 1]))
                else:
                    act.wait_ge(st_ready.sem, st_ready.at(i, n + 1))
                act.wait_ge(den_done.sem, den_done.at(i, n // 2 - 1))
                for half in range(2):
                    blk = 2 * e + half
                    first = lo(n, half)
                    last = nc.scalar.activation(probs[:, n % RING, half, first:TILE], st[:, n % 2, half, first:TILE],
                                                ACT.Exp, bias=bias_h[:, hp, j, blk:blk + 1])
                last.then_inc(exp_done.sem, 1)

            with act.Fori(0, CH) as i:
                round_k(i, 0)
                round_q(i, 0)
                round_q(i, 1)
                shift_rows(i, 0)
                round_k(i, 1)
                for n in range(NSTEP):
                    hp, j, e = STEPS[n]
                    b = hp * NT + j
                    if e == 0:
                        if b + 2 < NBLOCK:
                            round_q(i, b + 2)
                        if b % 2 and b // 2 + 2 < 2 * NKC:
                            round_k(i, b // 2 + 2)
                        if j == 0:
                            act.wait_ge(head_ready.sem, head_ready.at(i, hp + 1))
                    if e == 2 * j + 1 and b + 1 < NBLOCK:
                        shift_rows(i, b + 1)
                    exps(i, n)
                    if e == 0 and b >= 1:
                        copy_o(i, b - 1)
                copy_o(i, NBLOCK - 1)

        @block.vector
        def _(dve):
            n_setup = [0]

            def link(ins):
                n_setup[0] += 1
                ins.then_inc(setup, 1)
                dve.wait_ge(setup, n_setup[0])

            for t in k_one:
                link(nc.vector.memset(t[HD:P].bitcast(F32), 0.0))
                link(nc.vector.memset(t[HD:HD + 1].bitcast(F32), 1.0))
            link(nc.vector.memset(ones_r[:].bitcast(F32), 1.0))
            link(nc.vector.memset(max_parts[:], -BIG))
            link(nc.vector.memset(f_one[:], 1.0))
            link(nc.vector.tensor_tensor_scan(f_pre[:], f_one[:], keep["f_tot"][:], 0.0, ALU.mult, ALU.add))
            link(nc.vector.tensor_tensor(f_pre[:], f_pre[:], keep["f_tot"][:], ALU.subtract))
            link(nc.vector.tensor_tensor(f_spread[:], f_pre[:].unsqueeze(1).to_broadcast([H, H, NT]),
                                         keep["ident"][0:H, 0:H].unsqueeze(2).to_broadcast([H, H, NT]), ALU.mult))
            dve.wait_ge(setup_pe, 1)
            link(nc.vector.tensor_copy(base[:], mx[:, 0, 0:H * NT].rearrange("p (h s) -> p h s", h=H)))
            link(nc.vector.tensor_tensor(gap[:], base[:].unsqueeze(3).to_broadcast([P, H, NT, NT]),
                                         base[:].unsqueeze(2).to_broadcast([P, H, NT, NT]), ALU.subtract))
            for h in range(H):
                local = keep["f_cols"][:, :, h].rearrange("p (s t) -> p s t", t=TT)
                last = nc.vector.tensor_tensor(bias[:, h].rearrange("p j (s t) -> p j s t", t=TT),
                                               gap[:, h].unsqueeze(3).to_broadcast([P, NT, NT, TT]),
                                               local.unsqueeze(1).to_broadcast([P, NT, NT, TT]), ALU.subtract)
            link(last)

            def start_head(i, hp):
                h = i * 2 + hp
                nc.vector.tensor_copy(bias_h[:, hp], bias[:, bass.ds(h, 1)].rearrange("p a j g -> p (a j) g"))
                nc.vector.tensor_copy(base_h[:, hp], base[:, bass.ds(h, 1)].rearrange("p a j -> p (a j)")).then_inc(head_ready.sem, 1)

            def low_k(i, n):
                hp, c = divmod(n, NKC)
                dve.wait_ge(k_high.sem, k_high.at(i, n + 1))
                cols = slice(c * KCHUNK, (c + 1) * KCHUNK)
                low = k_all[hp][HD:P, cols]
                nc.vector.tensor_tensor(low, k_raw[HD:P, n % 2], low.bitcast(F32), ALU.subtract).then_inc(k_low.sem, 1)

            def low_q(i, b):
                dve.wait_ge(q_high.sem, q_high.at(i, b + 1))
                nc.vector.tensor_tensor(q_one[0:HD, b % 2], q_raw[0:HD, b % AHEAD], q_all[0:HD, b % AHEAD].bitcast(F32), ALU.subtract).then_inc(q_low.sem, 1)

            def unit(i, b, u):
                hp, j = divmod(b, NT)
                t, c = tile_and_chunk(b, u)
                k = unit_base[b] + u
                if u == 0:
                    if j == 0:
                        dve.wait_ge(f_loaded[hp], i * 16 + 16)
                    dve.wait_ge(f_diag_ready.sem, f_diag_ready.at(i, b + 1))
                wait_apart(dve, mx_ready.sem, mx_ready.at(i, k + 1), ticks)
                bank = mx[:, k % 2]
                if c < j:
                    nc.vector.tensor_tensor_reduce(out=bank, in0=bank, in1=f_neg[:, hp, c * TILE:(c + 1) * TILE], scale=1.0,
                                                   scalar=-BIG, op0=ALU.add, op1=ALU.max,
                                                   accum_out=max_parts[:, b % 2, t, c + 1:c + 2]).then_inc(mx_done.sem, 1)
                    return
                tile = bank[:, t * P:(t + 1) * P]
                ins = nc.vector.tensor_tensor_reduce(out=tile, in0=tile, in1=f_diag[:, b % AHEAD, t], scale=1.0,
                                                     scalar=-BIG, op0=ALU.add, op1=ALU.max, accum_out=max_parts[:, b % 2, t, c + 1:c + 2])
                if t > 0:
                    rest = bank[:, 0:t * P]
                    ins = nc.vector.tensor_tensor_reduce(out=rest, in0=rest, in1=f_neg[:, hp, c * TILE:c * TILE + t * P], scale=1.0,
                                                         scalar=-BIG, op0=ALU.add, op1=ALU.max, accum_out=max_parts[:, b % 2, t, 0:1])
                ins.then_inc(mx_done.sem, 1)

            def shift_of(i, b):
                hp, j = divmod(b, NT)
                dve.wait_ge(mx_done.sem, mx_done.at(i, unit_base[b + 1]))
                dve.wait_ge(head_ready.sem, head_ready.at(i, hp + 1))
                nc.vector.tensor_reduce(max_all[:], max_parts[:, b % 2, :, 0:j + 2], AX_X, ALU.max).then_inc(max_chain.sem, 1)
                dve.wait_ge(max_chain.sem, max_chain.at(i, 2 * b + 1))
                nc.vector.tensor_scalar(max_all[:], max_all[:], -1.0, base_h[:, hp, j:j + 1], ALU.mult, ALU.subtract).then_inc(max_chain.sem, 1)
                dve.wait_ge(max_chain.sem, max_chain.at(i, 2 * b + 2))
                dve.wait_ge(shift_turned.sem, shift_turned.at(i, b))
                nc.vector.tensor_tensor(shift[:], keep["ident"][:].unsqueeze(1).to_broadcast([P, TT, P]),
                                        max_all[:].unsqueeze(2).to_broadcast([P, TT, P]), ALU.mult).then_inc(shift_ready.sem, 1)

            def mask(i, n):
                hp, j, e = STEPS[n]
                dve.wait_ge(st_ready.sem, st_ready.at(i, n + 1))
                for half in range(2):
                    tile = st[:, n % 2, half, lo(n, half):lo(n, half) + P]
                    last = nc.vector.tensor_tensor(tile, tile, tri_t[:], ALU.add)
                if j == 0 and e == 0:
                    dve.wait_ge(den_done.sem, den_done.at(i, n // 2 - 1))
                    last = nc.vector.memset(probs[:, n % RING, 1, 0:P], 0.0)
                last.then_inc(masked.sem, 1)

            def copy_den(i, b):
                dve.wait_ge(den_done.sem, den_done.at(i, last_step[b] // 2 + 1))
                dve.wait_ge(den_stored[b % 2], i * (NBLOCK // 2 * 64) + (b // 2 + 1) * 64)
                rows = P if b % NT else P // 2
                if rows < P:
                    nc.vector.memset(den_out[rows:P, b % 2], 0.0)
                nc.vector.tensor_copy(den_out[0:rows, b % 2], den_ps[0:rows]).then_inc(den_copied.sem, 1)

            dve.wait_ge(tri_ready, 4)

            with dve.Fori(0, CH) as i:
                start_head(i, 0)
                low_k(i, 0)
                low_q(i, 0)
                for u in range(TT):
                    unit(i, 0, u)
                shift_of(i, 0)
                low_k(i, 1)
                for n in range(NSTEP):
                    hp, j, e = STEPS[n]
                    b = hp * NT + j
                    if e == 0 and b + 1 < NBLOCK:
                        low_q(i, b + 1)
                    if e == 0 and b % 2 and b // 2 + 2 < 2 * NKC:
                        low_k(i, b // 2 + 2)
                    if b == NT - 1 and e == 0:
                        start_head(i, 1)
                    if diagonal(n):
                        mask(i, n)
                    for bb, u in units_in(n):
                        unit(i, bb, u)
                    if e == 2 * j and b + 1 < NBLOCK:
                        shift_of(i, b + 1)
                    if b >= 1 and e == 1:
                        copy_den(i, b - 1)
                copy_den(i, NBLOCK - 1)

        @block.tensor
        def _(pe):
            pe.wait_ge(setup, 10)
            nc.tensor.matmul(mx[:, 0, 0:H * NT], keep["ones"][0:H], f_spread[:].rearrange("a h s -> a (h s)"), start=True, stop=True).then_inc(setup_pe, 1)
            pe.wait_ge(setup, 11)

            def unit(i, b, u):
                hp, j = divmod(b, NT)
                t, c = tile_and_chunk(b, u)
                k = unit_base[b] + u
                if u == 0:
                    pe.wait_ge(q_high.sem, q_high.at(i, b + 1))
                    if b % 2 == 0:
                        pe.wait_ge(k_low.sem, k_low.at(i, b // 2 + 1))
                pe.wait_ge(mx_done.sem, mx_done.at(i, k - 1))
                if k in spread_at:
                    pe.wait_ge(q_shift.sem, q_shift.at(i, max(c for c in range(NBLOCK) if spread_at[c] == k) + 1))
                width = TILE if c < j else (t + 1) * P
                nc.tensor.matmul(mx[:, k % 2, 0:width], q_all[:, b % AHEAD, t * P:(t + 1) * P],
                                 k_all[hp][:, c * TILE:c * TILE + width], start=True, stop=True).then_inc(mx_ready.sem, 1)

            def spread_shift(i, b):
                pe.wait_ge(shift_ready.sem, shift_ready.at(i, b + 1))
                pe.wait_ge(mx_done.sem, mx_done.at(i, spread_at[b] - 1))
                nc.tensor.matmul(mx[:, spread_at[b] % 2], ones_r[:], shift[:].rearrange("p t q -> p (t q)"), start=True, stop=True).then_inc(shift_turned.sem, 1)

            def scores(i, n):
                hp, j, e = STEPS[n]
                b = hp * NT + j
                if e == 0:
                    pe.wait_ge(q_shift.sem, q_shift.at(i, b + 1))
                    pe.wait_ge(q_low.sem, q_low.at(i, b + 1))
                pe.wait_ge(exp_done.sem, exp_done.at(i, n - 1))
                for half in range(2):
                    blk = 2 * e + half
                    first = lo(n, half)
                    keys = slice(blk * P, (blk + 1) * P)
                    nc.tensor.matmul(st[:, n % 2, half, first:TILE], k_all[hp][:, keys], q_all[:, b % AHEAD, first:TILE], start=True, stop=False)
                    last = nc.tensor.matmul(st[:, n % 2, half, first:TILE], k_one[hp][:, keys], q_one[:, b % 2, first:TILE], start=False, stop=True)
                last.then_inc(st_ready.sem, 1)

            def weigh(i, n):
                hp, j, e = STEPS[n]
                b = hp * NT + j
                pe.wait_ge(exp_done.sem, exp_done.at(i, n + 1))
                if e == 0:
                    pe.wait_ge(o_copied.sem, o_copied.at(i, b))
                    if j == 0:
                        pe.wait_ge(v_loaded[hp], i * 16 + 16)
                for half in range(2):
                    first = lo(n, half) if b % NT or e else 0
                    last = nc.tensor.matmul(o_ps[half * HD:(half + 1) * HD, first:TILE], v[:, hp, 2 * e + half],
                                            probs[:, n % RING, half, first:TILE], start=(e == 0), stop=(e == 2 * j + 1))
                last.then_inc(pv_done.sem, 1)

            def sum_probs(i, n):
                hp, j, e = STEPS[n]
                if e == 1:
                    pe.wait_ge(den_copied.sem, den_copied.at(i, hp * NT + j))
                for group in range(4):
                    step, half = n - 1 + group // 2, group % 2
                    first = lo(step, half) if j or group > 1 else 0
                    at = group if j else half
                    last = nc.tensor.matmul(den_ps[at * 32:(at + 1) * 32, first:TILE], keep["ones"][:, 0:32], probs[:, step % RING, half, first:TILE],
                                            start=(e == 1 and (j > 0 or group < 2)), stop=(e == 2 * j + 1 and (j > 0 or group > 1)))
                last.then_inc(den_done.sem, 1)

            with pe.Fori(0, CH) as i:
                for u in range(TT):
                    unit(i, 0, u)
                spread_shift(i, 0)
                for n in range(NSTEP):
                    hp, j, e = STEPS[n]
                    b = hp * NT + j
                    scores(i, n)
                    if e == 2 * j + 1 and b + 1 < NBLOCK:
                        spread_shift(i, b + 1)
                        early = 0
                    else:
                        early = 2
                    for bb, u in units_in(n)[:early]:
                        unit(i, bb, u)
                    if n >= 1:
                        weigh(i, n - 1)
                    for bb, u in units_in(n)[early:]:
                        unit(i, bb, u)
                    if n >= 1 and STEPS[n - 1][2] % 2:
                        sum_probs(i, n - 1)
                weigh(i, NSTEP - 1)
                sum_probs(i, NSTEP - 1)


INVERTED = 9
BANDS_READY = 12
LAST_COPY = 17


def phase_gates(nc, io, keep):
    NW = 3 * W
    DEN = H * SEQ // P
    HALO = 16
    with ExitStack() as ctx:
        m = Alloc(nc, ctx, "ga")
        w_high = m.sb("w_high", [P, KC, NW], F32R)
        w_low = m.sb("w_low", [P, KC, NW], F32R)
        norm_col = m.sb("norm_col", [P, KC])
        h_t = m.sb("h_t", [P, KC, TILE])
        h_high = m.sb("h_high", [P, KC, TILE], F32R)
        h_low = m.sb("h_low", [P, KC, TILE], F32R)
        stage = m.sb("stage", [P, 2, CH, TILE])
        pool_stage, gate_stage = stage[:, 0], stage[:, 1]
        w_raw = stage[:].rearrange("p a c t -> p (a c t)")
        u_t = m.sb("u_t", [P, CH, HALO + TILE])
        sums = m.sb("sums", [P, 2, HALO + TILE])
        early = m.sb("early", [P, CH, HALO])
        pooled_high = m.sb("pooled_high", [P, TILE], F32R)
        pooled_low = m.sb("pooled_low", [P, TILE], F32R)
        sig = m.sb("sig", [P, 2, TILE])
        pw_raw = m.sb("pw_raw", [P, CH, P])
        pw_high = m.sb("pw_high", [P, CH, P], F32R)
        pw_low = m.sb("pw_low", [P, CH, P], F32R)
        scale_col = m.sb("scale_col", [P, CH])
        hist = m.sb("hist", [DB * HIST, W])
        us_rows = m.sb("us_rows", [NS, W])
        sig_s = m.sb("sig_s", [NS, 2, W])
        scale_row = m.sb("scale_row", [NS, W])
        band_hist = m.sb("band_hist", [DB * HIST, CH, NS])
        band_new = m.sb("band_new", [NS, CH, NS])
        pooled_s = m.sb("pooled_s", [P, CH, NS])
        u_last = scale_row[0:HIST]
        den = sums[:].rearrange("p a t -> p (a t)")[:, 0:4 * DEN].rearrange("p (f t) -> p f t", f=4)

        acc = m.ps("acc", [P, 3, TILE])
        mixed = m.ps("mixed", [P, 2, TILE])
        s_ps = m.ps("s_ps", [P, CH, NS])
        last_ps = m.ps("last_ps", [HIST, W])

        den_loaded = m.sem("den_loaded")
        inv_stored = m.sem("inv_stored")
        const_loaded = m.sem("const_loaded")
        w_loaded = [m.sem(f"w_loaded{i}") for i in range(2)]
        w_high_ready = m.sem("w_high_ready")
        w_low_dve = m.sem("w_low_dve")
        h_loaded = m.sem("h_loaded")
        h_split = Count(m.sem("h_split"), KC)
        bands = m.sem("bands")
        setup = m.sem("setup")
        s_done = m.sem("s_done")
        s_sig = m.sem("s_sig")
        s_pooled = m.sem("s_pooled")
        s_stored = m.sem("s_stored")
        acc_done = Count(m.sem("acc_done"), 12)
        u_evac = Count(m.sem("u_evac"), CH)
        sig_ready = Count(m.sem("sig_ready"), 2 * CH)
        gate_done = Count(m.sem("gate_done"), 2 * CH, 3)
        halo_free = Count(m.sem("halo_free"), CH, CH)
        pooled_ready = Count(m.sem("pooled_ready"), CH)
        mixed_done = Count(m.sem("mixed_done"), CH)
        pool_out = Count(m.sem("pool_out"), CH, 2)
        PER = 4 * CH + sum(g + 1 for g in range(CH))
        dve_chain = m.sem("dve_chain")
        pool_stored = m.sem("pool_stored")
        gate_stored = m.sem("gate_stored")
        last_turned = m.sem("last_turned")

        w_in = io["w_in"][0]

        block = ctx.enter_context(nc.Block())

        @block.sync
        def _(sp):
            sp.dma_start(norm_col[:], io["norm_w"].rearrange("l (c p) -> p (l c)", p=P), allow_slow_non_contiguous=True).then_inc(const_loaded, 16)
            sp.dma_start(scale_col[:], io["pool_scale"].rearrange("l (c p) -> p (l c)", p=P), allow_slow_non_contiguous=True).then_inc(const_loaded, 16)
            sp.dma_start(scale_row[:], io["pool_scale"].to_broadcast([NS, W])).then_inc(const_loaded, 16)
            for c in range(KC):
                if c >= 2:
                    sp.wait_ge(w_low_dve, c - 1)
                rows = w_in[c * P:(c + 1) * P]
                slot = w_raw[:, (c % 2) * NW:(c % 2 + 1) * NW]
                sp.dma_start(slot[:, 0:2 * W], rows[:, U0:U0 + 2 * W]).then_inc(w_loaded[c % 2], 16)
                sp.dma_start(slot[:, 2 * W:NW], rows[:, GA0:GA0 + W]).then_inc(w_loaded[c % 2], 16)
                if c == 1:
                    sp.dma_start(h_t[:], io["h_t"][0]).then_inc(h_loaded, 16)
                    sp.dma_start(pw_raw[:], io["pool_w"].rearrange("l g c d -> c (l g) d")).then_inc(const_loaded, 16)
                    sp.dma_start(hist[:], io["state_pool"].rearrange("l b i c -> (l b i) c")).then_inc(const_loaded, 16)
                    sp.dma_start(den, io["den"].rearrange("f h (a t) -> (h a) f t", t=DEN)).then_inc(den_loaded, 16)
            sp.wait_ge(setup, INVERTED)
            sp.dma_start(io["inv_den"].rearrange("h (a t) -> (h a) t", t=DEN), den[:, 0]).then_inc(inv_stored, 16)
            sp.dma_start(io["pool_sample"][0, :, 0:HIST - DS], io["state_pool"][0, :, DS:HIST]).then_inc(s_stored, 16)
            sp.wait_ge(s_sig, 1)
            for b in range(DB):
                sp.dma_start(io["pool_sample"][0, b, HIST - DS:HIST], us_rows[b * DS:(b + 1) * DS]).then_inc(s_stored, 16)

            def super_tile(s, more):
                if more:
                    sp.wait_ge(h_split.sem, h_split.at(s, KC))
                    sp.dma_start(h_t[:], io["h_t"][bass.ds(s + 1, 1)].rearrange("a p k t -> p (a k) t")).then_inc(h_loaded, 16)
                sp.wait_ge(pool_out.sem, pool_out.at(s, CH))
                sp.dma_start(io["pool_t"].rearrange("c p t -> p c t")[:, :, bass.ds(s * TILE, TILE)], pool_stage).then_inc(pool_stored, 16)
                sp.wait_ge(gate_done.sem, gate_done.at(s, 2 * CH))
                sp.dma_start(io["gate_t"].rearrange("c p t -> p c t")[:, :, bass.ds(s * TILE, TILE)], gate_stage).then_inc(gate_stored, 16)

            with sp.Fori(0, NT - 1) as s:
                super_tile(s, True)
            super_tile(NT - 1, False)
            sp.wait_ge(setup, LAST_COPY)
            sp.dma_start(io["pool_prompt"].rearrange("l b i c -> (l b i) c"), u_last).then_inc(s_stored, 16)
            sp.wait_ge(s_stored, 16 * (DB + 2))
            sp.wait_ge(pool_stored, 16 * (NT + 1))
            sp.wait_ge(gate_stored, 16 * (NT + 1))

        @block.gpsimd
        def _(pool):
            for c in (gate_done, halo_free, pool_out):
                pool.sem_inc(c.sem, c.credit)
            pool.sem_inc(pool_stored, 16)
            pool.sem_inc(gate_stored, 16)
            n = 0
            for g, w in enumerate(WINDOWS):
                old, new = band_hist[:, g].rearrange("p (b t) -> p b t", b=DB), band_new[:, g].rearrange("p (b t) -> p b t", b=DB)
                steps = [lambda: nc.gpsimd.memset(old, 1.0 / w), lambda: nc.gpsimd.memset(new, 1.0 / w)]
                steps += [lambda o=o, a=a, p=p, k=k: nc.gpsimd.affine_select(out=o, in_=o, compare_op=ALU.is_ge, fill=0.0,
                                                                           base=a, pattern=p, channel_multiplier=k)
                          for o, a, p, k in ((old, w - HIST - 1, [[-HIST, DB], [-1, DS]], 1), (old, HIST - 1, [[HIST, DB], [0, DS]], -1),
                                             (new, 0, [[-DS, DB], [0, DS]], 1), (new, 0, [[DS, DB], [1, DS]], -1),
                                             (new, w - 1, [[-DS, DB], [-1, DS]], 1))]
                for step in steps:
                    n += 1
                    step().then_inc(bands, 1)
                    pool.wait_ge(bands, n)

        @block.scalar
        def _(act):
            act.wait_ge(const_loaded, 48)
            for c in range(KC):
                act.wait_ge(w_loaded[c % 2], 32 * (c // 2 + 1))
                nc.scalar.activation(w_high[:, c], w_raw[:, (c % 2) * NW:(c % 2 + 1) * NW], ACT.Copy, scale=norm_col[:, c:c + 1]).then_inc(w_high_ready, 1)
            for n in range(3):
                act.wait_ge(s_done, n + 1)
                if n == 0:
                    nc.scalar.activation(us_rows[:], acc[0:NS, 0], ACT.Copy).then_inc(s_sig, 1)
                else:
                    nc.scalar.activation(sig_s[:, n - 1], acc[0:NS, n], ACT.Sigmoid).then_inc(s_sig, 1)

            def super_tile(s):
                for u in range(3 * CH):
                    act.wait_ge(acc_done.sem, acc_done.at(s, u + 1))
                    if u < CH:
                        act.wait_ge(halo_free.sem, halo_free.at(s, u + 1 - CH))
                        nc.scalar.activation(u_t[:, u, HALO:], acc[:, u % 3], ACT.Copy).then_inc(u_evac.sem, 1)
                    else:
                        k = u - CH
                        act.wait_ge(gate_done.sem, gate_done.at(s, k - 1))
                        nc.scalar.activation(sig[:, k % 2], acc[:, u % 3], ACT.Sigmoid).then_inc(sig_ready.sem, 1)

            with act.Fori(0, NT) as s:
                super_tile(s)

        @block.vector
        def _(dve):
            n_setup = [0]

            def link(ins):
                n_setup[0] += 1
                ins.then_inc(setup, 1)
                dve.wait_ge(setup, n_setup[0])

            for g in range(CH):
                link(nc.vector.memset(u_t[:, g, 0:HALO], 0.0))
            link(nc.vector.memset(early[:], 1.0))
            for g, w in enumerate(WINDOWS):
                for t in range(w - 1):
                    last = nc.vector.memset(early[:, g, t:t + 1], w / (t + 1))
            link(last)
            dve.wait_ge(const_loaded, 48)

            for c in range(KC):
                dve.wait_ge(w_high_ready, c + 1)
                nc.vector.scalar_tensor_tensor(out=w_low[:, c], in0=w_raw[:, (c % 2) * NW:(c % 2 + 1) * NW], scalar=norm_col[:, c:c + 1],
                                               in1=w_high[:, c].bitcast(F32), op0=ALU.mult, op1=ALU.subtract).then_inc(w_low_dve, 1)
            dve.wait_ge(den_loaded, 16)
            link(nc.vector.tensor_tensor(den[:, 0:2], den[:, 0:2], den[:, 2:4], ALU.add))
            link(nc.vector.tensor_tensor(den[:, 0], den[:, 0], den[:, 1], ALU.add))
            link(nc.vector.reciprocal(den[:, 0], den[:, 0]))
            assert n_setup[0] == INVERTED
            dve.wait_ge(const_loaded, 80)
            link(nc.vector.tensor_copy(pw_high[:], pw_raw[:]))
            link(nc.vector.tensor_tensor(pw_low[:], pw_raw[:], pw_high[:].bitcast(F32), ALU.subtract))

            def split_h(s, chain):
                dve.wait_ge(h_loaded, s * 16 + 16)
                for c in range(KC):
                    chain.link(nc.vector.tensor_copy(h_high[:, c], h_t[:, c]))
                    nc.vector.tensor_tensor(h_low[:, c], h_t[:, c], h_high[:, c].bitcast(F32), ALU.subtract).then_inc(h_split.sem, 1)

            dve.wait_ge(bands, 7 * CH)
            for g in range(CH):
                last = nc.vector.tensor_tensor(band_new[:, g], band_new[:, g], keep["ident"][0:NS, 0:NS], ALU.subtract)
            link(last)
            ready = n_setup[0]
            dve.wait_ge(s_pooled, 1)
            link(nc.vector.tensor_copy(pooled_s[:], s_ps[:]))
            dve.wait_ge(s_sig, 3)
            link(nc.vector.tensor_tensor(sig_s[:, 0], acc[0:NS, 1], sig_s[:, 0], ALU.mult))
            link(nc.vector.tensor_tensor(sig_s[:, 0], sig_s[:, 0], scale_row[:], ALU.mult))
            nc.vector.tensor_tensor(keep["mix_s"][:, W:D], acc[0:NS, 2], sig_s[:, 1], ALU.mult).then_inc(s_pooled, 1)
            dve.wait_ge(s_pooled, 3)
            link(nc.vector.tensor_tensor(keep["mix_s"][:, 0:W], mixed[0:NS, 0], sig_s[:, 0], ALU.mult))
            nc.vector.nop().then_inc(s_pooled, 1)

            first = Chain(dve, dve_chain)
            split_h(0, first)
            dve.wait_ge(inv_stored, 16)
            base = first.n

            def super_tile(s, more):
                chain = Chain(dve, dve_chain, s * (PER + KC) + base)
                for g, w in enumerate(WINDOWS):
                    dve.wait_ge(u_evac.sem, u_evac.at(s, g + 1))
                    src, step = u_t[:, g], 1
                    for r in range(g + 1):
                        dst = sums[:, r % 2]
                        chain.link(nc.vector.tensor_tensor(dst[:, 2 * step - 1 if r < g else HALO:], src[:, 2 * step - 1 if r < g else HALO:],
                                                           src[:, (2 * step - 1 if r < g else HALO) - step:HALO + TILE - step], ALU.add))
                        src, step = dst, step * 2
                    chain.link(nc.vector.tensor_tensor(src[:, HALO:2 * HALO], src[:, HALO:2 * HALO], early[:, g], ALU.mult))
                    chain.link(nc.vector.scalar_tensor_tensor(out=src[:, HALO:], in0=src[:, HALO:], scalar=1.0 / w, in1=u_t[:, g, HALO:],
                                                              op0=ALU.mult, op1=ALU.subtract))
                    pooled = src[:, HALO:]
                    nc.vector.tensor_copy(u_t[:, g, 0:HALO], u_t[:, g, TILE:]).then_inc(halo_free.sem, 1)
                    dve.wait_ge(mixed_done.sem, mixed_done.at(s, g)) if g else None
                    if g == 0:
                        dve.wait_ge(pool_out.sem, pool_out.at(s, 0))
                    chain.link(nc.vector.tensor_copy(pooled_high[:], pooled))
                    chain.link(nc.vector.tensor_tensor(pooled_low[:], pooled, pooled_high[:].bitcast(F32), ALU.subtract))
                    nc.vector.nop().then_inc(pooled_ready.sem, 1)
                    if g == 0:
                        dve.wait_ge(pool_stored, s * 16 + 16)
                    dve.wait_ge(sig_ready.sem, sig_ready.at(s, g + 1))
                    gate = pool_stage[:, g]
                    nc.vector.tensor_tensor(gate, acc[:, (CH + g) % 3], sig[:, g % 2], ALU.mult).then_inc(gate_done.sem, 1)
                    dve.wait_ge(gate_done.sem, gate_done.at(s, g + 1))
                    dve.wait_ge(mixed_done.sem, mixed_done.at(s, g + 1))
                    nc.vector.scalar_tensor_tensor(out=gate, in0=mixed[:, g % 2], scalar=scale_col[:, g:g + 1], in1=gate,
                                                   op0=ALU.mult, op1=ALU.mult).then_inc(pool_out.sem, 1)
                for c in range(CH):
                    k = CH + c
                    if c == 0:
                        dve.wait_ge(gate_stored, s * 16 + 16)
                    dve.wait_ge(sig_ready.sem, sig_ready.at(s, k + 1))
                    nc.vector.tensor_tensor(gate_stage[:, c], acc[:, (CH + k) % 3], sig[:, k % 2], ALU.mult).then_inc(gate_done.sem, 1)
                    if c == CH - 1:
                        nc.vector.memset(early[:], 1.0)
                        if more:
                            split_h(s + 1, chain)
                assert chain.n == PER + (KC if more else 0), (chain.n, PER)

            with dve.Fori(0, NT - 1) as s:
                super_tile(s, True)
            super_tile(NT - 1, False)
            dve.wait_ge(last_turned, 1)
            link(nc.vector.tensor_copy(u_last, last_ps[:]))
            assert n_setup[0] == LAST_COPY, n_setup

        @block.tensor
        def _(pe):
            for c in range(KC):
                pe.wait_ge(w_low_dve, c + 1)
                for n in range(3):
                    cols = slice(n * W, (n + 1) * W)
                    last = three_pass(nc, acc[0:NS, n], keep["hs_high"][:, c], keep["hs_low"][:, c],
                                      w_high[:, c, cols], w_low[:, c, cols], c == 0, c == KC - 1)
                    if c == KC - 1:
                        last.then_inc(s_done, 1)
            pe.wait_ge(setup, BANDS_READY)
            pe.wait_ge(s_sig, 1)
            for g in range(CH):
                cols = slice(g * P, (g + 1) * P)
                nc.tensor.matmul(s_ps[:, g], hist[:, cols], band_hist[:, g], start=True, stop=False)
                last = nc.tensor.matmul(s_ps[:, g], us_rows[:, cols], band_new[:, g], start=False, stop=True)
            last.then_inc(s_pooled, 1)
            pe.wait_ge(setup, BANDS_READY + 1)
            for g in range(CH):
                last = nc.tensor.matmul(mixed[0:NS, 0, g * P:(g + 1) * P], pooled_s[:, g], pw_raw[:, g], start=True, stop=True)
            last.then_inc(s_pooled, 1)
            pe.wait_ge(s_pooled, 4)

            def super_tile(s):
                for u in range(3 * CH):
                    if u < 3:
                        pe.wait_ge(gate_done.sem, gate_done.at(s, u - 2))
                    elif u < CH + 3:
                        pe.wait_ge(u_evac.sem, u_evac.at(s, u - 2))
                    else:
                        pe.wait_ge(gate_done.sem, gate_done.at(s, u - CH - 2))
                    cols = slice(u * P, (u + 1) * P)
                    for c in range(KC):
                        if u == 0:
                            pe.wait_ge(h_split.sem, h_split.at(s, c + 1))
                        last = three_pass(nc, acc[:, u % 3], w_high[:, c, cols], w_low[:, c, cols],
                                          h_high[:, c], h_low[:, c], c == 0, c == KC - 1)
                    last.then_inc(acc_done.sem, 1)
                    if CH < u <= 2 * CH:
                        g = u - CH - 1
                        pe.wait_ge(pooled_ready.sem, pooled_ready.at(s, g + 1))
                        pe.wait_ge(pool_out.sem, pool_out.at(s, g - 1))
                        three_pass(nc, mixed[:, g % 2], pw_high[:, g], pw_low[:, g], pooled_high[:], pooled_low[:],
                                   True, True).then_inc(mixed_done.sem, 1)

            with pe.Fori(0, NT) as s:
                super_tile(s)
            for g in range(CH):
                last = nc.tensor.transpose(last_ps[:, g * P:(g + 1) * P], u_t[:, g, HALO + TILE - HIST:], keep["ident"][:])
            last.then_inc(last_turned, 1)


def phase_merge(nc, io, keep):
    UNIT = 2 * P
    A0, A1, GATE, POOL, INV = range(5)
    with ExitStack() as ctx:
        m = Alloc(nc, ctx, "mg")
        w_high = m.sb("w_high", [P, KC, D], F32R)
        w_low = m.sb("w_low", [P, KC, D], F32R)
        w_raw = m.sb("w_raw", [P, 2, D])
        raw = m.sb("raw", [P, 2, 5, CH, UNIT])
        mix_high = m.sb("mix_high", [P, 2, KC, UNIT], F32R)
        mix_low = m.sb("mix_low", [P, 2, KC, UNIT], F32R)
        x = m.sb("x", [P, TT, D])
        norm_row = m.sb("norm_row", [P, D])
        junk = m.sb("junk", [P, D], BF16)
        squares = m.sb("squares", [P, TT])
        rms = m.sb("rms", [P, TT])
        minus_half = m.sb("minus_half", [P, 1])
        eps_sum = m.sb("eps_sum", [P, 1])
        xs = m.sb("xs", [NS, D])
        attn_s = m.sb("attn_s", [NS, W])
        ms_high = m.sb("ms_high", [P, KC, NS], F32R)
        ms_low = m.sb("ms_low", [P, KC, NS], F32R)

        acc = m.ps("acc", [P, 2, D])
        s_ps = m.ps("s_ps", [P, KC, NS])

        const_loaded = m.sem("const_loaded")
        w_loaded = [m.sem(f"w_loaded{i}") for i in range(2)]
        w_split = m.sem("w_split")
        setup = m.sem("setup")
        s_turned = m.sem("s_turned")
        s_split = m.sem("s_split")
        s_done = m.sem("s_done")
        s_squares = m.sem("s_squares")
        s_rms = m.sem("s_rms")
        s_ready = m.sem("s_ready")
        s_stored = m.sem("s_stored")
        raw_loaded = [m.sem(f"raw_loaded{i}") for i in range(2)]
        raw_free = [m.sem(f"raw_free{i}") for i in range(2)]
        x_loaded = [m.sem(f"x_loaded{i}") for i in range(2)]
        y_stored = [m.sem(f"y_stored{i}") for i in range(2)]
        mix_ready = Count(m.sem("mix_ready"), 2)
        acc_done = Count(m.sem("acc_done"), TT, TT)
        added = Count(m.sem("added"), TT, 2)
        squares_ready = Count(m.sem("squares_ready"), TT)
        rms_ready = Count(m.sem("rms_ready"), TT)
        y_ready = Count(m.sem("y_ready"), TT)
        dve_chain = m.sem("dve_chain")
        pool_chain = m.sem("pool_chain")

        x_in = io["x_prompt"][0].rearrange("(u k p) d -> p u k d", p=P, k=2)
        y_out = io["y_prompt"][0].rearrange("(u k p) d -> p u k d", p=P, k=2)

        block = ctx.enter_context(nc.Block())

        @block.sync
        def _(sp):
            def load_mix(g, b):
                at = bass.ds(g * TILE + b * UNIT, UNIT)
                for kind, src in ((POOL, io["pool_t"]), (A0, io["attn_t"][0]), (A1, io["attn_t"][1]), (GATE, io["gate_t"])):
                    sp.dma_start(raw[:, b, kind], src.rearrange("c p t -> p c t")[:, :, at]).then_inc(raw_loaded[b], 16)
                for e, rows in enumerate((io["inv_den"].rearrange("(c e) t -> e c t", e=2)[0:1], io["inv_den"].rearrange("(c e) t -> e c t", e=2)[1:2])):
                    sp.dma_start(raw[e * HD:(e + 1) * HD, b, INV], rows[:, :, at].to_broadcast([HD, CH, UNIT])).then_inc(raw_loaded[b], 16)

            def load_x(g, b):
                sp.dma_start(x[:, 2 * b:2 * b + 2], x_in[:, bass.ds(g * 2 + b, 1)].rearrange("p a k d -> p (a k) d")).then_inc(x_loaded[b], 16)

            def store_y(g, b):
                sp.wait_ge(y_ready.sem, y_ready.at(g, 2 * b + 2))
                sp.dma_start(y_out[:, bass.ds(g * 2 + b, 1)].rearrange("p a k d -> p (a k) d"), x[:, 2 * b:2 * b + 2]).then_inc(y_stored[b], 16)

            for c in range(KC):
                if c >= 2:
                    sp.wait_ge(w_split, c - 1)
                sp.dma_start(w_raw[:, c % 2], io["w_out"][0, c * P:(c + 1) * P]).then_inc(w_loaded[c % 2], 16)
                if c == 1:
                    sp.dma_start(attn_s[:], io["attn_s"]).then_inc(const_loaded, 16)
                    sp.dma_start(xs[:], io["x_sample"].rearrange("b t d -> (b t) d")).then_inc(const_loaded, 16)
                    sp.dma_start(norm_row[:], io["norm_f"].rearrange("(a d) -> a d", a=1).to_broadcast([P, D])).then_inc(const_loaded, 16)
            for b in range(2):
                load_mix(0, b)
                load_x(0, b)
            sp.wait_ge(s_ready, 1)
            sp.dma_start(io["y_sample"].rearrange("b t d -> (b t) d"), xs[:]).then_inc(s_stored, 16)

            with sp.Fori(0, NT - 1) as g:
                for b in range(2):
                    sp.wait_ge(raw_free[b], g + 1)
                    load_mix(g + 1, b)
                    store_y(g, b)
                    sp.wait_ge(y_stored[b], g * 16 + 16)
                    load_x(g + 1, b)
            for b in range(2):
                store_y(NT - 1, b)
            sp.wait_ge(s_stored, 16)
            for b in range(2):
                sp.wait_ge(y_stored[b], NT * 16)

        @block.gpsimd
        def _(pool):
            pool.sem_inc(acc_done.sem, acc_done.credit)
            pool.sem_inc(added.sem, added.credit)
            nc.gpsimd.memset(minus_half[:], -0.5)
            nc.gpsimd.memset(eps_sum[:], D * EPS).then_inc(pool_chain, 1)
            pool.wait_ge(pool_chain, 1)

            def rms_of(rows, n, done, chain):
                out = rms[0:rows, n:n + 1]
                chain.link(nc.gpsimd.tensor_tensor(out, squares[0:rows, n:n + 1], eps_sum[0:rows], ALU.add))
                nc.gpsimd.tensor_tensor(out, out, minus_half[0:rows], ALU.pow).then_inc(done, 1)

            pool.wait_ge(s_squares, 1)
            rms_of(NS, 0, s_rms, Chain(pool, pool_chain, 1))
            with pool.Fori(0, NT) as g:
                chain = Chain(pool, pool_chain, g * TT + 2)
                for t in range(TT):
                    pool.wait_ge(squares_ready.sem, squares_ready.at(g, t + 1))
                    rms_of(P, t, rms_ready.sem, chain)

        @block.scalar
        def _(act):
            act.wait_ge(s_done, 2)
            nc.scalar.activation(junk[0:NS], xs[:], ACT.Square, accum_out=squares[0:NS, 0:1]).then_inc(s_squares, 1)
            act.wait_ge(s_ready, 1)
            with act.Fori(0, NT) as g:
                for t in range(TT):
                    act.wait_ge(added.sem, added.at(g, t + 1))
                    if t:
                        act.wait_ge(squares_ready.sem, squares_ready.at(g, t))
                    nc.scalar.activation(junk[:], x[:, t], ACT.Square, accum_out=squares[:, t:t + 1]).then_inc(squares_ready.sem, 1)
                act.wait_ge(squares_ready.sem, squares_ready.at(g, TT))

        @block.vector
        def _(dve):
            start = Chain(dve, setup)
            for c in range(KC):
                dve.wait_ge(w_loaded[c % 2], 16 * (c // 2 + 1))
                start.link(nc.vector.tensor_copy(w_high[:, c], w_raw[:, c % 2]))
                nc.vector.tensor_tensor(w_low[:, c], w_raw[:, c % 2], w_high[:, c].bitcast(F32), ALU.subtract).then_inc(w_split, 1)
                if c == 1:
                    dve.wait_ge(const_loaded, 48)
                    start.link(nc.vector.tensor_tensor(keep["mix_s"][:, W:D], keep["mix_s"][:, W:D], attn_s[:], ALU.mult))
                    nc.vector.nop().then_inc(s_split, 1)
                    start.link(nc.vector.tensor_scalar(norm_row[:], norm_row[:], ROOT_D, None, ALU.mult))
                if c == 2:
                    dve.wait_ge(s_turned, 1)
                    start.link(nc.vector.tensor_copy(ms_high[:], s_ps[:]))
                    nc.vector.tensor_tensor(ms_low[:], s_ps[:], ms_high[:].bitcast(F32), ALU.subtract).then_inc(s_split, 1)

            def split_mix(g, b, chain):
                dve.wait_ge(raw_loaded[b], g * 96 + 96)
                dve.wait_ge(acc_done.sem, acc_done.at(g, 2 * b + 2 - TT))
                r, high, low = raw[:, b], mix_high[:, b], mix_low[:, b]
                nc.vector.tensor_tensor(r[:, A0], r[:, A0], r[:, A1], ALU.add)
                nc.vector.tensor_tensor(r[:, GATE], r[:, GATE], r[:, INV], ALU.mult)
                chain.link(nc.vector.tensor_copy(high[:, 0:CH], r[:, POOL]))
                nc.vector.tensor_tensor(low[:, 0:CH], r[:, POOL], high[:, 0:CH].bitcast(F32), ALU.subtract)
                chain.link(nc.vector.tensor_tensor(r[:, A0], r[:, A0], r[:, GATE], ALU.mult))
                chain.link(nc.vector.tensor_copy(high[:, CH:KC], r[:, A0]))
                nc.vector.tensor_tensor(low[:, CH:KC], r[:, A0], high[:, CH:KC].bitcast(F32), ALU.subtract).then_inc(mix_ready.sem, 1)
                nc.vector.nop().then_inc(raw_free[b], 1)

            def add_x(g, t):
                if t % 2 == 0:
                    dve.wait_ge(x_loaded[t // 2], g * 16 + 16)
                dve.wait_ge(acc_done.sem, acc_done.at(g, t + 1))
                nc.vector.tensor_tensor(x[:, t], acc[:, t % 2], x[:, t], ALU.add).then_inc(added.sem, 1)

            def scale(g, t):
                dve.wait_ge(rms_ready.sem, rms_ready.at(g, t + 1))
                nc.vector.scalar_tensor_tensor(out=x[:, t], in0=x[:, t], scalar=rms[:, t:t + 1], in1=norm_row[:],
                                               op0=ALU.mult, op1=ALU.mult).then_inc(y_ready.sem, 1)

            split_mix(0, 0, Chain(dve, dve_chain))
            dve.wait_ge(s_done, 1)
            nc.vector.tensor_tensor(xs[:], acc[0:NS, 0], xs[:], ALU.add).then_inc(s_done, 1)
            dve.wait_ge(s_rms, 1)
            nc.vector.scalar_tensor_tensor(out=xs[:], in0=xs[:], scalar=rms[0:NS, 0:1], in1=norm_row[0:NS],
                                           op0=ALU.mult, op1=ALU.mult).then_inc(s_ready, 1)

            def finish(g, b):
                add_x(g, 2 * b)
                scale(g, 2 * b)
                add_x(g, 2 * b + 1)

            def step(g, last):
                split_mix(g, 1, Chain(dve, dve_chain, g * 6 + 3))
                finish(g, 0)
                if not last:
                    split_mix(g + 1, 0, Chain(dve, dve_chain, g * 6 + 6))
                scale(g, 1)
                finish(g, 1)
                scale(g, 3)

            with dve.Fori(0, NT - 1) as g:
                step(g, False)
            step(NT - 1, True)

        @block.tensor
        def _(pe):
            pe.wait_ge(s_split, 1)
            for c in range(KC):
                last = nc.tensor.transpose(s_ps[:, c], keep["mix_s"][:, c * P:(c + 1) * P], keep["ident"][0:NS, 0:NS])
            last.then_inc(s_turned, 1)
            pe.wait_ge(s_split, 2)
            for c in range(KC):
                pe.wait_ge(w_split, c + 1)
                for half in range(2):
                    cols = slice(half * W, (half + 1) * W)
                    last = three_pass(nc, acc[0:NS, 0, cols], ms_high[:, c], ms_low[:, c], w_high[:, c, cols], w_low[:, c, cols],
                                      c == 0, c == KC - 1)
            last.then_inc(s_done, 1)
            pe.wait_ge(s_done, 2)

            with pe.Fori(0, NT) as g:
                for t in range(TT):
                    b, tile = t // 2, slice(t % 2 * P, (t % 2 + 1) * P)
                    if t % 2 == 0:
                        pe.wait_ge(mix_ready.sem, mix_ready.at(g, b + 1))
                    pe.wait_ge(added.sem, added.at(g, t - 1))
                    for half in range(2):
                        cols = slice(half * W, (half + 1) * W)
                        for c in range(KC):
                            last = three_pass(nc, acc[:, t % 2, cols], mix_high[:, b, c, tile], mix_low[:, b, c, tile],
                                              w_high[:, c, cols], w_low[:, c, cols], c == 0, c == KC - 1)
                    last.then_inc(acc_done.sem, 1)


def phase_decode(nc, io, keep):
    HB = DB // 2
    PG = 2
    STEP = PG * PAGE
    RING = 4
    STEPS = NPAGE // PG
    ITERS = STEPS // RING
    PAST = NPAGE * PAGE
    LOADED = HB // 2 * PG * 16
    R = HB * H * DS
    with ExitStack() as ctx:
        m = Alloc(nc, ctx, "dc")
        table = m.sb("table", [1, DB * NPAGE], I32)
        page_of = m.sb("page_of", [P, 2], I32)
        lf_pages = m.sb("lf_pages", [P, 2, PAGE * H])
        lf_rows = m.sb("lf_rows", [P, NPAGE, R])
        after = m.sb("after", [P, NPAGE])
        pages = m.sb("pages", [P, RING, HB, PG, W])
        k_t = m.sb("k_t", [P, 2, HB, CH, STEP])
        s = m.sb("s", [P, PAST + NS])
        probs = m.sb("probs", [P, RING, STEP])
        probs_new = m.sb("probs_new", [P, NS])
        probs_t = m.sb("probs_t", [P, 2, PG, R])
        new_t = m.sb("new_t", [NS, R])
        shift = m.sb("shift", [P, 1])
        sums = m.sb("sums", [P, STEPS + 1])
        inv = m.sb("inv", [P, 1])
        picked = m.sb("picked", [P, 2, W])
        out_s = m.sb("out_s", [NS, W])
        qs = m.sb("qs", [NS, W])
        ks = m.sb("ks", [NS, W])
        vs = m.sb("vs", [NS, W])
        lfs = m.sb("lfs", [NS, H])
        q_blocks = m.sb("q_blocks", [P, DB, CH, H * DS])
        ks_t = m.sb("ks_t", [P, CH, NS])
        later = m.sb("later", [P, PAGE])
        mask_s = m.sb("mask_s", [NS, NS])
        upto_s = m.sb("upto_s", [NS, NS])
        sel = m.sb("sel", [NS, 2, R])
        sel_t = m.sb("sel_t", [P, 2, NS])
        head_sel = m.sb("head_sel", [H, R])
        head_mask = m.sb("head_mask", [P, H])
        lfs_rows = m.sb("lfs_rows", [NS, R])

        kt = m.ps("kt", [P, 4, 512])
        sc = m.ps("sc", [P, 2, 512])
        o = m.ps("o", [P, W])
        misc = m.ps("misc", [P, 512])
        tot_ps, new_ps, pn_ps = misc[:, 0:NPAGE], misc[:, 32:64], misc[0:NS, 64:192]
        hm_ps, sel_ps = misc[:, 192:200], misc[:, 200:264]
        qk_ps = sc[:, 0, 0:2 * CH * NS]

        const_loaded = m.sem("const_loaded")
        table_loaded = m.sem("table_loaded")
        page_loaded_sp = [m.sem(f"page_loaded_sp{k}") for k in range(RING)]
        page_loaded_pool = [m.sem(f"page_loaded_pool{k}") for k in range(RING)]
        page_free = [m.sem(f"page_free{k}") for k in range(RING)]
        lf_gathered = m.sem("lf_gathered")
        masks = m.sem("masks")
        consts = m.sem("consts")
        setup = m.sem("setup")
        turned = m.sem("turned")
        lf_turned = m.sem("lf_turned")
        lf_ready = m.sem("lf_ready")
        tot_done = m.sem("tot_done")
        after_ready = m.sem("after_ready")
        bias_done = m.sem("bias_done")
        bias_evac = m.sem("bias_evac")
        new_done = m.sem("new_done")
        kt_done = m.sem("kt_done")
        kt_evac_act = m.sem("kt_evac_act")
        kt_evac_dve = m.sem("kt_evac_dve")
        sc_done = m.sem("sc_done")
        sc_evac = m.sem("sc_evac")
        shift_ready = m.sem("shift_ready")
        exp_done = m.sem("exp_done")
        exp_new = m.sem("exp_new")
        new_turned = m.sem("new_turned")
        new_copied = m.sem("new_copied")
        pt_done = m.sem("pt_done")
        pt_copied = m.sem("pt_copied")
        o_picked = m.sem("o_picked")
        dve_chain = m.sem("dve_chain")
        out_done = m.sem("out_done")
        out_copied = m.sem("out_copied")
        out_stored = m.sem("out_stored")

        def load_pages(eng, sequences, loaded):
            eng.wait_ge(table_loaded, 32)
            for half in range(2):
                for kind, cache in enumerate((io["cache_k"], io["cache_v"])):
                    rows = cache[0].rearrange("n t h d -> t n (h d)")
                    with eng.Fori(0, ITERS) as j:
                        for k in range(RING):
                            eng.wait_ge(page_free[k], j + ((half * 2 + kind) * ITERS + 1))
                            for b in sequences:
                                for g in range(PG):
                                    at = j * (RING * PG) + ((half * HB + b) * NPAGE + k * PG + g)
                                    page = eng.value_load(table[0:1, bass.ds(at, 1)], min_val=0, max_val=cache.shape[1] - 1)
                                    eng.dma_start(pages[:, k, b, g], rows[:, bass.ds(page, 1)].rearrange("t n c -> t (n c)")).then_inc(loaded[k], 16)

        block = ctx.enter_context(nc.Block())

        @block.sync
        def _(sp):
            sp.dma_start(table[:], io["page_table"].rearrange("(a b) p -> a (b p)", a=1)).then_inc(table_loaded, 16)
            sp.dma_start(page_of[:], io["page_table"].rearrange("(f b) p -> (b p) f", f=2), allow_slow_non_contiguous=True).then_inc(table_loaded, 16)
            sp.dma_start(qs[:], io["q_s"]).then_inc(const_loaded, 16)
            sp.dma_start(ks[:], io["k_sample"].rearrange("l b t h d -> (l b t) (h d)")).then_inc(const_loaded, 16)
            sp.dma_start(vs[:], io["v_sample"].rearrange("l b t h d -> (l b t) (h d)")).then_inc(const_loaded, 16)
            sp.dma_start(lfs[:], io["logf_sample"].rearrange("l b t h -> (l b t) h")).then_inc(const_loaded, 16)
            load_pages(sp, range(0, HB // 2), page_loaded_sp)
            sp.wait_ge(out_copied, 1)
            sp.dma_start(io["attn_s"], out_s[:]).then_inc(out_stored, 16)
            sp.wait_ge(out_stored, 16)

        @block.gpsimd
        def _(pool):
            for k in range(RING):
                pool.sem_inc(page_free[k], 1)
            for sem in (kt_evac_act, kt_evac_dve, sc_evac, pt_copied):
                pool.sem_inc(sem, 2)
            pool.sem_inc(sc_done, 2)
            pool.sem_inc(pt_done, RING)
            pool.wait_ge(table_loaded, 32)
            for half in range(2):
                nc.gpsimd.indirect_dma_start(lf_pages[:, half], None, io["cache_logf"][0].rearrange("n t h -> n (t h)"),
                                             bass.IndirectOffsetOnAxis(page_of[:, half:half + 1], 0)).then_inc(lf_gathered, 16)
            chain = Chain(pool, masks)
            chain.link(nc.gpsimd.memset(later[:], 1.0))
            chain.link(nc.gpsimd.affine_select(out=later[:], in_=later[:], compare_op=ALU.is_ge, fill=0.0, base=-1, pattern=[[-1, PAGE]], channel_multiplier=1))
            ms, us = mask_s[:].rearrange("p (b t) -> p b t", b=DB), upto_s[:].rearrange("p (b t) -> p b t", b=DB)
            chain.link(nc.gpsimd.memset(ms, 0.0))
            chain.link(nc.gpsimd.affine_select(out=ms, in_=ms, compare_op=ALU.is_ge, fill=-BIG, base=0, pattern=[[-DS, DB], [-1, DS]], channel_multiplier=1))
            chain.link(nc.gpsimd.affine_select(out=ms, in_=ms, compare_op=ALU.is_ge, fill=-BIG, base=DS - 1, pattern=[[DS, DB], [0, DS]], channel_multiplier=-1))
            chain.link(nc.gpsimd.memset(us, -1.0))
            chain.link(nc.gpsimd.affine_select(out=us, in_=us, compare_op=ALU.is_ge, fill=0.0, base=0, pattern=[[DS, DB], [1, DS]], channel_multiplier=-1))
            nc.gpsimd.affine_select(out=us, in_=us, compare_op=ALU.is_ge, fill=0.0, base=0, pattern=[[-DS, DB], [0, DS]], channel_multiplier=1).then_inc(consts, 1)
            load_pages(pool, range(HB // 2, HB), page_loaded_pool)

        @block.scalar
        def _(act):
            for half in range(2):
                with act.Fori(0, ITERS) as j:
                    for k in range(RING):
                        g = j * RING + (half * STEPS + k)
                        act.wait_ge(sc_done, g + 1)
                        for b in range(HB):
                            act.wait_ge(kt_done, g * 8 + (2 * b + 1))
                            nc.scalar.activation(k_t[:, k % 2, b, 0:2].rearrange("p c t -> p (c t)"), kt[:, 2 * b % 4], ACT.Copy).then_inc(kt_evac_act, 1)
                act.wait_ge(shift_ready, half + 1)
                nc.scalar.activation(probs_new[:], s[:, PAST:], ACT.Exp, bias=shift[:], accum_out=sums[:, STEPS:STEPS + 1]).then_inc(exp_new, 1)
                with act.Fori(0, ITERS) as j:
                    for k in range(RING):
                        act.wait_ge(pt_done, j * RING + (half * STEPS + k + 1))
                        nc.scalar.activation(probs[:, k], s[:, bass.ds(j * (RING * STEP) + k * STEP, STEP)], ACT.Exp, bias=shift[:],
                                             accum_out=sums[:, bass.ds(j * RING + k, 1)]).then_inc(exp_done, 1)

        @block.vector
        def _(dve):
            start = Chain(dve, setup)
            ident = keep["ident"]
            start.link(nc.vector.memset(q_blocks[:], 0.0))
            start.link(nc.vector.memset(after[:, 0:1], 0.0))
            for half in range(2):
                tokens = ident[0:NS, half * HB * DS:(half + 1) * HB * DS].rearrange("p (b q) -> p b q", b=HB)
                nc.vector.tensor_copy(sel[:, half].rearrange("p (b h q) -> p b h q", b=HB, h=H),
                                      tokens.unsqueeze(2).to_broadcast([NS, HB, H, DS]))
            nc.vector.tensor_copy(head_sel[:].rearrange("p (b h q) -> p b h q", b=HB, h=H),
                                  ident[0:H, 0:H].unsqueeze(1).unsqueeze(3).to_broadcast([H, HB, H, DS]))
            dve.wait_ge(const_loaded, 64)
            start.link(nc.vector.tensor_copy(lfs_rows[:].rearrange("p (b h q) -> p b h q", b=HB, h=H),
                                             lfs[:].unsqueeze(1).unsqueeze(3).to_broadcast([NS, HB, H, DS])))
            dve.wait_ge(turned, 1)
            qt = qk_ps[:, 0:CH * NS].rearrange("p (c b q) -> p c b q", c=CH, b=DB)
            for c in range(CH):
                for e in range(2):
                    h = 2 * c + e
                    nc.vector.tensor_copy(q_blocks[e * HD:(e + 1) * HD, :, c, h * DS:(h + 1) * DS], qt[e * HD:(e + 1) * HD, c])
            nc.vector.tensor_copy(ks_t[:], qk_ps[:, CH * NS:].rearrange("p (c t) -> p c t", c=CH))
            nc.vector.tensor_copy(head_mask[:], hm_ps)
            start.link(nc.vector.tensor_copy(sel_t[:], sel_ps.rearrange("p (f t) -> p f t", f=2)))

            n_chain = 0
            for half in range(2):
                dve.wait_ge(lf_turned, half + 1)
                lf = kt[:, 0:2].rearrange("p a (h b g) -> p (a h) b g", h=CH, b=HB)
                for b in range(HB):
                    rows = lf_rows[:].rearrange("p g (b h q) -> p b g h q", b=HB, h=H)[:, b]
                    last = nc.vector.tensor_copy(rows, lf[:, :, b].rearrange("p h g -> p g h").unsqueeze(3).to_broadcast([P, NPAGE, H, DS]))
                last.then_inc(lf_ready, 1)
                dve.wait_ge(tot_done, half + 1)
                nc.vector.tensor_tensor_scan(after[:, 1:NPAGE], keep["ones"][:, 0:NPAGE - 1], tot_ps[:, 0:NPAGE - 1], 0.0, ALU.mult, ALU.add).then_inc(after_ready, 1)
                dve.wait_ge(after_ready, half + 1)
                for n in range(NPAGE // 4):
                    dve.wait_ge(bias_done, half * (NPAGE // 4) + n + 1)
                    for i in range(4):
                        page = 4 * n + i
                        last = nc.vector.tensor_scalar(s[:, page * PAGE:(page + 1) * PAGE], kt[:, n % 4, i * PAGE:(i + 1) * PAGE],
                                                       after[:, NPAGE - 1 - page:NPAGE - page], None, ALU.add)
                    last.then_inc(bias_evac, 1)
                dve.wait_ge(new_done, half + 1)
                nc.vector.tensor_copy(s[:, PAST:], new_ps).then_inc(dve_chain, 1)
                dve.wait_ge(bias_evac, (half + 1) * (NPAGE // 4))
                dve.wait_ge(dve_chain, n_chain + 1)

                with dve.Fori(0, ITERS) as j:
                    def evac_kt(k):
                        g = j * RING + (half * STEPS + k)
                        dve.wait_ge(sc_done, g + 1)
                        for b in range(HB):
                            dve.wait_ge(kt_done, g * 8 + (2 * b + 2))
                            nc.vector.tensor_copy(k_t[:, k % 2, b, 2:4].rearrange("p c t -> p (c t)"), kt[:, (2 * b + 1) % 4]).then_inc(kt_evac_dve, 1)
                        nc.vector.nop().then_inc(page_free[k], 1)

                    def evac_scores(k):
                        g = j * RING + (half * STEPS + k)
                        dve.wait_ge(sc_done, g + 3)
                        cols = s[:, bass.ds(j * (RING * STEP) + k * STEP, STEP)]
                        nc.vector.tensor_tensor(cols, sc[:, k % 2, 0:STEP], cols, ALU.add).then_inc(sc_evac, 1)

                    evac_kt(0)
                    for k in range(1, RING):
                        evac_kt(k)
                        evac_scores(k - 1)
                    evac_scores(RING - 1)

                dve.wait_ge(sc_evac, 2 + (half + 1) * STEPS)
                nc.vector.tensor_reduce(shift[:], s[:], AX_X, ALU.max).then_inc(dve_chain, 1)
                dve.wait_ge(dve_chain, n_chain + 2)
                nc.vector.tensor_scalar(shift[:], shift[:], -1.0, None, ALU.mult).then_inc(shift_ready, 1)
                dve.wait_ge(new_turned, half + 1)
                nc.vector.tensor_copy(new_t[:], pn_ps).then_inc(new_copied, 1)
                with dve.Fori(0, ITERS) as j:
                    for k in range(RING):
                        g = j * RING + (half * STEPS + k)
                        dve.wait_ge(pt_done, g + (RING + 1))
                        dve.wait_ge(page_free[(k + 2) % RING], j + ((half * 2 + 1) * ITERS + (2 if k >= 2 else 1)))
                        nc.vector.tensor_copy(probs_t[:, k % 2].rearrange("p g r -> p (g r)"), kt[:, k % 2, 0:PG * R]).then_inc(pt_copied, 1)
                dve.wait_ge(page_free[RING - 1], (half + 1) * 2 * ITERS + 1)
                nc.vector.tensor_reduce(inv[:], sums[:], AX_X, ALU.add).then_inc(dve_chain, 1)
                dve.wait_ge(dve_chain, n_chain + 3)
                nc.vector.reciprocal(inv[:], inv[:]).then_inc(dve_chain, 1)
                dve.wait_ge(dve_chain, n_chain + 4)
                n_chain += 4
                nc.vector.scalar_tensor_tensor(out=picked[:, half].rearrange("p (h d) -> p h d", h=H), in0=o[:].rearrange("p (h d) -> p h d", h=H),
                                               scalar=inv[:], in1=head_mask[:].unsqueeze(2).to_broadcast([P, H, HD]),
                                               op0=ALU.mult, op1=ALU.mult).then_inc(o_picked, 1)
            dve.wait_ge(out_done, 1)
            nc.vector.tensor_copy(out_s[:], o[0:NS]).then_inc(out_copied, 1)

        @block.tensor
        def _(pe):
            ident = keep["ident"]
            pe.wait_ge(const_loaded, 64)
            pe.wait_ge(setup, 3)
            for n, rows in enumerate((qs, ks)):
                for c in range(CH):
                    nc.tensor.transpose(qk_ps[:, (n * CH + c) * NS:(n * CH + c + 1) * NS], rows[:, c * P:(c + 1) * P], ident[0:NS, 0:NS])
            for half in range(2):
                nc.tensor.transpose(sel_ps[:, half * NS:(half + 1) * NS], sel[:, half], ident[0:NS, 0:NS])
            nc.tensor.matmul(hm_ps, head_sel[:], ident[0:H, 0:H], start=True, stop=True).then_inc(turned, 1)
            pe.wait_ge(setup, 4)
            pe.wait_ge(consts, 1)
            for half in range(2):
                pe.wait_ge(lf_gathered, 32)
                by_head = lf_pages[:, half].rearrange("p (t h) -> p t h", h=H)
                for h in range(H):
                    last = nc.tensor.transpose(kt[:, h // 4, h % 4 * P:(h % 4 + 1) * P], by_head[:, :, h], ident[:])
                last.then_inc(lf_turned, 1)
                pe.wait_ge(lf_ready, half + 1)
                for page in range(NPAGE):
                    last = nc.tensor.matmul(tot_ps[:, NPAGE - 1 - page:NPAGE - page], lf_rows[:, page], keep["ones"][:, 0:1], start=True, stop=True)
                last.then_inc(tot_done, 1)
                for n in range(NPAGE // 4):
                    if n >= 4:
                        pe.wait_ge(bias_evac, half * (NPAGE // 4) + n - 3)
                    for i in range(4):
                        last = nc.tensor.matmul(kt[:, n % 4, i * PAGE:(i + 1) * PAGE], lf_rows[:, 4 * n + i], later[:], start=True, stop=True)
                    last.then_inc(bias_done, 1)
                nc.tensor.matmul(new_ps, sel[:, half], mask_s[:], start=True, stop=False)
                nc.tensor.matmul(new_ps, lfs_rows[:], upto_s[:], start=False, stop=False)
                for c in range(CH):
                    for b in range(HB):
                        last = nc.tensor.matmul(new_ps[b * 32:(b + 1) * 32], q_blocks[:, half * HB + b, c], ks_t[:, c], start=False, stop=(c == CH - 1))
                last.then_inc(new_done, 1)
                pe.wait_ge(bias_evac, (half + 1) * (NPAGE // 4))

                with pe.Fori(0, ITERS) as j:
                    def turn(k):
                        g = j * RING + (half * STEPS + k)
                        for loaded in (page_loaded_sp, page_loaded_pool):
                            pe.wait_ge(loaded[k], j * LOADED + (half * 2 * ITERS + 1) * LOADED)
                        for b in range(HB):
                            for pair, evac in enumerate((kt_evac_act, kt_evac_dve)):
                                pe.wait_ge(evac, g * HB + (b + 1))
                                bank = kt[:, (2 * b + pair) % 4].rearrange("p (c t) -> p c t", c=2)
                                for c in range(2):
                                    for i in range(PG):
                                        chunk = 2 * pair + c
                                        last = nc.tensor.transpose(bank[:, c, i * PAGE:(i + 1) * PAGE], pages[:, k, b, i, chunk * P:(chunk + 1) * P], ident[:])
                                last.then_inc(kt_done, 1)

                    def score(k):
                        g = j * RING + (half * STEPS + k)
                        pe.wait_ge(kt_evac_act, g * HB + (HB + 2))
                        pe.wait_ge(kt_evac_dve, g * HB + (HB + 2))
                        pe.wait_ge(sc_evac, g + 1)
                        for c in range(CH):
                            for b in range(HB):
                                last = nc.tensor.matmul(sc[b * 32:(b + 1) * 32, k % 2, 0:STEP], q_blocks[:, half * HB + b, c], k_t[:, k % 2, b, c],
                                                        start=(c == 0), stop=(c == CH - 1))
                        last.then_inc(sc_done, 1)

                    turn(0)
                    for k in range(1, RING):
                        turn(k)
                        score(k - 1)
                    score(RING - 1)

                pe.wait_ge(exp_new, half + 1)
                nc.tensor.transpose(pn_ps, probs_new[:], ident[:]).then_inc(new_turned, 1)
                pe.wait_ge(new_copied, half + 1)
                if half:
                    pe.wait_ge(o_picked, half)
                nc.tensor.matmul(o[:], new_t[:], vs[:], start=True, stop=False)

                def turn_probs(j, k):
                    g = j * RING + (half * STEPS + k)
                    pe.wait_ge(exp_done, g + 1)
                    pe.wait_ge(pt_copied, g + 1)
                    for i in range(PG):
                        last = nc.tensor.transpose(kt[:, k % 2, i * R:(i + 1) * R], probs[:, k, i * PAGE:(i + 1) * PAGE], ident[:])
                    last.then_inc(pt_done, 1)

                def weigh(j, k, final):
                    g = j * RING + (half * STEPS + k)
                    pe.wait_ge(pt_copied, g + 3)
                    for loaded in (page_loaded_sp, page_loaded_pool):
                        pe.wait_ge(loaded[k], j * LOADED + ((half * 2 + 1) * ITERS + 1) * LOADED)
                    for i in range(PG):
                        for b in range(HB):
                            last = nc.tensor.matmul(o[b * 32:(b + 1) * 32], probs_t[:, k % 2, i, b * 32:(b + 1) * 32], pages[:, k, b, i],
                                                    start=False, stop=(final and k == RING - 1 and i == PG - 1))
                    last.then_inc(page_free[k], 1)

                def iteration(j, final):
                    turn_probs(j, 0)
                    for k in range(1, RING):
                        turn_probs(j, k)
                        weigh(j, k - 1, final)
                    weigh(j, RING - 1, final)

                with pe.Fori(0, ITERS - 1) as j:
                    iteration(j, False)
                iteration(ITERS - 1, True)
            pe.wait_ge(o_picked, 2)
            nc.tensor.matmul(o[0:NS], sel_t[:, 0], picked[:, 0], start=True, stop=False)
            nc.tensor.matmul(o[0:NS], sel_t[:, 1], picked[:, 1], start=False, stop=True).then_inc(out_done, 1)


def build(nc, io):
    with ExitStack() as ctx:
        m = Alloc(nc, ctx, "keep")
        keep = {
            "ident": m.sb("ident", [P, P]),
            "ones": m.sb("ones", [P, P]),
            "hs_high": m.sb("hs_high", [P, KC, NS], F32R),
            "hs_low": m.sb("hs_low", [P, KC, NS], F32R),
            "f_cols": m.sb("f_cols", [P, NBLK, H]),
            "f_tot": m.sb("f_tot", [H, NT]),
        }
        phase_project(nc, io, keep)
        phase_decode(nc, io, keep)
        phase_attend(nc, io, keep)
        keep["mix_s"] = m.sb("mix_s", [NS, D])
        phase_gates(nc, io, keep)
        phase_merge(nc, io, keep)


_INS = ["x_prompt", "x_sample", "cache_k", "cache_v", "cache_logf", "state_pool", "page_table",
        "norm_w", "w_in", "b_forget", "pool_w", "pool_scale", "w_out", "norm_f"]
_OUTS = [("y_prompt", (1, SEQ, D)), ("y_sample", (DB, DS, D)),
         ("k_prompt", (1, 1, SEQ, H, HD)), ("v_prompt", (1, 1, SEQ, H, HD)),
         ("logf_prompt", (1, 1, SEQ, H)), ("pool_prompt", (1, 1, HIST, W)),
         ("k_sample", (1, DB, DS, H, HD)), ("v_sample", (1, DB, DS, H, HD)),
         ("logf_sample", (1, DB, DS, H)), ("pool_sample", (1, DB, HIST, W))]
_SCRATCH = [("h_t", (NT, P, KC, TILE)), ("q_t", (CH, P, SEQ)), ("k_t", (CH, P, SEQ)), ("f_neg", (H, SEQ)),
            ("q_s", (NS, W)), ("attn_t", (2, CH, P, SEQ)), ("den", (4, H, SEQ)), ("inv_den", (H, SEQ)), ("attn_s", (NS, W)), ("pool_t", (CH, P, SEQ)),
            ("gate_t", (CH, P, SEQ)), ("pool_s", (NS, W)), ("gate_s", (NS, W))]


def kernel(**inputs):
    import numpy as _np
    import concourse.bacc as _bacc
    from concourse import mybir as _mybir
    from concourse.bass_utils import run_bass_kernel_spmd as _run

    nc = _bacc.Bacc("TRN2", target_bir_lowering=False, num_devices=1)
    arrays, io = {}, {}
    for name in _INS:
        a = _np.ascontiguousarray(inputs[name])
        arrays[f"in_{name}_dram"] = a
        io[name] = nc.dram_tensor(f"in_{name}_dram", a.shape, _mybir.dt.from_np(a.dtype), kind="ExternalInput").ap()
    for name, shape in _OUTS:
        io[name] = nc.dram_tensor(f"out_{name}_dram", shape, F32, kind="ExternalOutput").ap()
    for name, shape in _SCRATCH:
        io[name] = nc.dram_tensor(f"scratch_{name}", shape, F32, kind="Internal").ap()
    build(nc, io)
    r = _run(nc, [arrays], core_ids=[0])
    return tuple(r.results[0][f"out_{name}_dram"] for name, _ in _OUTS)
```
